# Optimizing a Trainium2 kernel written in Bass

```python
import jax, jax.numpy as jnp
from jax import lax
import numpy as np

D_MODEL = 1024
BATCH = 1
SEQ = 128
DEPTH = 1
DEC_BATCH = 1
DEC_SEQ = 512
PAST_LEN = 128

GRID_W = 64
Q_BLOCK = 128
RMS_EPS = 1e-6
ROPE_THETA = 10000.0
N_MOD = 6
H_A = 8
KV_A = 2
HD_A = 128
H_B = 8
Q_LORA = 256
KV_LORA = 128
NOPE_B = 128
ROPE_B = 64
VD_B = 128
N_EXPERTS = 64
TOP_K = 8
N_GROUPS = 8
TOPK_GROUPS = 4
D_EXPERT = 256
D_SHARED = 256
ROUTED_SCALE = 2.5
EXPERT_BLOCK = 128
IN_SIZES = (H_A * HD_A, KV_A * HD_A, KV_A * HD_A, Q_LORA, KV_LORA, ROPE_B, D_MODEL, D_MODEL)
D_IN = H_A * HD_A + 2 * KV_A * HD_A + Q_LORA + KV_LORA + ROPE_B + 2 * D_MODEL

kernel_name = 'hybrid_gqa_mla_moe_diffusion_step'

def rmsnorm(x, g):
    xf = x.astype(jnp.float32)
    y = xf * lax.rsqrt(jnp.mean(xf * xf, axis=-1, keepdims=True) + RMS_EPS)
    return (y * g.astype(jnp.float32)).astype(x.dtype)

def axial_rope(n_tokens, rot_dim):
    rows = n_tokens // GRID_W
    t = jnp.arange(rows * GRID_W)
    row = (t // GRID_W).astype(jnp.float32)
    col = (t % GRID_W).astype(jnp.float32)
    axis_dim = rot_dim // 2
    inv = ROPE_THETA ** (-jnp.arange(0, axis_dim, 2, dtype=jnp.float32) / axis_dim)
    ang = jnp.concatenate([row[:, None] * inv, col[:, None] * inv], axis=-1)
    return jnp.cos(ang), jnp.sin(ang)

def apply_rope(x, cos, sin):
    half = x.shape[-1] // 2
    xf = x.astype(jnp.float32)
    x1, x2 = xf[..., :half], xf[..., half:]
    return jnp.concatenate([x1 * cos - x2 * sin, x2 * cos + x1 * sin], axis=-1).astype(x.dtype)

def block_attention(q, k, v, scale):
    b, kv, g, s, dk = q.shape
    nb = s // Q_BLOCK
    qb = q.reshape(b, kv, g, nb, Q_BLOCK, dk).transpose(3, 0, 1, 2, 4, 5)

    def one_block(q_blk):
        sc = jnp.einsum('bkgqd,bksd->bkgqs', q_blk, k).astype(jnp.float32) * scale
        p = jax.nn.softmax(sc, axis=-1).astype(v.dtype)
        return jnp.einsum('bkgqs,bksd->bkgqd', p, v)

    o = lax.map(one_block, qb)
    return o.transpose(1, 2, 3, 0, 4, 5).reshape(b, kv, g, s, v.shape[-1])

def mixing_sublayer(h, lw, rope_a, rope_b, ctx):
    b, s, _ = h.shape
    z = h @ lw['w_in']
    cuts = np.cumsum(IN_SIZES)[:-1].tolist()
    q_a, k_a, v_a, c_q, c_kv, k_r, g_a, g_b = jnp.split(z, cuts, axis=-1)
    qa = rmsnorm(q_a.reshape(b, s, H_A, HD_A), lw['gqa_qn']).transpose(0, 2, 1, 3)
    ka = rmsnorm(k_a.reshape(b, s, KV_A, HD_A), lw['gqa_kn']).transpose(0, 2, 1, 3)
    va = v_a.reshape(b, s, KV_A, HD_A).transpose(0, 2, 1, 3)
    cq = rmsnorm(c_q, lw['mla_qa_g'])
    qb = (cq @ lw['w_qb']).reshape(b, s, H_B, NOPE_B + ROPE_B).transpose(0, 2, 1, 3)
    qb_nope = rmsnorm(qb[..., :NOPE_B], lw['mla_qn_nope'])
    qb_rope = rmsnorm(qb[..., NOPE_B:], lw['mla_qn_rope'])
    ckv = rmsnorm(c_kv, lw['mla_kva_g'])
    kr = rmsnorm(k_r, lw['mla_kn_rope'])
    if ctx is None:
        ctx_out = (ka, va, ckv, kr)
        ka_all, va_all, ckv_all, kr_all = ka, va, ckv, kr
    else:
        ctx_out = None
        qa = apply_rope(qa, *rope_a)
        ka = apply_rope(ka, *rope_a)
        qb_rope = apply_rope(qb_rope, *rope_b)
        kr = apply_rope(kr, *rope_b)
        ka_all = jnp.concatenate([ctx[0], ka], axis=2)
        va_all = jnp.concatenate([ctx[1], va], axis=2)
        ckv_all = jnp.concatenate([ctx[2], ckv], axis=1)
        kr_all = jnp.concatenate([ctx[3], kr], axis=1)
    o_a = block_attention(qa.reshape(b, KV_A, H_A // KV_A, s, HD_A), ka_all, va_all, HD_A ** -0.5)
    o_a = o_a.reshape(b, H_A, s, HD_A).transpose(0, 2, 1, 3).reshape(b, s, H_A * HD_A)
    n_keys = ckv_all.shape[1]
    kvb = (ckv_all @ lw['w_kvb']).reshape(b, n_keys, H_B, NOPE_B + VD_B).transpose(0, 2, 1, 3)
    kb_nope = rmsnorm(kvb[..., :NOPE_B], lw['mla_kn_nope'])
    vb = kvb[..., NOPE_B:]
    kb = jnp.concatenate([kb_nope, jnp.broadcast_to(kr_all[:, None], (b, H_B, n_keys, ROPE_B))], axis=-1)
    qb_full = jnp.concatenate([qb_nope, qb_rope], axis=-1)
    o_b = block_attention(qb_full[:, :, None], kb, vb, (NOPE_B + ROPE_B) ** -0.5)
    o_b = o_b.reshape(b, H_B, s, VD_B).transpose(0, 2, 1, 3).reshape(b, s, H_B * VD_B)
    merged = jax.nn.sigmoid(g_a) * (o_a @ lw['w_oa']) + jax.nn.sigmoid(g_b) * (o_b @ lw['w_ob'])
    return merged @ lw['w_out'], ctx_out

def swiglu(x, w1, w3, w2):
    return (jax.nn.silu(x @ w1) * (x @ w3)) @ w2

def routed_experts(h, idx, w, w_e1, w_e3, w_e2):
    t, d = h.shape
    n = t * TOP_K
    flat_e = idx.reshape(n)
    flat_tok = jnp.repeat(jnp.arange(t, dtype=jnp.int32), TOP_K)
    flat_w = w.reshape(n)
    order = jnp.argsort(flat_e)
    se, stok, sw = flat_e[order], flat_tok[order], flat_w[order]
    counts = jnp.bincount(flat_e, length=N_EXPERTS)
    padded = (counts + EXPERT_BLOCK - 1) // EXPERT_BLOCK * EXPERT_BLOCK
    pad_end = jnp.cumsum(padded)
    pad_start = pad_end - padded
    start = jnp.cumsum(counts) - counts
    dest = pad_start[se] + (jnp.arange(n) - start[se])
    n_blocks = -(-n // EXPERT_BLOCK) + N_EXPERTS
    n_rows = n_blocks * EXPERT_BLOCK
    xd = jnp.zeros((n_rows, d), h.dtype).at[dest].set(h[stok])
    wd = jnp.zeros((n_rows,), h.dtype).at[dest].set(sw)
    td = jnp.zeros((n_rows,), jnp.int32).at[dest].set(stok)
    blk_e = jnp.minimum(jnp.searchsorted(pad_end, jnp.arange(n_blocks) * EXPERT_BLOCK, side='right'), N_EXPERTS - 1)

    def run_block(args):
        xb, e = args
        return swiglu(xb, w_e1[e], w_e3[e], w_e2[e])

    yd = lax.map(run_block, (xd.reshape(n_blocks, EXPERT_BLOCK, d), blk_e)).reshape(n_rows, d)
    return jax.ops.segment_sum(yd * wd[:, None], td, num_segments=t)

def moe_ffn(h, lw):
    t = h.shape[0]
    scores = jax.nn.sigmoid(h.astype(jnp.float32) @ lw['w_router'].astype(jnp.float32))
    biased = scores + lw['router_bias'].astype(jnp.float32)
    grp = biased.reshape(t, N_GROUPS, N_EXPERTS // N_GROUPS)
    grp_score = jnp.sum(lax.top_k(grp, 2)[0], axis=-1)
    _, top_g = lax.top_k(grp_score, TOPK_GROUPS)
    gmask = jnp.sum(jax.nn.one_hot(top_g, N_GROUPS, dtype=jnp.int32), axis=-2) > 0
    emask = jnp.repeat(gmask, N_EXPERTS // N_GROUPS, axis=-1)
    _, idx = lax.top_k(jnp.where(emask, biased, -jnp.inf), TOP_K)
    w = jnp.take_along_axis(scores, idx, axis=-1)
    w = (w / jnp.sum(w, axis=-1, keepdims=True) * ROUTED_SCALE).astype(h.dtype)
    routed = routed_experts(h, idx, w, lw['w_e1'], lw['w_e3'], lw['w_e2'])
    return routed + swiglu(h, lw['w_s1'], lw['w_s3'], lw['w_s2'])

def trunk_layer(x, cond, lw, rope_a, rope_b, ctx):
    mod = (jax.nn.silu(cond) @ lw['w_mod'] + lw['b_mod'])[:, None, :]
    sh1, sc1, g1, sh2, sc2, g2 = jnp.split(mod, N_MOD, axis=-1)
    h = rmsnorm(x, lw['norm1_g']) * (1 + sc1) + sh1
    a, ctx_out = mixing_sublayer(h, lw, rope_a, rope_b, ctx)
    x = x + g1 * a
    h = rmsnorm(x, lw['norm2_g']) * (1 + sc2) + sh2
    b, s, d = h.shape
    x = x + g2 * moe_ffn(h.reshape(b * s, d), lw).reshape(b, s, d)
    return x, ctx_out

def _normal(k, shape, scale):
    return jax.random.normal(k, shape, jnp.float32) * scale

def _gain(k, shape):
    return 1.0 + 0.02 * jax.random.normal(k, shape, jnp.float32)

def setup_inputs(seed: int = 0) -> dict:
    key = jax.random.key(seed)
    ks = iter(jax.random.split(key, 40))
    L, D, E = DEPTH, D_MODEL, N_EXPERTS
    return {
        'x_prompt': _normal(next(ks), (BATCH, SEQ, D), 1.0),
        'x_sample': _normal(next(ks), (DEC_BATCH, DEC_SEQ, D), 1.0),
        'c': _normal(next(ks), (DEC_BATCH, D), 1.0),
        'cache_gqa_k': _normal(next(ks), (DEC_BATCH, L, KV_A, PAST_LEN, HD_A), 1.0),
        'cache_gqa_v': _normal(next(ks), (DEC_BATCH, L, KV_A, PAST_LEN, HD_A), 1.0),
        'cache_mla_ckv': _normal(next(ks), (DEC_BATCH, L, PAST_LEN, KV_LORA), 1.0),
        'cache_mla_krope': _normal(next(ks), (DEC_BATCH, L, PAST_LEN, ROPE_B), 1.0),
        'c_ctx': _normal(next(ks), (D,), 1.0),
        'w_mod': _normal(next(ks), (L, D, N_MOD * D), 0.5 * D ** -0.5),
        'b_mod': _normal(next(ks), (L, N_MOD * D), 0.02),
        'norm1_g': _gain(next(ks), (L, D)),
        'norm2_g': _gain(next(ks), (L, D)),
        'w_in': _normal(next(ks), (L, D, D_IN), D ** -0.5),
        'gqa_qn': _gain(next(ks), (L, HD_A)),
        'gqa_kn': _gain(next(ks), (L, HD_A)),
        'mla_qa_g': _gain(next(ks), (L, Q_LORA)),
        'mla_kva_g': _gain(next(ks), (L, KV_LORA)),
        'w_qb': _normal(next(ks), (L, Q_LORA, H_B * (NOPE_B + ROPE_B)), Q_LORA ** -0.5),
        'w_kvb': _normal(next(ks), (L, KV_LORA, H_B * (NOPE_B + VD_B)), KV_LORA ** -0.5),
        'mla_qn_nope': _gain(next(ks), (L, NOPE_B)),
        'mla_qn_rope': _gain(next(ks), (L, ROPE_B)),
        'mla_kn_nope': _gain(next(ks), (L, NOPE_B)),
        'mla_kn_rope': _gain(next(ks), (L, ROPE_B)),
        'w_oa': _normal(next(ks), (L, H_A * HD_A, D), (H_A * HD_A) ** -0.5),
        'w_ob': _normal(next(ks), (L, H_B * VD_B, D), (H_B * VD_B) ** -0.5),
        'w_out': _normal(next(ks), (L, D, D), D ** -0.5),
        'w_router': _normal(next(ks), (L, D, E), D ** -0.5),
        'router_bias': _normal(next(ks), (L, E), 0.01),
        'w_e1': _normal(next(ks), (L, E, D, D_EXPERT), D ** -0.5),
        'w_e3': _normal(next(ks), (L, E, D, D_EXPERT), D ** -0.5),
        'w_e2': _normal(next(ks), (L, E, D_EXPERT, D), D_EXPERT ** -0.5),
        'w_s1': _normal(next(ks), (L, D, D_SHARED), D ** -0.5),
        'w_s3': _normal(next(ks), (L, D, D_SHARED), D ** -0.5),
        'w_s2': _normal(next(ks), (L, D_SHARED, D), D_SHARED ** -0.5),
    }

def reference(x_prompt, x_sample, c, cache_gqa_k, cache_gqa_v, cache_mla_ckv, cache_mla_krope, c_ctx,
              w_mod, b_mod, norm1_g, norm2_g, w_in, gqa_qn, gqa_kn, mla_qa_g, mla_kva_g, w_qb, w_kvb,
              mla_qn_nope, mla_qn_rope, mla_kn_nope, mla_kn_rope, w_oa, w_ob, w_out, w_router, router_bias,
              w_e1, w_e3, w_e2, w_s1, w_s3, w_s2):
    n_lat = x_sample.shape[1]
    rope_a = axial_rope(n_lat, HD_A)
    rope_b = axial_rope(n_lat, ROPE_B)
    cond_ctx = c_ctx[None, :]
    xp, xs = x_prompt, x_sample
    ks, vs, ckvs, krs = [], [], [], []
    for l in range(DEPTH):
        lw = {
            'w_mod': w_mod[l], 'b_mod': b_mod[l], 'norm1_g': norm1_g[l], 'norm2_g': norm2_g[l],
            'w_in': w_in[l], 'gqa_qn': gqa_qn[l], 'gqa_kn': gqa_kn[l],
            'mla_qa_g': mla_qa_g[l], 'mla_kva_g': mla_kva_g[l], 'w_qb': w_qb[l], 'w_kvb': w_kvb[l],
            'mla_qn_nope': mla_qn_nope[l], 'mla_qn_rope': mla_qn_rope[l],
            'mla_kn_nope': mla_kn_nope[l], 'mla_kn_rope': mla_kn_rope[l],
            'w_oa': w_oa[l], 'w_ob': w_ob[l], 'w_out': w_out[l],
            'w_router': w_router[l], 'router_bias': router_bias[l],
            'w_e1': w_e1[l], 'w_e3': w_e3[l], 'w_e2': w_e2[l],
            'w_s1': w_s1[l], 'w_s3': w_s3[l], 'w_s2': w_s2[l],
        }
        xp, ctx_l = trunk_layer(xp, cond_ctx, lw, None, None, None)
        ks.append(ctx_l[0])
        vs.append(ctx_l[1])
        ckvs.append(ctx_l[2])
        krs.append(ctx_l[3])
        cached = (cache_gqa_k[:, l], cache_gqa_v[:, l], cache_mla_ckv[:, l], cache_mla_krope[:, l])
        xs, _ = trunk_layer(xs, c, lw, rope_a, rope_b, cached)
    new_gqa_k = jnp.stack(ks, axis=1)
    new_gqa_v = jnp.stack(vs, axis=1)
    new_mla_ckv = jnp.stack(ckvs, axis=1)
    new_mla_krope = jnp.stack(krs, axis=1)
    return (xp, xs, new_gqa_k, new_gqa_v, new_mla_ckv, new_mla_krope)


_drawn_inputs = setup_inputs


def setup_inputs(seed=0):
    import zlib

    import numpy as np

    out = dict(_drawn_inputs(seed))
    spreads = {}
    factors = {'cache_gqa_k': 2.947,
     'cache_gqa_v': 2.698,
     'cache_mla_ckv': 3.251,
     'cache_mla_krope': 4.509,
     'norm1_g': 3.047,
     'gqa_qn': 8.0,
     'gqa_kn': 2.849,
     'mla_qa_g': 8.0,
     'mla_kva_g': 2.685,
     'mla_qn_nope': 8.0,
     'mla_qn_rope': 8.0,
     'mla_kn_nope': 8.0,
     'mla_kn_rope': 9.23}
    for name, (base, spread) in spreads.items():
        noise = np.random.default_rng([zlib.crc32(name.encode()), seed]).standard_normal(out[name].shape)
        drawn = base * np.exp(spread * noise) if base else spread * noise
        out[name] = __import__('jax').numpy.asarray(drawn.astype(out[name].dtype))
    for name, factor in factors.items():
        out[name] = (out[name] * factor).astype(out[name].dtype)
    return out
```

```python
from contextlib import ExitStack

import numpy as np

import concourse.bass as bass
from concourse import mybir

F32 = mybir.dt.float32
I32 = mybir.dt.int32
ALU = mybir.AluOpType
ACT = mybir.ActivationFunctionType
AX_X = mybir.AxisListType.X

P = 128
D = 1024
SEQ, LAT, PAST = 128, 512, 128
TOK = SEQ + LAT
NT = TOK // P
KT = D // P
GRID_W = 64
EPS = 1e-6
THETA = 10000.0
N_MOD = 6
HA, KVA, HD = 8, 2, 128
HB, QL, KVL, NOPE, ROPE, VD = 8, 256, 128, 128, 64, 128
KEYS = TOK + PAST
NK = KEYS // P
NE, TOPK, NG, TOPG = 64, 8, 8, 4
FE = 256
ROUTED_SCALE = 2.5
BIG = 1e30
OVF = TOK * TOPK // P
NBLK = NE + OVF
RING = 4
C_QA, C_KA, C_VA = 0, 1024, 1280
C_CQ, C_CKV, C_KR = 1536, 1792, 1920
C_GA, C_GB = 1984, 3008
ZN = C_GA - C_KA
Z_K, Z_V, Z_CQ, Z_CKV, Z_KR = 0, 256, 512, 768, 896


def key_col(t):
    return 0 if t == 0 else P * (t + 1)


class Mem:

    def __init__(self, tensor):
        self.t = tensor

    def at(self, off, *shape, rows=P):
        n = int(np.prod(shape))
        v = self.t[0:rows, off:off + n]
        if len(shape) == 2:
            v = v.rearrange("p (a b) -> p a b", a=shape[0])
        if len(shape) == 3:
            v = v.rearrange("p (a b c) -> p a b c", a=shape[0], b=shape[1])
        return v


def program(nc, I, O, S):
    ctx = ExitStack()
    with ctx:
        build(nc, I, O, S, ctx)


def build(nc, I, O, S, ctx):
    def sb(name, shape, dt=F32):
        return ctx.enter_context(nc.sbuf_tensor(name, shape, dt))

    def sem(name):
        return ctx.enter_context(nc.semaphore(name))

    M_H, M_OA, M_OB, M_R, M_SC, M_TB = 0, 5120, 10240, 15360, 31744, 40320
    M_END = M_TB + 9728
    mem = Mem(sb("mem", [P, M_END]))
    hT = mem.at(M_H, KT, TOK)
    oA = mem.at(M_OA, HA, TOK)
    oB = mem.at(M_OB, HB, TOK)
    ident = sb("ident", [P, P])
    cols = sb("cols", [P, 84])
    modc = sb("modc", [P, 48, 2])
    small = sb("small", [P, 128])
    nhalf = sb("nhalf", [P, 16])
    psum = ctx.enter_context(nc.psum_tensor("psum", [P, 4096], F32))

    def bank(b, n=1):
        return psum[:, b * 512:(b + n) * 512]

    CqA = mem.at(M_TB, NT, HD)
    SqA = mem.at(M_TB + 640, NT, HD)
    CkA = mem.at(M_TB + 1280, NT, HD)
    SkA = mem.at(M_TB + 1920, NT, HD)
    CqB = mem.at(M_TB + 2560, NT, ROPE)
    SqB = mem.at(M_TB + 2880, NT, ROPE)
    CkB = mem.at(M_TB + 3200, NT, ROPE)
    SkB = mem.at(M_TB + 3520, NT, ROPE)
    kTA = mem.at(M_TB + 3840, KVA, KEYS)
    vA = mem.at(M_TB + 5376, NK, KVA, HD)
    krT = mem.at(M_TB + 6912, KEYS, rows=ROPE)
    cqT = mem.at(M_TB + 7680, 2, TOK)
    ckvT = mem.at(M_TB + 8960, KEYS)

    A1, rstd = small[:, 0:16].rearrange("p (k y) -> p k y", y=2), small[:, 16:21]
    ss = small[:, 24:29]
    invlen = small[:, 32:37]
    qk_gain = small[:, 40:41]

    SCALE_A = float(HD) ** -0.5
    SCALE_B = float(NOPE + ROPE) ** -0.5

    s_const = sem("s_const")
    s_rows = sem("s_rows")
    s_x = [sem(f"s_x{t}") for t in range(NT)]
    s_wm = [sem(f"s_wm{b}") for b in range(4)]
    s_wz = sem("s_wz")
    s_silu = sem("s_silu")
    s_rowsT = sem("s_rowsT")
    s_cols = sem("s_cols")
    s_mod1 = sem("s_mod1")
    s_A1 = sem("s_A1")
    s_sqx = sem("s_sqx")
    s_rstd = sem("s_rstd")
    s_xs = sem("s_xs")
    s_xT = sem("s_xT")
    s_xeV, s_xeA = sem("s_xeV"), sem("s_xeA")
    s_v = sem("s_v")
    s_p = sem("s_p")
    s_tabs = sem("s_tabs")
    s_gain = sem("s_gain")

    rows = mem.at(M_SC + 5120, 128, rows=84)
    xt = mem.at(M_SC, NT, D)
    sqd = mem.at(M_SC + 5248, D)
    gA = mem.at(M_R + 6144 + 7680, 4, HD)
    gB = mem.at(M_R + 6144 + 7680 + 512, 4, ROPE)
    wmod = [mem.at(M_OA + 4096 * b, KT, 512) for b in range(4)]
    wz = mem.at(M_R + 6144, KT, ZN)
    w_mod_v = I["w_mod"][0].rearrange("(k p) n -> p k n", p=P)
    w_in_v = I["w_in"][0].rearrange("(k p) n -> p k n", p=P)
    pm = bank(7)[:, 0:96].rearrange("p (c y) -> p c y", y=2)

    class Chain:

        def __init__(self, eng, s, n=0):
            self.eng, self.s, self.n = eng, s, n

        def __call__(self, ins):
            self.n = self.n + 1
            ins.then_inc(self.s, 1)
            self.eng.wait_ge(self.s, self.n)

    def mod_chunk(pe, c):
        pe.wait_ge(s_wm[c % 4], 16 * (c // 4 + 1))
        for j in range(4):
            for k in range(KT):
                mm = pe.matmul(pm[:, 4 * c + j, :], wmod[c % 4][:, k, j * P:(j + 1) * P],
                               cols[:, k:k + 9:8], start=(k == 0), stop=(k == KT - 1))
        mm.then_inc(s_mod1, 1)

    with nc.Block() as block:
        @block.sync
        def _(sp):
            sp.dma_start(rows[0:8, :], I["c_ctx"].rearrange("(k p) -> k p", p=P)).then_inc(s_rows, 16)
            sp.dma_start(rows[8:16, :], I["c"].rearrange("a (k p) -> (a k) p", p=P)).then_inc(s_rows, 16)
            sp.dma_start(rows[16:64, :], I["b_mod"].rearrange("a (k p) -> (a k) p", p=P)).then_inc(s_rows, 16)
            sp.dma_start(rows[64:72, :], I["norm1_g"].rearrange("a (k p) -> (a k) p", p=P)).then_inc(s_rows, 16)
            sp.dma_start(rows[72:80, :], I["norm2_g"].rearrange("a (k p) -> (a k) p", p=P)).then_inc(s_rows, 16)
            sp.dma_start(rows[80:82, :], I["mla_qa_g"].rearrange("a (k p) -> (a k) p", p=P)).then_inc(s_rows, 16)
            sp.dma_start(rows[82:83, :], I["mla_qn_nope"]).then_inc(s_rows, 16)
            sp.dma_start(rows[83:84, :], I["mla_kn_nope"]).then_inc(s_rows, 16)
            sp.dma_start(ident[:, :], I["ident"]).then_inc(s_const, 16)
            sp.dma_start(xt[:, 0, :], I["x_prompt"][0]).then_inc(s_x[0], 16)
            for c in range(4):
                sp.dma_start(wmod[c], w_mod_v[:, :, c * 512:(c + 1) * 512]).then_inc(s_wm[c], 16)
            for t in range(1, NT):
                sp.dma_start(xt[:, t, :], I["x_sample"][0, (t - 1) * P:t * P, :]).then_inc(s_x[t], 16)
            sp.dma_start(wz, w_in_v[:, :, C_KA:C_GA]).then_inc(s_wz, 16)

        @block.gpsimd
        def _(pool):
            for n, (dst, src, w) in enumerate((
                    (gA[:, 0:2, :], I["gqa_qn"], HD), (gA[:, 2:4, :], I["gqa_kn"], HD),
                    (gB[:, 0:2, :], I["mla_qn_rope"], ROPE), (gB[:, 2:4, :], I["mla_kn_rope"], ROPE))):
                h = w // 2
                pool.dma_start(dst[:, 0, :], src.to_broadcast([P, w])).then_inc(s_gain, 16)
                pool.dma_start(dst[:, 1, 0:h], src[:, h:w].to_broadcast([P, h])).then_inc(s_gain, 16)
                pool.dma_start(dst[:, 1, h:w], src[:, 0:h].to_broadcast([P, h])).then_inc(s_gain, 16)
            for dst, src in ((CqA, I["cos_a"]), (SqA, I["sin_a"]), (CqB, I["cos_b"]), (SqB, I["sin_b"])):
                pool.dma_start(dst, src.rearrange("(t p) w -> p t w", p=P)).then_inc(s_tabs, 16)
            pool.memset(nhalf[:, :], -0.5).then_inc(s_p, 1)
            pool.memset(invlen[:, 0:2], 1.0 / HD).then_inc(s_p, 1)
            pool.memset(invlen[:, 2:3], 1.0 / QL).then_inc(s_p, 1)
            pool.memset(invlen[:, 3:4], 1.0 / KVL).then_inc(s_p, 1)
            pool.memset(invlen[:, 4:5], 1.0 / ROPE).then_inc(s_p, 1)
            pool.wait_ge(s_sqx, NT)
            pool.wait_ge(s_p, 5)
            pool.tensor_scalar(ss, ss, 1.0 / D, EPS, ALU.mult, ALU.add).then_inc(s_p, 1)
            pool.wait_ge(s_p, 6)
            pool.tensor_tensor(rstd, ss, nhalf[:, 0:NT], ALU.pow).then_inc(s_rstd, 1)

        @block.scalar
        def _(act):
            act.wait_ge(s_rows, 16 * 8)
            act.activation(rows[0:16, :], rows[0:16, :], ACT.Silu).then_inc(s_silu, 1)
            for t in range(NT):
                act.wait_ge(s_x[t], 16)
                if t:
                    act.wait_ge(s_sqx, t)
                act.activation(sqd, xt[:, t, :], ACT.Square, accum_out=ss[:, t:t + 1]).then_inc(s_sqx, 1)
            act.wait_ge(s_A1, 3)
            for t in range(NT):
                y = min(t, 1)
                act.wait_ge(s_xT, t + 1)
                for k in range(4, 8):
                    ins = act.activation(hT[:, k, t * P:(t + 1) * P],
                                         bank(2 * (t % 2) + 1)[:, (k - 4) * P:(k - 3) * P], ACT.Identity,
                                         bias=modc[:, k, y:y + 1], scale=A1[:, k, y:y + 1])
                ins.then_inc(s_xeA, 1)

        @block.vector
        def _(dve):
            chain = Chain(dve, s_v)
            dve.wait_ge(s_gain, 16 * 12)
            dve.wait_ge(s_tabs, 16 * 4)

            def over(g, w):
                return g.unsqueeze(1).to_broadcast([P, NT, w])

            for q, k, raw, g, w, scale in ((CqA, CkA, CqA, gA, HD, SCALE_A), (SqA, SkA, SqA, gA, HD, SCALE_A),
                                           (CqB, CkB, CqB, gB, ROPE, SCALE_B), (SqB, SkB, SqB, gB, ROPE, SCALE_B)):
                swapped = int(raw is SqA or raw is SqB)
                chain(dve.tensor_tensor(k, raw, over(g[:, 2 + swapped, :], w), ALU.mult))
                chain(dve.tensor_tensor(q, raw, over(g[:, swapped, :], w), ALU.mult))
                chain(dve.tensor_scalar(q, q, scale, None, ALU.mult))
            dve.wait_ge(s_rowsT, 1)
            chain(dve.tensor_copy(cols[:, :], bank(6)[:, 0:84]))
            dve.sem_inc(s_cols, 1)
            chain(dve.tensor_tensor(qk_gain, cols[:, 82:83], cols[:, 83:84], ALU.mult))
            chain(dve.tensor_scalar(qk_gain, qk_gain, SCALE_B, None, ALU.mult))
            dve.wait_ge(s_rstd, 1)
            for t in range(NT):
                dve.tensor_scalar(xt[:, t, :], xt[:, t, :], rstd[:, t:t + 1], None, ALU.mult).then_inc(s_xs, 1)
            dve.wait_ge(s_mod1, 4)
            bias = cols[:, 16:32].unsqueeze(2).to_broadcast([P, 16, 2])
            dve.tensor_tensor(modc[:, 0:16, :], pm[:, 0:16, :], bias, ALU.add).then_inc(s_A1, 1)
            dve.wait_ge(s_A1, 1)
            dve.tensor_scalar(A1, modc[:, 8:16, :], 1.0, None, ALU.add).then_inc(s_A1, 1)
            dve.wait_ge(s_A1, 2)
            gain = cols[:, 64:72].unsqueeze(2).to_broadcast([P, KT, 2])
            dve.tensor_tensor(A1, A1, gain, ALU.mult).then_inc(s_A1, 1)
            dve.wait_ge(s_A1, 3)
            for t in range(NT):
                y = min(t, 1)
                dve.wait_ge(s_xT, t + 1)
                for k in range(4):
                    ins = dve.tensor_scalar(hT[:, k, t * P:(t + 1) * P],
                                            bank(2 * (t % 2))[:, k * P:(k + 1) * P],
                                            A1[:, k, y:y + 1], modc[:, k, y:y + 1], ALU.mult, ALU.add)
                ins.then_inc(s_xeV, 1)

        @block.tensor
        def _(pe):
            pe.wait_ge(s_const, 16)
            pe.wait_ge(s_silu, 1)
            pe.transpose(bank(6)[:, 0:84], rows[0:84, :], ident[0:84, 0:84]).then_inc(s_rowsT, 1)
            pe.wait_ge(s_cols, 1)
            for c in range(4):
                mod_chunk(pe, c)
            for t in range(NT):
                pe.wait_ge(s_xs, t + 1)
                if t >= 2:
                    pe.wait_ge(s_xeV, t - 1)
                    pe.wait_ge(s_xeA, t - 1)
                for k in range(KT):
                    tr = pe.transpose(bank(2 * (t % 2), 2)[:, k * P:(k + 1) * P],
                                      xt[:, t, k * P:(k + 1) * P], ident[:, :])
                tr.then_inc(s_xT, 1)

    zs = [mem.at(M_SC + 960 * b, ZN) for b in range(2)]
    zq = [mem.at(M_SC + 1920 + 960 * b, ZN) for b in range(2)]
    zn = [mem.at(M_SC + 3840 + 960 * b, ZN) for b in range(2)]
    rot = mem.at(M_SC + 5760, 256)
    kgB = mem.at(M_SC + 6016, KVL)
    cache = mem.at(M_SC + 6144, 448)
    s_z = sem("s_z")
    s_zs = sem("s_zs")
    s_zq = sem("s_zq")
    s_zm = sem("s_zm")
    s_zr = sem("s_zr")
    s_zn = sem("s_zn")
    s_zT = sem("s_zT")
    s_zeV, s_zeA = sem("s_zeV"), sem("s_zeA")
    s_cache = sem("s_cache")
    s_out = sem("s_out")
    s_v2 = sem("s_v2")
    s_p2 = sem("s_p2")
    s_wq = sem("s_wq")
    s_vc = sem("s_vc")

    with nc.Block() as block:
        @block.sync
        def _(sp):
            for g in range(KVA):
                sp.dma_start(cache[:, g * HD:(g + 1) * HD], I["cache_gqa_k"][0, 0, g]).then_inc(s_cache, 16)
                sp.dma_start(vA[:, 1, g, :], I["cache_gqa_v"][0, 0, g]).then_inc(s_vc, 16)
            sp.dma_start(cache[:, 256:384], I["cache_mla_ckv"][0, 0]).then_inc(s_cache, 16)
            sp.dma_start(cache[:, 384:448], I["cache_mla_krope"][0, 0]).then_inc(s_cache, 16)
            sp.dma_start(kgB, I["mla_kva_g"].to_broadcast([P, KVL])).then_inc(s_cache, 16)
            for c in range(4, 8):
                sp.wait_ge(s_mod1, c - 3)
                sp.dma_start(wmod[c % 4], w_mod_v[:, :, c * 512:(c + 1) * 512]).then_inc(s_wm[c % 4], 16)
            sp.wait_ge(s_zn, 1)
            for g in range(KVA):
                sp.dma_start(O["gk"][0, 0, g], zn[0][:, Z_K + g * HD:Z_K + (g + 1) * HD]).then_inc(s_out, 16)
                sp.dma_start(O["gv"][0, 0, g], vA[:, 0, g, :]).then_inc(s_out, 16)
            sp.dma_start(O["ckv"][0, 0], zn[0][:, Z_CKV:Z_CKV + KVL]).then_inc(s_out, 16)
            sp.dma_start(O["kr"][0, 0], zn[0][:, Z_KR:Z_KR + ROPE]).then_inc(s_out, 16)
            sp.wait_ge(s_out, 16 * 6)

        @block.tensor
        def _(pe):
            pe.wait_ge(s_wz, 16)

            def project(t):
                b = 2 * (t % 2)
                if t >= 2:
                    pe.wait_ge(s_zs, t - 1)
                for c0, c1, bb in ((0, 512, b), (512, ZN, b + 1)):
                    for k in range(KT):
                        mm = pe.matmul(bank(bb)[:, 0:c1 - c0], hT[:, k, t * P:(t + 1) * P], wz[:, k, c0:c1],
                                       start=(k == 0), stop=(k == KT - 1))
                mm.then_inc(s_z, 1)

            def turn(t):
                if t < NT:
                    pe.wait_ge(s_zn, t + 1)
                    src = [zn[t % 2][:, o:o + w] for o, w in ((0, P), (P, P), (Z_CQ, P), (Z_CQ + P, P),
                                                              (Z_CKV, P), (Z_KR, ROPE))]
                    at = [0, 1, 2, 3, 4, 5]
                else:
                    pe.wait_ge(s_cache, 16 * 5)
                    src = [cache[:, o:o + w] for o, w in ((0, P), (P, P), (256, P), (384, ROPE))]
                    at = [0, 1, 4, 5]
                if t >= 1:
                    pe.wait_ge(s_zeV, t)
                    pe.wait_ge(s_zeA, t)
                for a, s in zip(at, src):
                    w = ROPE if a == 5 else P
                    tr = pe.transpose(bank(4, 2)[0:w, a * P:(a + 1) * P], s, ident[:, :])
                tr.then_inc(s_zT, 1)

            project(0)
            for t in range(1, NT):
                project(t)
                turn(t - 1)
            turn(NT - 1)
            turn(NT)

        @block.scalar
        def _(act):
            def take(t):
                act.wait_ge(s_z, t + 1)
                if t >= 2:
                    act.wait_ge(s_zn, t - 1)
                act.activation(zs[t % 2], psum[:, 1024 * (t % 2):1024 * (t % 2) + ZN], ACT.Copy).then_inc(s_zs, 1)
                act.wait_ge(s_zs, t + 1)
                act.activation(vA[:, key_col(t) // P, :, :].rearrange("p g d -> p (g d)"),
                               zs[t % 2][:, Z_V:Z_V + 256], ACT.Copy)
                act.activation(zq[t % 2], zs[t % 2], ACT.Square).then_inc(s_zq, 1)

            def untangle(t):
                act.wait_ge(s_zT, t + 1)
                c = key_col(t) if t < NT else P
                act.activation(ckvT[:, c:c + P], bank(5)[:, 0:P], ACT.Copy)
                act.activation(krT[:, c:c + P], bank(5)[0:ROPE, P:2 * P], ACT.Copy).then_inc(s_zeA, 1)

            take(0)
            take(1)
            for t in range(NT):
                untangle(t)
                if t + 2 < NT:
                    take(t + 2)
            untangle(NT)

        @block.gpsimd
        def _(pool):
            for t in range(NT):
                pool.wait_ge(s_zm, t + 1)
                pool.tensor_scalar(ss, ss, EPS, None, ALU.add).then_inc(s_p2, 1)
                pool.wait_ge(s_p2, t + 1)
                pool.tensor_tensor(rstd, ss, nhalf[:, 0:5], ALU.pow).then_inc(s_zr, 1)

        @block.vector
        def _(dve):
            chain = Chain(dve, s_v2)
            dve.wait_ge(s_cache, 16 * 5)

            def norms(t):
                z, q, n = zs[t % 2], zq[t % 2], zn[t % 2]
                dve.wait_ge(s_zq, t + 1)
                if t >= 1:
                    dve.wait_ge(s_zr, t)
                for a, b, c, w in ((0, 2, Z_K, HD), (2, 3, Z_CQ, QL), (3, 4, Z_CKV, KVL), (4, 5, Z_KR, ROPE)):
                    chain(dve.tensor_reduce(ss[:, a:b], q[:, c:c + (b - a) * w].rearrange("p (a w) -> p a w", w=w),
                                            AX_X, ALU.add))
                dve.tensor_tensor(ss, ss, invlen, ALU.mult).then_inc(s_zm, 1)
                dve.wait_ge(s_zr, t + 1)
                if t >= 2:
                    dve.wait_ge(s_zT, t - 1)
                if t == 2:
                    dve.wait_ge(s_out, 16 * 6)
                k3 = n[:, 0:256].rearrange("p (g d) -> p g d", g=KVA)
                z3 = z[:, 0:256].rearrange("p (g d) -> p g d", g=KVA)
                q3 = q[:, 0:256].rearrange("p (g d) -> p g d", g=KVA)
                r3 = rot.rearrange("p (g d) -> p g d", g=KVA)
                chain(dve.tensor_tensor(q3, z3, rstd[:, 0:2].unsqueeze(2).to_broadcast([P, KVA, HD]), ALU.mult))
                h = HD // 2
                for a, b in ((0, h), (h, 0)):
                    chain(dve.tensor_tensor(r3[:, :, a:a + h], q3[:, :, b:b + h],
                                            SkA[:, t, a:a + h].unsqueeze(1).to_broadcast([P, KVA, h]), ALU.mult))
                chain(dve.tensor_tensor(k3, q3, CkA[:, t, :].unsqueeze(1).to_broadcast([P, KVA, HD]), ALU.mult))
                chain(dve.tensor_tensor(k3, k3, r3, ALU.add))
                chain(dve.tensor_scalar(n[:, Z_CQ:Z_CQ + QL], z[:, Z_CQ:Z_CQ + QL], rstd[:, 2:3], None, ALU.mult))
                chain(dve.scalar_tensor_tensor(out=n[:, Z_CKV:Z_CKV + KVL], in0=z[:, Z_CKV:Z_CKV + KVL],
                                               scalar=rstd[:, 3:4], in1=kgB, op0=ALU.mult, op1=ALU.mult))
                zr, nr, qr = z[:, Z_KR:], n[:, Z_KR:], q[:, Z_KR:]
                h = ROPE // 2
                for a, b in ((0, h), (h, 0)):
                    chain(dve.scalar_tensor_tensor(out=qr[:, a:a + h], in0=zr[:, b:b + h], scalar=rstd[:, 4:5],
                                                   in1=SkB[:, t, a:a + h], op0=ALU.mult, op1=ALU.mult))
                chain(dve.scalar_tensor_tensor(out=nr[:, 0:ROPE], in0=zr[:, 0:ROPE], scalar=rstd[:, 4:5],
                                               in1=CkB[:, t, :], op0=ALU.mult, op1=ALU.mult))
                dve.tensor_tensor(nr[:, 0:ROPE], nr[:, 0:ROPE], qr[:, 0:ROPE], ALU.add).then_inc(s_zn, 1)

            def untangle(t):
                dve.wait_ge(s_zT, t + 1)
                c = key_col(t) if t < NT else P
                ins = dve.tensor_copy(kTA[:, :, c:c + P], bank(4)[:, 0:256].rearrange("p (g d) -> p g d", g=KVA))
                if t < NT:
                    for j in range(2):
                        ins = dve.tensor_scalar(cqT[:, j, t * P:(t + 1) * P], bank(4)[:, (2 + j) * P:(3 + j) * P],
                                                cols[:, 80 + j:81 + j], None, ALU.mult)
                ins.then_inc(s_zeV, 1)

            norms(0)
            norms(1)
            for t in range(NT):
                untangle(t)
                if t + 2 < NT:
                    norms(t + 2)
            untangle(NT)

    wq = mem.at(M_R + 6144, KT, HA * HD)
    G = mem.at(M_SC, 8, KT)
    Grow = mem.at(M_SC + 64, P, rows=64)
    s_m2 = sem("s_m2")
    s_G = sem("s_G")
    s_GT = sem("s_GT")
    s_Gr = sem("s_Gr")
    s_mrow = sem("s_mrow")
    with nc.Block() as block:
        @block.sync
        def _(sp):
            sp.dma_start(wq, w_in_v[:, :, C_QA:C_KA]).then_inc(s_wq, 16)
            for c in range(8, 12):
                sp.wait_ge(s_mod1, c - 3)
                sp.dma_start(wmod[c % 4], w_mod_v[:, :, c * 512:(c + 1) * 512]).then_inc(s_wm[c % 4], 16)
            sp.wait_ge(s_Gr, 1)
            sp.dma_start(S["mod_rows"], Grow).then_inc(s_mrow, 16)
            sp.wait_ge(s_mrow, 16)

        @block.tensor
        def _(pe):
            for c in range(4, 12):
                mod_chunk(pe, c)
            pe.wait_ge(s_G, 5)
            pe.transpose(bank(6)[0:64, 0:P], G.rearrange("p a k -> p (a k)"), ident[:, :]).then_inc(s_GT, 1)

        @block.vector
        def _(dve):
            dve.wait_ge(s_mod1, 12)
            bias = cols[:, 32:64].unsqueeze(2).to_broadcast([P, 32, 2])
            dve.tensor_tensor(modc[:, 16:48, :], pm[:, 16:48, :], bias, ALU.add).then_inc(s_m2, 1)
            dve.wait_ge(s_m2, 1)
            for a, c in ((0, 40), (2, 16), (4, 32), (6, 24)):
                dve.tensor_copy(G[:, a:a + 2, :], modc[:, c:c + KT, :].rearrange("p k y -> p y k")).then_inc(s_G, 1)
            dve.wait_ge(s_G, 4)
            gain = cols[:, 72:80].unsqueeze(1).to_broadcast([P, 2, KT])
            dve.scalar_tensor_tensor(out=G[:, 4:6, :], in0=G[:, 4:6, :], scalar=1.0, in1=gain,
                                     op0=ALU.add, op1=ALU.mult).then_inc(s_G, 1)
            dve.wait_ge(s_GT, 1)
            dve.tensor_copy(Grow, bank(6)[0:64, 0:P]).then_inc(s_Gr, 1)

    hz = mem.at(M_SC, 960)
    hq = mem.at(M_SC + 960, 960)
    hr = mem.at(M_SC + 1920, 640)
    qTh = mem.at(M_SC + 2560, TOK)
    qrT = mem.at(M_SC + 3200, TOK, rows=ROPE)
    pr = [mem.at(M_SC + 3840 + 640 * b, 640) for b in range(2)]
    pT = mem.at(M_SC + 5120, 5, LAT)
    pTc = mem.at(M_SC + 7680, P)
    vh = mem.at(M_SC + 7808, NK, VD)
    nmax = small[:, 48:53]
    rsum = small[:, 56:61]
    rinv = small[:, 64:69]
    hss = small[:, 72:82]
    hrs = small[:, 88:98]
    pZ, pS, pT_ps, pO, pC = psum[:, 0:1024], psum[:, 1024:2048], psum[:, 2048:3072], bank(6), bank(7)[:, 0:P]
    KEY_TILES = [2, 3, 4, 5, 1]

    def attend(kind, wqh, oT, kT_of, v_of, s_w):
        mla = kind == "b"
        names = ("S", "nm", "exp", "ri", "pn", "T", "TeV", "TeA", "Z", "sq", "ss", "ms", "rs", "qn", "rot", "q",
                 "QT", "qe", "O", "Oe", "vh", "qr")
        s = {n: nc.alloc_semaphore(name=f"s_{kind}_{n}") for n in names}
        nh = HA
        W = (NOPE + ROPE) if mla else HD
        NS = 2 if mla else 1

        with nc.Block() as block:
            @block.tensor
            def _(pe):
                pe.wait_ge(s_w, 16)

                def project(h, t):
                    if mla:
                        for k in range(2):
                            pe.matmul(pZ[:, t * P:(t + 1) * P], cqT[:, k, t * P:(t + 1) * P],
                                      wqh[:, k, bass.ds(h * W, NOPE)], start=(k == 0), stop=(k == 1))
                        for k in range(2):
                            mm = pe.matmul(pZ[:, 640 + t * ROPE:640 + (t + 1) * ROPE], cqT[:, k, t * P:(t + 1) * P],
                                           wqh[:, k, bass.ds(h * W + NOPE, ROPE)], start=(k == 0), stop=(k == 1))
                    else:
                        for k in range(KT):
                            mm = pe.matmul(pZ[:, t * P:(t + 1) * P], hT[:, k, t * P:(t + 1) * P],
                                           wqh[:, k, bass.ds(h * W, W)], start=(k == 0), stop=(k == KT - 1))
                    if t == NT - 1:
                        mm.then_inc(s["Z"], 1)

                def turn_q(h):
                    pe.wait_ge(s["q"], h + 1)
                    for t in range(NT):
                        tr = pe.transpose(pZ[:, t * P:(t + 1) * P], hq[:, t * P:(t + 1) * P], ident[:, :])
                    tr.then_inc(s["QT"], 1)
                    if mla:
                        pe.wait_ge(s["qe"], 2 * h + 1)
                        pe.matmul(pZ[0:ROPE, 0:P], hq[:, 640:640 + ROPE], ident[:, :], start=True, stop=True)
                        for t in range(1, NT):
                            tr = pe.transpose(pZ[0:ROPE, t * P:(t + 1) * P],
                                              hq[:, 640 + t * ROPE:640 + (t + 1) * ROPE], ident[:, :])
                        tr.then_inc(s["qr"], 1)

                def scores(h, t):
                    if t == 0:
                        pe.wait_ge(s["qe"], NS * h + NS)
                    else:
                        pe.wait_ge(s["exp"], NT * h + t)
                    kT = kT_of(h)
                    q = qTh[:, t * P:(t + 1) * P]
                    r = qrT[:, t * P:(t + 1) * P]
                    parts = [(0, 0, P)] if t == 0 else [(0, 2 * P, LAT), (LAT, P, P)]
                    for o, c, w in parts:
                        mm = pe.matmul(pS[:, o:o + w], q, kT(c, w), start=True, stop=not mla)
                        if mla:
                            mm = pe.matmul(pS[:, o:o + w], r, krT[:, c:c + w], start=False, stop=True)
                    mm.then_inc(s["S"], 1)

                def turn_p(h, t):
                    pe.wait_ge(s["pn"], NT * h + t + 1)
                    if t >= 1:
                        pe.wait_ge(s["TeV"], NT * h + t)
                        if t >= 2:
                            pe.wait_ge(s["TeA"], (NT - 1) * h + t - 1)
                    for j in range(1 if t == 0 else 5):
                        tr = pe.transpose(pT_ps[:, j * P:(j + 1) * P], pr[t % 2][:, j * P:(j + 1) * P], ident[:, :])
                    tr.then_inc(s["T"], 1)

                def values(h):
                    pe.wait_ge(s["TeV"], NT * h + NT)
                    pe.wait_ge(s["TeA"], (NT - 1) * (h + 1))
                    pe.wait_ge(s["vh"], h + 1)
                    pe.wait_ge(s["Oe"], h + 1)
                    pe.matmul(pC, vh[:, 0, :], pTc, start=True, stop=True)
                    for j, kt in enumerate(KEY_TILES):
                        mm = pe.matmul(pO, vh[:, kt, :], pT[:, j, :], start=(j == 0), stop=(j == 4))
                    mm.then_inc(s["O"], 1)

                def head(h, more):
                    for t in range(NT):
                        scores(h, t)
                        if more:
                            project(h + 1, t)
                        if t >= 1:
                            turn_p(h, t - 1)
                    turn_p(h, NT - 1)
                    if more:
                        turn_q(h + 1)
                    values(h)

                for t in range(NT):
                    project(0, t)
                turn_q(0)
                with pe.Fori(0, nh - 1) as h:
                    head(h, True)
                head(nh - 1, False)

            @block.scalar
            def _(act):
                def squares(h):
                    act.wait_ge(s["Z"], h + 1)
                    n = 960 if mla else 640
                    act.activation(hz[:, 0:n], pZ[:, 0:n], ACT.Square).then_inc(s["sq"], 1)

                def take_q(h):
                    act.wait_ge(s["QT"], h + 1)
                    if mla:
                        act.activation(qTh, pZ[:, 0:TOK], ACT.Copy, scale=qk_gain).then_inc(s["qe"], 1)
                        act.wait_ge(s["qr"], h + 1)
                        act.activation(qrT, pZ[0:ROPE, 0:TOK], ACT.Copy).then_inc(s["qe"], 1)
                    else:
                        act.activation(qTh, pZ[:, 0:TOK], ACT.Copy).then_inc(s["qe"], 1)

                def take_p(h, t):
                    act.wait_ge(s["T"], NT * h + t + 1)
                    act.activation(pT[:, 4, (t - 1) * P:t * P], pT_ps[:, 512:640], ACT.Copy).then_inc(s["TeA"], 1)

                def head(h, more):
                    for t in range(NT):
                        w = P if t == 0 else 640
                        act.wait_ge(s["nm"], NT * h + t + 1)
                        if t >= 2:
                            act.wait_ge(s["T"], NT * h + t - 1)
                        act.activation(pr[t % 2][:, 0:w], pS[:, 0:w], ACT.Exp, bias=nmax[:, t:t + 1],
                                       accum_out=rsum[:, t:t + 1]).then_inc(s["exp"], 1)
                        if t >= 2:
                            take_p(h, t - 1)
                    if more:
                        squares(h + 1)
                    take_p(h, NT - 1)
                    if more:
                        take_q(h + 1)
                    act.wait_ge(s["O"], h + 1)
                    act.activation(oT[:, bass.ds(h, 1), 0:P].rearrange("p a t -> p (a t)"), pC, ACT.Copy)
                    act.activation(oT[:, bass.ds(h, 1), P:TOK].rearrange("p a t -> p (a t)"), pO,
                                   ACT.Copy).then_inc(s["Oe"], 1)

                act.sem_inc(s["Oe"], 1)
                squares(0)
                take_q(0)
                with act.Fori(0, nh - 1) as h:
                    head(h, True)
                head(nh - 1, False)

            @block.gpsimd
            def _(pool):
                ns = NT * NS

                def prep(h):
                    pool.wait_ge(s["ms"], h + 1)
                    pool.tensor_tensor(hrs[:, 0:ns], hss[:, 0:ns], nhalf[:, 0:ns], ALU.pow).then_inc(s["rs"], 1)

                def copy_v(h):
                    pool.tensor_copy(vh, v_of(h)).then_inc(s["vh"], 1)

                prep(0)
                copy_v(0)
                with pool.Fori(0, nh - 1) as h:
                    prep(h + 1)
                    pool.wait_ge(s["O"], h + 1)
                    copy_v(h + 1)

            @block.vector
            def _(dve):
                def prep(h):
                    dve.wait_ge(s["sq"], h + 1)
                    a = hz[:, 0:640].rearrange("p (t d) -> p t d", t=NT)
                    ins = dve.tensor_reduce(hss[:, 0:NT], a, AX_X, ALU.add)
                    if mla:
                        b = hz[:, 640:960].rearrange("p (t d) -> p t d", t=NT)
                        ins.then_inc(s["ss"], 1)
                        dve.tensor_reduce(hss[:, NT:2 * NT], b, AX_X, ALU.add).then_inc(s["ss"], 1)
                        dve.wait_ge(s["ss"], 3 * h + 2)
                        dve.tensor_scalar(hss[:, 0:NT], hss[:, 0:NT], 1.0 / HD, EPS, ALU.mult, ALU.add)\
                           .then_inc(s["ss"], 1)
                        dve.tensor_scalar(hss[:, NT:2 * NT], hss[:, NT:2 * NT], 1.0 / ROPE, EPS, ALU.mult, ALU.add)\
                           .then_inc(s["ms"], 1)
                    else:
                        ins.then_inc(s["ss"], 1)
                        dve.wait_ge(s["ss"], h + 1)
                        dve.tensor_scalar(hss[:, 0:NT], hss[:, 0:NT], 1.0 / HD, EPS, ALU.mult, ALU.add)\
                           .then_inc(s["ms"], 1)
                    dve.wait_ge(s["rs"], h + 1)
                    w = ROPE if mla else HD
                    o = 640 if mla else 0
                    z3 = pZ[:, o:o + NT * w].rearrange("p (t d) -> p t d", t=NT)
                    n3 = hz[:, o:o + NT * w].rearrange("p (t d) -> p t d", t=NT)
                    q3 = hq[:, o:o + NT * w].rearrange("p (t d) -> p t d", t=NT)
                    r3 = hr[:, 0:NT * w].rearrange("p (t d) -> p t d", t=NT)
                    C, Sn = (CqB, SqB) if mla else (CqA, SqA)
                    rs = hrs[:, NT * (NS - 1):NT * NS].unsqueeze(2).to_broadcast([P, NT, w])
                    if mla:
                        dve.tensor_tensor(hq[:, 0:640].rearrange("p (t d) -> p t d", t=NT),
                                          pZ[:, 0:640].rearrange("p (t d) -> p t d", t=NT),
                                          hrs[:, 0:NT].unsqueeze(2).to_broadcast([P, NT, NOPE]), ALU.mult)
                    dve.tensor_tensor(n3, z3, rs, ALU.mult).then_inc(s["qn"], 1)
                    dve.wait_ge(s["qn"], h + 1)
                    x = w // 2
                    dve.tensor_tensor(r3[:, :, 0:x], n3[:, :, x:w], Sn[:, :, 0:x], ALU.mult).then_inc(s["rot"], 1)
                    dve.tensor_tensor(r3[:, :, x:w], n3[:, :, 0:x], Sn[:, :, x:w], ALU.mult).then_inc(s["rot"], 1)
                    dve.tensor_tensor(q3, n3, C, ALU.mult).then_inc(s["rot"], 1)
                    dve.wait_ge(s["rot"], 3 * h + 3)
                    dve.tensor_tensor(q3, q3, r3, ALU.add).then_inc(s["q"], 1)

                def maximum(h, t):
                    w = P if t == 0 else 640
                    dve.wait_ge(s["S"], NT * h + t + 1)
                    dve.tensor_reduce(nmax[:, t:t + 1], pS[:, 0:w], AX_X, ALU.max, negate=True).then_inc(s["nm"], 1)

                def normalise(h, t):
                    w = P if t == 0 else 640
                    dve.wait_ge(s["exp"], NT * h + t + 1)
                    dve.reciprocal(rinv[:, t:t + 1], rsum[:, t:t + 1]).then_inc(s["ri"], 1)
                    dve.wait_ge(s["ri"], NT * h + t + 1)
                    dve.tensor_scalar(pr[t % 2][:, 0:w], pr[t % 2][:, 0:w], rinv[:, t:t + 1], None, ALU.mult)\
                       .then_inc(s["pn"], 1)

                def take_p(h, t):
                    dve.wait_ge(s["T"], NT * h + t + 1)
                    if t == 0:
                        dve.tensor_copy(pTc, pT_ps[:, 0:P]).then_inc(s["TeV"], 1)
                    else:
                        dve.tensor_copy(pT[:, 0:4, (t - 1) * P:t * P],
                                        pT_ps[:, 0:512].rearrange("p (j q) -> p j q", j=4)).then_inc(s["TeV"], 1)

                def head(h, more):
                    for t in range(NT):
                        maximum(h, t)
                        normalise(h, t)
                        if t >= 1:
                            take_p(h, t - 1)
                    take_p(h, NT - 1)
                    if more:
                        prep(h + 1)

                prep(0)
                with dve.Fori(0, nh - 1) as h:
                    head(h, True)
                head(nh - 1, False)

        nc.clear_and_free_semaphores(list(s.values()))
        nc.all_engine_barrier()

    def kT_gqa(h):
        return lambda c, w: kTA[:, h // (HA // KVA), c:c + w] if isinstance(h, int) else \
            kTA[:, bass.ds(h // (HA // KVA), 1), c:c + w].rearrange("p a k -> p (a k)")

    def v_gqa(h):
        if isinstance(h, int):
            return vA[:, :, h // (HA // KVA), :]
        return vA[:, :, bass.ds(h // (HA // KVA), 1), :].rearrange("p k a d -> p k (a d)")

    attend("a", wq, oA, kT_gqa, v_gqa, s_wq)

    kB = mem.at(M_R, HB, KEYS)
    vB = mem.at(M_R + 6144, NK, HB, VD)
    wqb = mem.at(M_R + 12288, 2, HB * (NOPE + ROPE))
    wkvb = mem.at(M_SC, HB * (NOPE + VD))
    kz = mem.at(M_SC + 2048, KEYS)
    kn = mem.at(M_SC + 2816, KEYS)
    kss = small[:, 100:106]
    krs = small[:, 108:114]
    s_wqb = sem("s_wqb")
    s_wkvb = sem("s_wkvb")
    names = ("kv", "sq", "ss", "ms", "rs", "kn", "v", "T", "e")
    sk = {n: sem(f"s_k_{n}") for n in names}
    pKV = psum[:, 0:1536]
    pKT = psum[:, 1536:2560]
    with nc.Block() as block:
        @block.sync
        def _(sp):
            sp.dma_start(wkvb, I["w_kvb"][0]).then_inc(s_wkvb, 16)
            sp.dma_start(wqb, I["w_qb"][0].rearrange("(k p) n -> p k n", p=P)).then_inc(s_wqb, 16)

        @block.tensor
        def _(pe):
            pe.wait_ge(s_wkvb, 16)

            def expand(h):
                for part in range(2):
                    for kt in range(NK):
                        mm = pe.matmul(pKV[:, (part * NK + kt) * P:(part * NK + kt + 1) * P],
                                       ckvT[:, kt * P:(kt + 1) * P], wkvb[:, bass.ds(h * 256 + part * P, P)],
                                       start=True, stop=True)
                mm.then_inc(sk["kv"], 1)

            def turn(h):
                pe.wait_ge(sk["kn"], h + 1)
                for kt in range(NK):
                    tr = pe.transpose(pKT[:, kt * P:(kt + 1) * P], kn[:, kt * P:(kt + 1) * P], ident[:, :])
                tr.then_inc(sk["T"], 1)

            expand(0)
            with pe.Fori(0, HB - 1) as h:
                pe.wait_ge(sk["kn"], h + 1)
                pe.wait_ge(sk["v"], h + 1)
                expand(h + 1)
                turn(h)
            turn(HB - 1)

        @block.scalar
        def _(act):
            with act.Fori(0, HB) as h:
                act.wait_ge(sk["kv"], h + 1)
                act.activation(kz, pKV[:, 0:KEYS], ACT.Square).then_inc(sk["sq"], 1)
                act.wait_ge(sk["kn"], h + 1)
                act.activation(vB[:, :, bass.ds(h, 1), :].rearrange("p k a d -> p k (a d)"),
                               pKV[:, KEYS:2 * KEYS].rearrange("p (k d) -> p k d", k=NK), ACT.Copy)\
                   .then_inc(sk["v"], 1)

        @block.gpsimd
        def _(pool):
            with pool.Fori(0, HB) as h:
                pool.wait_ge(sk["ms"], h + 1)
                pool.tensor_tensor(krs, kss, nhalf[:, 0:NK], ALU.pow).then_inc(sk["rs"], 1)

        @block.vector
        def _(dve):
            def norm(h, first):
                dve.wait_ge(sk["sq"], h + 1)
                dve.tensor_reduce(kss, kz.rearrange("p (k d) -> p k d", k=NK), AX_X, ALU.add).then_inc(sk["ss"], 1)
                dve.wait_ge(sk["ss"], h + 1)
                dve.tensor_scalar(kss, kss, 1.0 / NOPE, EPS, ALU.mult, ALU.add).then_inc(sk["ms"], 1)
                dve.wait_ge(sk["rs"], h + 1)
                if not first:
                    dve.wait_ge(sk["T"], h)
                dve.tensor_tensor(kn.rearrange("p (k d) -> p k d", k=NK),
                                  pKV[:, 0:KEYS].rearrange("p (k d) -> p k d", k=NK),
                                  krs.unsqueeze(2).to_broadcast([P, NK, NOPE]), ALU.mult).then_inc(sk["kn"], 1)

            def take(h):
                dve.wait_ge(sk["T"], h + 1)
                dve.tensor_copy(kB[:, bass.ds(h, 1), :].rearrange("p a k -> p (a k)"), pKT[:, 0:KEYS])\
                   .then_inc(sk["e"], 1)

            norm(0, True)
            with dve.Fori(0, HB - 1) as h:
                take(h)
                norm(h + 1, False)
            take(HB - 1)

    attend("b", wqb, oB,
           lambda h: (lambda c, w: kB[:, bass.ds(h, 1), c:c + w].rearrange("p a k -> p (a k)")),
           lambda h: vB[:, :, bass.ds(h, 1), :].rearrange("p k a d -> p k (a d)"), s_wqb)

    wm = [[mem.at(M_R + 4096 * b + 1024 * q, KT, P) for q in range(4)] for b in range(2)]
    mT = mem.at(M_R + 8192, KT, TOK)
    wout = mem.at(M_SC, KT, D)
    HALF = TOK // 2
    sig = [mem.at(M_TB + 640 * b, 2, HALF) for b in range(2)]
    mx = [mem.at(M_TB + 1280 + 640 * b, 2, HALF) for b in range(2)]
    s_mw = [sem(f"s_mw{b}") for b in range(2)]
    s_wout = sem("s_wout")
    names = ("mm", "sig", "x", "m")
    sg = {n: [sem(f"s_g_{n}{f}") for f in range(2)] for n in names}
    with nc.Block() as block:
        @block.sync
        def _(sp):
            w_oa_v = I["w_oa"][0].rearrange("(k p) n -> p k n", p=P)
            w_ob_v = I["w_ob"][0].rearrange("(k p) n -> p k n", p=P)

            def load(j, b):
                for q, (w, c) in enumerate(((w_in_v, C_GA), (w_oa_v, 0), (w_in_v, C_GB), (w_ob_v, 0))):
                    sp.dma_start(wm[b][q], w[:, :, bass.ds(j * P + c, P)]).then_inc(s_mw[b], 16)

            load(0, 0)
            load(1, 1)
            sp.dma_start(wout, I["w_out"][0].rearrange("(k p) n -> p k n", p=P)).then_inc(s_wout, 16)
            with sp.Fori(1, KT // 2) as i:
                for b in range(2):
                    sp.wait_ge(sg["mm"][1], 2 * i - 1 + b)
                    load(2 * i + b, b)

        @block.tensor
        def _(pe):
            def chunk(i, b, first):
                pe.wait_ge(s_mw[b], 64 * (i + 1))
                for f in range(2):
                    if not first:
                        pe.wait_ge(sg["m"][f], 2 * i + b)
                    for q, src in enumerate((hT, oA, hT, oB)):
                        for k in range(KT):
                            mm = pe.matmul(bank(4 * f + q)[:, 0:HALF], wm[b][q][:, k, :],
                                           src[:, k, f * HALF:(f + 1) * HALF], start=(k == 0), stop=(k == KT - 1))
                    mm.then_inc(sg["mm"][f], 1)

            chunk(0, 0, True)
            chunk(0, 1, False)
            with pe.Fori(1, KT // 2) as i:
                for b in range(2):
                    chunk(i, b, False)

        @block.scalar
        def _(act):
            def gates(j, f, first):
                act.wait_ge(sg["mm"][f], j + 1)
                if not first:
                    act.wait_ge(sg["m"][f], j)
                for g in range(2):
                    ins = act.activation(sig[f][:, g, :], bank(4 * f + 2 * g)[:, 0:HALF], ACT.Sigmoid)
                ins.then_inc(sg["sig"][f], 1)

            for f in range(2):
                gates(0, f, True)
            with act.Fori(1, KT) as j:
                for f in range(2):
                    gates(j, f, False)

        @block.vector
        def _(dve):
            with dve.Fori(0, KT) as j:
                for f in range(2):
                    dve.wait_ge(sg["sig"][f], j + 1)
                    for g in range(2):
                        dve.tensor_tensor(mx[f][:, g, :], sig[f][:, g, :], bank(4 * f + 2 * g + 1)[:, 0:HALF],
                                          ALU.mult).then_inc(sg["x"][f], 1)
                    dve.wait_ge(sg["x"][f], 2 * j + 2)
                    dve.tensor_tensor(mT[:, bass.ds(j, 1), f * HALF:(f + 1) * HALF].rearrange("p a t -> p (a t)"),
                                      mx[f][:, 0, :], mx[f][:, 1, :], ALU.add).then_inc(sg["m"][f], 1)

    modb = mem.at(M_OA, 8, D)
    h2T = hT
    x1 = mem.at(M_TB, NT, D)
    xres = [mem.at(M_TB + 5120 + 1024 * b, D) for b in range(2)]
    h2 = mem.at(M_TB + 7168, D)
    h2p = mem.at(M_TB + 8192, D)
    wr = mem.at(M_OB + 3072, KT, NE)
    rbias = sb("rbias", [P, NE])
    sc = mem.at(M_OB + 3584, NT, NE)
    RS1, RS2 = small[:, 0:1], small[:, 1:2]
    s_modb = sem("s_modb")
    s_wr = sem("s_wr")
    s_rb = sem("s_rb")
    s_xr = [sem(f"s_xr{b}") for b in range(2)]
    s_hp = sem("s_hp")
    names = ("a", "x", "sq", "ms", "rs", "h", "hp", "T", "teV", "teA", "lg", "sc", "c")
    sr = {n: sem(f"s_r_{n}") for n in names}
    with nc.Block() as block:
        @block.sync
        def _(sp):
            sp.wait_ge(s_mrow, 16)
            mr = S["mod_rows"].rearrange("(a k) p -> a (k p)", a=8)
            sp.dma_start(xres[0], I["x_prompt"][0]).then_inc(s_xr[0], 16)
            for a in (2, 3, 4, 5, 6, 7, 0, 1):
                sp.dma_start(modb[:, a, :], mr[a:a + 1, :].to_broadcast([P, D])).then_inc(s_modb, 16)
            sp.dma_start(xres[1], I["x_sample"][0, 0:P, :]).then_inc(s_xr[1], 16)
            sp.dma_start(wr, I["w_router"][0].rearrange("(k p) n -> p k n", p=P)).then_inc(s_wr, 16)
            sp.dma_start(rbias[:, :], I["router_bias"].to_broadcast([P, NE])).then_inc(s_rb, 16)
            for t in range(NT):
                if t >= 1 and t + 1 < NT:
                    sp.wait_ge(sr["x"], 2 * t)
                    sp.dma_start(xres[(t + 1) % 2], I["x_sample"][0, t * P:(t + 1) * P, :])\
                      .then_inc(s_xr[(t + 1) % 2], 16)
                sp.wait_ge(sr["hp"], t + 1)
                sp.dma_start(S["h2"][t * P:(t + 1) * P, :], h2p).then_inc(s_hp, 16)

        @block.tensor
        def _(pe):
            pe.wait_ge(s_wout, 16)

            def out_proj(t):
                if t >= 2:
                    pe.wait_ge(sr["x"], 2 * (t - 2) + 2)
                for c in range(2):
                    for k in range(KT):
                        mm = pe.matmul(bank(2 * (t % 2) + c), mT[:, k, t * P:(t + 1) * P],
                                       wout[:, k, c * 512:(c + 1) * 512], start=(k == 0), stop=(k == KT - 1))
                mm.then_inc(sr["a"], 1)

            def turn(t):
                pe.wait_ge(sr["h"], 2 * (t + 1))
                if t >= 1:
                    pe.wait_ge(sr["teV"], t)
                    pe.wait_ge(sr["teA"], t)
                for k in range(KT):
                    tr = pe.transpose(bank(4, 2)[:, k * P:(k + 1) * P], h2[:, k * P:(k + 1) * P], ident[:, :])
                tr.then_inc(sr["T"], 1)

            def router(t):
                if t == 0:
                    pe.wait_ge(s_wr, 16)
                pe.wait_ge(sr["teV"], t + 1)
                pe.wait_ge(sr["teA"], t + 1)
                if t >= 1:
                    pe.wait_ge(sr["sc"], t)
                for k in range(KT):
                    mm = pe.matmul(bank(6)[:, t * NE:(t + 1) * NE], h2T[:, k, t * P:(t + 1) * P], wr[:, k, :],
                                   start=(k == 0), stop=(k == KT - 1))
                mm.then_inc(sr["lg"], 1)

            out_proj(0)
            for t in range(1, NT):
                out_proj(t)
                turn(t - 1)
                router(t - 1)
            turn(NT - 1)
            router(NT - 1)

        @block.scalar
        def _(act):
            for t in range(NT):
                act.wait_ge(sr["x"], 2 * t + 2)
                if t >= 1:
                    act.wait_ge(sr["hp"], t)
                    act.wait_ge(s_hp, 16 * t)
                act.activation(h2p, x1[:, t, :], ACT.Square, accum_out=RS1).then_inc(sr["sq"], 1)
                act.wait_ge(sr["h"], 2 * t + 2)
                act.activation(h2p.rearrange("q (k p) -> q k p", k=KT), h2.rearrange("q (p k) -> q k p", k=KT),
                               ACT.Copy).then_inc(sr["hp"], 1)
                act.wait_ge(sr["T"], t + 1)
                act.activation(h2T[:, 4:8, t * P:(t + 1) * P], bank(5).rearrange("p (k t) -> p k t", k=4), ACT.Copy)\
                   .then_inc(sr["teA"], 1)
                act.wait_ge(sr["lg"], t + 1)
                act.activation(sc[:, t, :], bank(6)[:, t * NE:(t + 1) * NE], ACT.Sigmoid).then_inc(sr["sc"], 1)

        @block.gpsimd
        def _(pool):
            for t in range(NT):
                pool.wait_ge(sr["sq"], t + 1)
                pool.tensor_scalar(RS1, RS1, 1.0 / D, EPS, ALU.mult, ALU.add).then_inc(sr["ms"], 1)
                pool.wait_ge(sr["ms"], t + 1)
                pool.tensor_tensor(RS2, RS1, nhalf[:, 0:1], ALU.pow).then_inc(sr["rs"], 1)

        @block.vector
        def _(dve):
            dve.wait_ge(s_modb, 16 * 8)
            for t in range(NT):
                y = min(t, 1)
                dve.wait_ge(sr["a"], t + 1)
                dve.wait_ge(s_xr[t % 2], 16 * (t // 2 + 1))
                dve.tensor_tensor(x1[:, t, :], bank(2 * (t % 2), 2), modb[:, 2 + y, :], ALU.mult)\
                   .then_inc(sr["x"], 1)
                dve.wait_ge(sr["x"], 2 * t + 1)
                dve.tensor_tensor(x1[:, t, :], x1[:, t, :], xres[t % 2], ALU.add).then_inc(sr["x"], 1)
                dve.wait_ge(sr["rs"], t + 1)
                if t >= 1:
                    dve.wait_ge(sr["T"], t)
                    dve.wait_ge(sr["hp"], t)
                dve.scalar_tensor_tensor(out=h2, in0=x1[:, t, :], scalar=RS2, in1=modb[:, 4 + y, :],
                                         op0=ALU.mult, op1=ALU.mult).then_inc(sr["h"], 1)
                dve.wait_ge(sr["h"], 2 * t + 1)
                dve.tensor_tensor(h2, h2, modb[:, 6 + y, :], ALU.add).then_inc(sr["h"], 1)
                dve.wait_ge(sr["T"], t + 1)
                dve.tensor_copy(h2T[:, 0:4, t * P:(t + 1) * P], bank(4).rearrange("p (k t) -> p k t", k=4))\
                   .then_inc(sr["teV"], 1)

    g2b = modb[:, 0:2, :]
    ysh = mem.at(M_OA + 2048, NT, D)
    w13 = [mem.at(M_R + 6144 * u, 2, KT, FE) for u in range(RING)]
    w2 = [mem.at(M_R + 6144 * u + 4096, 2, D) for u in range(RING)]
    SH = RING - 1
    B0 = M_TB + 5120
    hs = mem.at(B0, FE)
    gg = mem.at(B0 + 256, FE)
    gT = mem.at(B0 + 512, 2, P)
    rt = mem.at(B0 + 768, 3840)

    def rv(n, *shape):
        off = n * 320
        v = rt[:, off:off + int(np.prod(shape))]
        return v.rearrange("p (a b) -> p a b", a=shape[0]) if len(shape) == 2 else v

    biased, msk, rep, sel, wn = (rv(n, NT, NE) for n in range(5))
    gm8 = rt[:, 1600:1920].rearrange("p (a b) -> p a b", b=8)
    posv, jv, gsel = (rv(n, NT, NE) for n in (6, 7, 8))
    ostart, oend = rt[:, 2880:2944], rt[:, 2944:3008]
    gs, rank, wsum = rt[:, 3008:3048], rt[:, 3048:3088], rt[:, 3088:3093]
    m8 = rt[:, 3096:3136].rearrange("p (t k) -> p t k", k=8)
    k8 = rt[:, 3136:3176].rearrange("p (t k) -> p t k", k=8)
    w8 = rt[:, 3176:3216].rearrange("p (t k) -> p t k", k=8)
    oblk, oblkb = rt[0:NE, 3216:3217], rt[0:NE, 3220:3348]
    ecol = rt[:, 3349:3350]
    cnt = rt[0:NE, 3350:3351]
    eqb = mem.at(M_OB + 2048, TOPK * NE)
    cst = sb("cst", [P, 128 + 128 + 64 + 64 + 1 + 64 + 64])
    tri, ones = cst[:, 0:128], cst[:, 128:256]
    enum, gtri, pnum = cst[:, 256:320], cst[:, 320:384], cst[:, 384:385]
    triX, triI = cst[0:NE, 385:449], cst[0:NE, 449:513]
    recs = sb("recs", [P, NT * TOPK, 4], I32)
    kidx = sb("kidx", [P, NT * TOPK], I32)
    tabs = sb("tabs", [P, NBLK + RING, 4], I32)
    ove = sb("ove", [1, P], I32)
    nblk = sb("nblk", [1, 1], I32)
    s_cst = sem("s_cst")
    s_rec = sem("s_rec")
    s_tin = sem("s_tin")
    s_tz = sem("s_tz")
    s_shw = sem("s_shw")
    s_rv = sem("s_rv")
    s_sel = sem("s_sel")
    s_pos = sem("s_pos")
    s_cnt = sem("s_cnt")
    s_ob = sem("s_ob")
    s_os = sem("s_os")
    s_ec = sem("s_ec")
    s_er = sem("s_er")
    s_ove = sem("s_ove")
    s_k8 = sem("s_k8")
    s_tsc = sem("s_tsc")
    s_tab = sem("s_tab")
    s_w13 = [sem(f"s_w13_{u}") for u in range(RING)]
    s_w2 = [sem(f"s_w2_{u}") for u in range(RING)]
    names = ("h", "si", "g", "T", "te", "y", "ye")
    sh = {n: sem(f"s_sh_{n}") for n in names}
    w13_src = [I[n][0].rearrange("e (p k) n -> p e k n", k=KT) for n in ("w_e1", "w_e3")]
    w2_src = I["w_e2"][0].rearrange("e (f p) n -> p e f n", p=P)

    def load_w13(sp, n, u):
        for a in range(2):
            sp.dma_start(w13[u][:, a], w13_src[a][:, bass.ds(n, 1)].rearrange("p e k n -> p (e k) n"))\
              .then_inc(s_w13[u], 16)

    def load_w2(sp, n, u):
        sp.dma_start(w2[u], w2_src[:, bass.ds(n, 1)].rearrange("p e f n -> p (e f) n")).then_inc(s_w2[u], 16)

    with nc.Block() as block:
        @block.sync
        def _(sp):
            sp.dma_start(cst[:, :], I["route_consts"]).then_inc(s_cst, 16)
            for a, n in enumerate(("w_s1", "w_s3")):
                sp.dma_start(w13[SH][:, a], I[n][0].rearrange("(k p) n -> p k n", p=P)).then_inc(s_shw, 16)
            sp.dma_start(w2[SH], I["w_s2"][0].rearrange("(f p) n -> p f n", p=P)).then_inc(s_shw, 16)
            sp.dma_start(recs[:, :, :], I["records"]).then_inc(s_rec, 16)
            sp.dma_start(tabs[:, 0:NBLK, :], I["empty_slots"]).then_inc(s_tz, 16)
            sp.wait_ge(s_tz, 16)
            sp.dma_start(S["slots"].rearrange("(p n) w -> p n w", n=NBLK), tabs[:, 0:NBLK, :]).then_inc(s_tin, 16)
            for u in range(SH):
                load_w13(sp, u, u)
                load_w2(sp, u, u)
            sp.wait_ge(s_tsc, 16 * NT * TOPK)
            sp.dma_start(tabs[:, 0:NBLK, :], S["slots"].rearrange("(p n) w -> p n w", n=NBLK)).then_inc(s_tab, 16)

        @block.tensor
        def _(pe):
            def up(t):
                if t >= 1:
                    pe.wait_ge(sh["g"], t)
                for k in range(KT):
                    mm = pe.matmul(bank(0).rearrange("p (a n) -> p a n", a=2), h2T[:, k, t * P:(t + 1) * P],
                                   w13[SH][:, :, k, :], start=(k == 0), stop=(k == KT - 1))
                mm.then_inc(sh["h"], 1)

            def turn(t):
                pe.wait_ge(sh["g"], t + 1)
                for f in range(2):
                    tr = pe.transpose(bank(1)[:, f * P:(f + 1) * P], gg[:, f * P:(f + 1) * P], ident[:, :])
                tr.then_inc(sh["T"], 1)

            def down(t):
                pe.wait_ge(sh["te"], t + 1)
                if t >= 1:
                    pe.wait_ge(sh["ye"], t)
                for c in range(2):
                    for f in range(2):
                        mm = pe.matmul(bank(2 + c), gT[:, f, :], w2[SH][:, f, c * 512:(c + 1) * 512],
                                       start=(f == 0), stop=(f == 1))
                mm.then_inc(sh["y"], 1)

            pe.wait_ge(s_shw, 48)
            up(0)
            pe.wait_ge(s_cst, 16)
            pe.wait_ge(s_sel, NT)
            for t in range(NT):
                for a in range(t + 1):
                    mm = pe.matmul(bank(4)[:, t * NE:(t + 1) * NE], tri if a == t else ones, sel[:, a, :],
                                   start=(a == 0), stop=(a == t))
            mm.then_inc(s_pos, 1)
            for t in range(NT):
                mm = pe.matmul(bank(5)[0:NE, 0:1], sel[:, t, :], ones[:, 0:1], start=(t == 0), stop=(t == NT - 1))
            mm.then_inc(s_cnt, 1)
            pe.wait_ge(s_ob, 1)
            pe.matmul(bank(6)[:, 0:NE], oblkb, triX, start=True, stop=True)
            pe.matmul(bank(6)[:, NE:2 * NE], oblkb, triI, start=True, stop=True).then_inc(s_os, 1)
            pe.wait_ge(s_ec, 1)
            pe.matmul(bank(7)[0:1, 0:P], ecol, ident[:, :], start=True, stop=True).then_inc(s_er, 1)
            turn(0)
            for t in range(1, NT):
                up(t)
                down(t - 1)
                turn(t)
            down(NT - 1)

        @block.scalar
        def _(act):
            def silu(t):
                act.wait_ge(sh["h"], t + 1)
                act.activation(hs, bank(0)[:, 0:FE], ACT.Silu).then_inc(sh["si"], 1)

            silu(0)
            for t in range(NT):
                act.wait_ge(sh["T"], t + 1)
                act.activation(gT.rearrange("p f t -> p (f t)"), bank(1)[:, 0:256], ACT.Copy).then_inc(sh["te"], 1)
                if t + 1 < NT:
                    act.wait_ge(sh["g"], t + 1)
                    silu(t + 1)
                act.wait_ge(sh["y"], t + 1)
                act.activation(ysh[:, t, :], bank(2, 2), ACT.Copy).then_inc(sh["ye"], 1)

        @block.gpsimd
        def _(pool):
            pool.wait_ge(s_tin, 16)
            pool.wait_ge(s_k8, 2)
            for n in range(NT * TOPK):
                pool.indirect_dma_start(out=S["slots"], out_offset=bass.IndirectOffsetOnAxis(ap=kidx[:, n:n + 1], axis=0),
                                        in_=recs[:, n, :], in_offset=None,
                                        bounds_check=P * NBLK - 1, oob_is_err=False).then_inc(s_tsc, 16)

        @block.vector
        def _(dve):
            def product(t):
                dve.wait_ge(sh["si"], t + 1)
                if t >= 1:
                    dve.wait_ge(sh["T"], t)
                dve.tensor_tensor(gg, hs, bank(0)[:, FE:2 * FE], ALU.mult).then_inc(sh["g"], 1)

            chain = Chain(dve, s_rv)
            dve.wait_ge(s_rb, 16)
            dve.wait_ge(s_hp, 16 * NT)
            dve.wait_ge(s_cst, 16)
            chain(dve.tensor_tensor(biased, sc, rbias[:, :].unsqueeze(1).to_broadcast([P, NT, NE]), ALU.add))
            for g in range(NT * NG):
                t, o = g // NG, (g % NG) * 8
                ins = dve.max(gm8[:, g, :], biased[:, t, o:o + 8])
            chain(ins)
            chain(dve.tensor_tensor(gs.unsqueeze(2), gm8[:, :, 0:1], gm8[:, :, 1:2], ALU.add))
            g4 = gs.rearrange("p (t g) -> p t g", g=NG)
            for t in range(NT):
                other = g4[:, t, :].unsqueeze(1).to_broadcast([P, NG, NG])
                own = g4[:, t, :].unsqueeze(2).to_broadcast([P, NG, NG])
                a, b = eqb[:, 0:64].rearrange("p (a b) -> p a b", a=8), eqb[:, 64:128].rearrange("p (a b) -> p a b", a=8)
                chain(dve.tensor_tensor(a, other, own, ALU.is_gt))
                chain(dve.tensor_tensor(b, other, own, ALU.is_equal))
                chain(dve.tensor_tensor(b, b, gtri.rearrange("p (a b) -> p a b", a=8), ALU.mult))
                chain(dve.tensor_tensor(a, a, b, ALU.add))
                chain(dve.tensor_reduce(rank[:, t * NG:(t + 1) * NG], a, AX_X, ALU.add))
            chain(dve.tensor_scalar(rank, rank, float(TOPG), None, ALU.is_lt))
            chain(dve.tensor_scalar(gs, rank, BIG, -BIG, ALU.mult, ALU.add))
            bv = biased.rearrange("p t (g e) -> p (t g) e", g=NG)
            mv = msk.rearrange("p t (g e) -> p (t g) e", g=NG)
            chain(dve.tensor_tensor(mv, bv, rank.unsqueeze(2).to_broadcast([P, NT * NG, 8]), ALU.mult))
            chain(dve.tensor_tensor(mv, mv, gs.unsqueeze(2).to_broadcast([P, NT * NG, 8]), ALU.add))
            for t in range(NT):
                chain(dve.max(m8[:, t, :], msk[:, t, :]))
                chain(dve.match_replace(rep[:, t, :], m8[:, t, :], msk[:, t, :], -2 * BIG))
                dve.tensor_scalar(sel[:, t, :], rep[:, t, :], -1.5 * BIG, None, ALU.is_lt).then_inc(s_sel, 1)
            dve.wait_ge(s_sel, NT)
            chain(dve.tensor_tensor(wn, sc, sel, ALU.mult))
            chain(dve.tensor_reduce(wsum, wn, AX_X, ALU.add))
            chain(dve.reciprocal(wsum, wsum))
            chain(dve.tensor_scalar(wsum, wsum, ROUTED_SCALE, None, ALU.mult))
            chain(dve.tensor_tensor(wn, wn, wsum.unsqueeze(2).to_broadcast([P, NT, NE]), ALU.mult))
            product(0)
            dve.wait_ge(s_cnt, 1)
            chain(dve.tensor_copy(cnt, bank(5)[0:NE, 0:1]))
            chain(dve.tensor_scalar(oblk, cnt, float(P), None, ALU.is_gt))
            for a in range(2, NT):
                chain(dve.scalar_tensor_tensor(out=oblk, in0=cnt, scalar=float(P * a), in1=oblk,
                                               op0=ALU.is_gt, op1=ALU.add))
            dve.tensor_scalar(oblkb, ones[0:NE, :], oblk, None, ALU.mult).then_inc(s_ob, 1)
            dve.wait_ge(s_os, 1)
            chain(dve.tensor_copy(rt[:, 2880:3008], bank(6)[:, 0:2 * NE]))
            chain(dve.tensor_scalar(eqb[:, 0:NE], oend, pnum, None, ALU.is_le))
            chain(dve.tensor_reduce(ecol, eqb[:, 0:NE], AX_X, ALU.add))
            dve.tensor_scalar(ecol, ecol, float(NE - 1), None, ALU.min).then_inc(s_ec, 1)
            chain(dve.tensor_scalar(nblk[:, :], oend[0:1, NE - 1:NE], float(NE), None, ALU.add))
            dve.wait_ge(s_er, 1)
            chain(dve.tensor_copy(ove[:, :], bank(7)[0:1, 0:P]))
            dve.wait_ge(s_pos, 1)
            chain(dve.tensor_copy(posv, bank(4)[:, 0:NT * NE].rearrange("p (t e) -> p t e", t=NT)))
            chain(dve.tensor_scalar(jv, posv, float(P), None, ALU.is_ge))
            for a in range(2, NT):
                chain(dve.scalar_tensor_tensor(out=jv, in0=posv, scalar=float(P * a), in1=jv,
                                               op0=ALU.is_ge, op1=ALU.add))
            chain(dve.scalar_tensor_tensor(out=posv, in0=jv, scalar=-float(P), in1=posv, op0=ALU.mult, op1=ALU.add))
            chain(dve.tensor_tensor(ostart, ostart, enum, ALU.subtract))
            chain(dve.tensor_scalar(ostart, ostart, float(NE - 1), None, ALU.add))
            chain(dve.tensor_tensor(gsel, jv, ostart.unsqueeze(1).to_broadcast([P, NT, NE]), ALU.add))
            chain(dve.tensor_scalar(jv, jv, 1.0, None, ALU.is_ge))
            chain(dve.tensor_tensor(gsel, gsel, jv, ALU.mult))
            chain(dve.tensor_tensor(gsel, gsel, enum.unsqueeze(1).to_broadcast([P, NT, NE]), ALU.add))
            chain(dve.scalar_tensor_tensor(out=gsel, in0=posv, scalar=float(NBLK), in1=gsel,
                                           op0=ALU.mult, op1=ALU.add))
            chain(dve.scalar_tensor_tensor(out=gsel, in0=gsel, scalar=1.0, in1=sel, op0=ALU.add, op1=ALU.mult))
            for t in range(NT):
                chain(dve.max(k8[:, t, :], gsel[:, t, :]))
                e3 = eqb.rearrange("p (k e) -> p k e", k=TOPK)
                chain(dve.tensor_tensor(e3, gsel[:, t, :].unsqueeze(1).to_broadcast([P, TOPK, NE]),
                                        k8[:, t, :].unsqueeze(2).to_broadcast([P, TOPK, NE]), ALU.is_equal))
                chain(dve.tensor_tensor(e3, e3, wn[:, t, :].unsqueeze(1).to_broadcast([P, TOPK, NE]), ALU.mult))
                chain(dve.tensor_reduce(w8[:, t, :], e3, AX_X, ALU.add))
            dve.tensor_scalar(kidx[:, :], k8.rearrange("p t k -> p (t k)"), -1.0, None, ALU.add).then_inc(s_k8, 1)
            dve.wait_ge(s_rec, 16)
            dve.tensor_copy(recs[:, :, 2:3].bitcast(F32), w8.rearrange("p t k -> p (t k)").unsqueeze(2))\
               .then_inc(s_k8, 1)
            for t in range(1, NT):
                product(t)

    xg = [mem.at(B0 + 768 + 1024 * b, D) for b in range(2)]
    xT = mem.at(B0 + 2816, KT, P)
    yb = sb("yb", [P, D])
    held = sb("held", [1, 1])
    gi = [sb(f"gi{b}", [P, 1], I32) for b in range(2)]
    si = sb("si", [P, 1], I32)
    names = ("gi", "si", "Tx", "xeV", "xeA", "u", "sl", "g", "Th", "te", "y", "yV", "yA", "z")
    se = {n: sem(f"s_e_{n}") for n in names}
    s_xg = [sem(f"s_xg{b}") for b in range(2)]
    s_sc = sem("s_sc")
    pX, pH, pG, pY = psum[:, 0:1024], bank(2), bank(3), psum[:, 2048:3072]

    def wslot(tab, n, w):
        return tab[:, bass.ds(n, 1), w:w + 1].rearrange("p n w -> p (n w)")

    with nc.Block() as block:
        def run(eng, step, total=None):
            for u in range(RING):
                step(u, 0, u, lambda k, u=u: None if u >= k else False)
            with eng.Fori(1, NE // RING) as i:
                for u in range(RING):
                    step(RING * i + u, i, u, lambda k: None)
            nb = eng.value_load(nblk[0:1, 0:1], min_val=NE, max_val=NBLK)
            with eng.Fori(NE // RING, NBLK // RING + 1) as i:
                for u in range(RING):
                    n = RING * i + u
                    step(n, i, u, lambda k, n=n: n - k < nb)
            return nb

        def due(eng, cond, what):
            if cond is None:
                what()
            elif cond is not False:
                with eng.If(cond):
                    what()

        @block.sync
        def _(sp):
            def step(n, i, u, guard):
                def loads():
                    if isinstance(n, int):
                        if n < SH:
                            return
                        load_w13(sp, n, u)
                        load_w2(sp, n, u)
                        return
                    e = n
                    if past[0]:
                        e = sp.value_load(ove[0:1, bass.ds(n - NE, 1)], min_val=0, max_val=NE - 1)
                    sp.wait_ge(se["u"], n - RING + 1)
                    load_w13(sp, e, u)
                    sp.wait_ge(se["y"], n - RING + 1)
                    load_w2(sp, e, u)
                due(sp, guard(0), loads)

            past = [False]
            for u in range(RING):
                step(u, 0, u, lambda k: None)
            with sp.Fori(1, NE // RING) as i:
                for u in range(RING):
                    step(RING * i + u, i, u, lambda k: None)
            past[0] = True
            nb = sp.value_load(nblk[0:1, 0:1], min_val=NE, max_val=NBLK)
            with sp.Fori(NE // RING, NBLK // RING) as i:
                for u in range(RING):
                    n = RING * i + u
                    step(n, i, u, lambda k, n=n: n < nb)

        @block.gpsimd
        def _(pool):
            pool.memset(xg[0], 0.0).then_inc(se["z"], 1)
            pool.memset(xg[1], 0.0).then_inc(se["z"], 1)
            pool.wait_ge(s_tab, 16)
            pool.wait_ge(s_hp, 16 * NT)
            pool.wait_ge(se["z"], 2)

            def hold(pool):
                pool.tensor_tensor(held[:, :], nhalf[0:1, 0:1], nhalf[0:1, 0:1], ALU.add)

            def step(n, i, u, guard):
                first = isinstance(n, int)

                def gather():
                    if not first or u >= 2:
                        pool.wait_ge(se["Tx"], n - 1)
                    pool.tensor_copy(gi[u % 2][:, :], wslot(tabs, n, 0)).then_inc(se["gi"], 1)
                    pool.wait_ge(se["gi"], n + 1)
                    hold(pool)
                    pool.indirect_dma_start(out=xg[u % 2], out_offset=None, in_=S["h2"],
                                            in_offset=bass.IndirectOffsetOnAxis(ap=gi[u % 2][:, 0:1], axis=0),
                                            bounds_check=TOK - 1, oob_is_err=False).then_inc(s_xg[u % 2], 16)

                def scatter():
                    m = n - 3
                    if not (first and u == 3):
                        pool.wait_ge(s_sc, 16 * m)
                    pool.tensor_copy(si[:, :], wslot(tabs, m, 1)).then_inc(se["si"], 1)
                    pool.wait_ge(se["si"], m + 1)
                    pool.wait_ge(se["yV"], m + 1)
                    pool.wait_ge(se["yA"], m + 1)
                    hold(pool)
                    pool.indirect_dma_start(out=S["rows"], out_offset=bass.IndirectOffsetOnAxis(ap=si[:, 0:1], axis=0),
                                            in_=yb[:, :], in_offset=None,
                                            bounds_check=TOK * TOPK - 1, oob_is_err=False).then_inc(s_sc, 16)

                due(pool, guard(0), gather)
                due(pool, guard(3), scatter)

            nb = run(pool, step)
            pool.wait_ge(s_sc, nb * 16)

        @block.tensor
        def _(pe):
            def step(n, i, u, guard):
                def turn_x():
                    pe.wait_ge(s_xg[u % 2], 32 * i + 16 * (u // 2 + 1))
                    for k in range(KT):
                        tr = pe.transpose(pX[:, k * P:(k + 1) * P], xg[u % 2][:, k * P:(k + 1) * P], ident[:, :])
                    tr.then_inc(se["Tx"], 1)

                def down():
                    v = (u - 2) % RING
                    pe.wait_ge(se["te"], n - 1)
                    pe.wait_ge(s_w2[v], 16 * (i + 1 if u >= 2 else i))
                    if not (isinstance(n, int) and u == 2):
                        pe.wait_ge(se["yV"], n - 2)
                        pe.wait_ge(se["yA"], n - 2)
                    for c in range(2):
                        for f in range(2):
                            mm = pe.matmul(pY[:, c * 512:(c + 1) * 512], gT[:, f, :],
                                           w2[v][:, f, c * 512:(c + 1) * 512], start=(f == 0), stop=(f == 1))
                    mm.then_inc(se["y"], 1)

                def turn_g():
                    pe.wait_ge(se["g"], n)
                    for f in range(2):
                        tr = pe.transpose(pG[:, f * P:(f + 1) * P], gg[:, f * P:(f + 1) * P], ident[:, :])
                    tr.then_inc(se["Th"], 1)

                def up():
                    pe.wait_ge(se["xeV"], n + 1)
                    pe.wait_ge(se["xeA"], n + 1)
                    pe.wait_ge(s_w13[u], 32 * (i + 1))
                    for k in range(KT):
                        mm = pe.matmul(pH.rearrange("p (a n) -> p a n", a=2), xT[:, k, :], w13[u][:, :, k, :],
                                       start=(k == 0), stop=(k == KT - 1))
                    mm.then_inc(se["u"], 1)

                due(pe, guard(0), turn_x)
                due(pe, guard(2), down)
                due(pe, guard(1), turn_g)
                due(pe, guard(0), up)

            run(pe, step)

        @block.scalar
        def _(act):
            def step(n, i, u, guard):
                def take_x():
                    act.wait_ge(se["Tx"], n + 1)
                    act.activation(xT[:, 4:8, :].rearrange("p k t -> p (k t)"), pX[:, 512:1024], ACT.Copy)\
                       .then_inc(se["xeA"], 1)

                def take_y():
                    m = n - 2
                    act.wait_ge(se["y"], m + 1)
                    if not (isinstance(n, int) and u == 2):
                        act.wait_ge(s_sc, 16 * m)
                    act.activation(yb[:, 512:1024], pY[:, 512:1024], ACT.Copy,
                                   scale=wslot(tabs, m, 2).bitcast(F32)).then_inc(se["yA"], 1)

                def silu():
                    act.wait_ge(se["u"], n + 1)
                    if not (isinstance(n, int) and u == 0):
                        act.wait_ge(se["g"], n)
                    act.activation(hs, pH[:, 0:FE], ACT.Silu).then_inc(se["sl"], 1)

                due(act, guard(0), take_x)
                due(act, guard(2), take_y)
                due(act, guard(0), silu)

            run(act, step)

        @block.vector
        def _(dve):
            def step(n, i, u, guard):
                def take_x():
                    dve.wait_ge(se["Tx"], n + 1)
                    dve.tensor_copy(xT[:, 0:4, :].rearrange("p k t -> p (k t)"), pX[:, 0:512]).then_inc(se["xeV"], 1)

                def take_y():
                    m = n - 2
                    dve.wait_ge(se["y"], m + 1)
                    if not (isinstance(n, int) and u == 2):
                        dve.wait_ge(s_sc, 16 * m)
                    dve.tensor_scalar(yb[:, 0:512], pY[:, 0:512], wslot(tabs, m, 2).bitcast(F32), None,
                                      ALU.mult).then_inc(se["yV"], 1)

                def take_g():
                    dve.wait_ge(se["Th"], n)
                    dve.tensor_copy(gT.rearrange("p f t -> p (f t)"), pG[:, 0:256]).then_inc(se["te"], 1)

                def product():
                    dve.wait_ge(se["sl"], n + 1)
                    dve.tensor_tensor(gg, hs, pH[:, FE:2 * FE], ALU.mult).then_inc(se["g"], 1)

                due(dve, guard(0), take_x)
                due(dve, guard(2), take_y)
                due(dve, guard(1), take_g)
                due(dve, guard(0), product)

            run(dve, step)

    yk = [mem.at(M_R + 8192 * b, TOPK, D) for b in range(2)]
    rsm = [mem.at(B0 + 1024 * b, D) for b in range(2)]
    s_yk = [sem(f"s_yk{b}") for b in range(2)]
    names = ("s", "a", "b", "c")
    sc_ = {n: sem(f"s_c_{n}") for n in names}
    s_fin = [sem(f"s_fin{b}") for b in range(2)]
    rows_v = S["rows"].rearrange("(t p k) d -> t p (k d)", p=P, k=TOPK)
    with nc.Block() as block:
        @block.sync
        def _(sp):
            for t in range(NT):
                if t >= 2:
                    sp.wait_ge(sc_["s"], t - 1)
                sp.dma_start(yk[t % 2].rearrange("p k d -> p (k d)"), rows_v[t]).then_inc(s_yk[t % 2], 16)

        @block.scalar
        def _(act):
            for t in range(NT):
                act.wait_ge(sc_["c"], t + 1)
                dst = O["yp"][0] if t == 0 else O["ys"][0, (t - 1) * P:t * P, :]
                act.dma_start(dst, rsm[t % 2]).then_inc(s_fin[t % 2], 16)
            act.wait_ge(s_fin[0], 16 * 3)
            act.wait_ge(s_fin[1], 16 * 2)

        @block.vector
        def _(dve):
            for t in range(NT):
                y = min(t, 1)
                r = rsm[t % 2]
                dve.wait_ge(s_yk[t % 2], 16 * (t // 2 + 1))
                if t >= 2:
                    dve.wait_ge(s_fin[t % 2], 16 * (t // 2))
                dve.tensor_reduce(r, yk[t % 2].rearrange("p k d -> p d k"), AX_X, ALU.add).then_inc(sc_["s"], 1)
                dve.wait_ge(sc_["s"], t + 1)
                dve.tensor_tensor(r, r, ysh[:, t, :], ALU.add).then_inc(sc_["a"], 1)
                dve.wait_ge(sc_["a"], t + 1)
                dve.tensor_tensor(r, r, g2b[:, y, :], ALU.mult).then_inc(sc_["b"], 1)
                dve.wait_ge(sc_["b"], t + 1)
                dve.tensor_tensor(r, r, x1[:, t, :], ALU.add).then_inc(sc_["c"], 1)


def rope_tables(width):
    t = np.arange(LAT)
    axis = width // 2
    inv = THETA ** (-np.arange(0, axis, 2, dtype=np.float32) / axis)
    ang = np.concatenate([(t // GRID_W)[:, None] * inv, (t % GRID_W)[:, None] * inv], -1).astype(np.float32)
    cos, sin = np.cos(ang), np.sin(ang)
    c = np.concatenate([np.ones((SEQ, width)), np.concatenate([cos, cos], -1)], 0)
    s = np.concatenate([np.zeros((SEQ, width)), np.concatenate([-sin, sin], -1)], 0)
    return c.astype(np.float32), s.astype(np.float32)


def constants():
    c = {"ident": np.eye(P, dtype=np.float32)}
    c["cos_a"], c["sin_a"] = rope_tables(HD)
    c["cos_b"], c["sin_b"] = rope_tables(ROPE)
    i = np.arange(P)
    e = np.arange(NE)
    g = np.arange(NG)
    route = np.zeros((P, 513), np.float32)
    route[:, 0:128] = i[:, None] < i[None, :]
    route[:, 128:256] = 1
    route[:, 256:320] = e
    route[:, 320:384] = (g[None, :] < g[:, None]).reshape(1, -1)
    route[:, 384] = i
    route[0:NE, 385:449] = e[:, None] < e[None, :]
    route[0:NE, 449:513] = e[:, None] <= e[None, :]
    c["route_consts"] = route
    rec = np.zeros((P, NT, TOPK, 4), np.int32)
    tok = np.arange(NT)[None, :, None] * P + i[:, None, None]
    rec[..., 0] = tok
    rec[..., 1] = tok * TOPK + np.arange(TOPK)
    c["records"] = rec.reshape(P, NT * TOPK, 4)
    empty = np.zeros((P, NBLK, 4), np.int32)
    empty[..., 0] = TOK
    empty[..., 1] = TOK * TOPK
    c["empty_slots"] = empty
    return c


_INS = ["x_prompt", "x_sample", "c", "cache_gqa_k", "cache_gqa_v", "cache_mla_ckv", "cache_mla_krope", "c_ctx",
        "w_mod", "b_mod", "norm1_g", "norm2_g", "w_in", "gqa_qn", "gqa_kn", "mla_qa_g", "mla_kva_g", "w_qb",
        "w_kvb", "mla_qn_nope", "mla_qn_rope", "mla_kn_nope", "mla_kn_rope", "w_oa", "w_ob", "w_out",
        "w_router", "router_bias", "w_e1", "w_e3", "w_e2", "w_s1", "w_s3", "w_s2"]
_OUTS = [("yp", (1, SEQ, D)), ("ys", (1, LAT, D)), ("gk", (1, 1, KVA, SEQ, HD)), ("gv", (1, 1, KVA, SEQ, HD)),
         ("ckv", (1, 1, SEQ, KVL)), ("kr", (1, 1, SEQ, ROPE))]


def kernel(**inputs):
    import concourse.bacc as bacc
    from concourse.bass_utils import run_bass_kernel_spmd

    nc = bacc.Bacc("TRN2", target_bir_lowering=False, num_devices=1)
    arrays, ins = {}, {}
    for name, a in [(n, inputs[n]) for n in _INS] + list(constants().items()):
        a = np.ascontiguousarray(a)
        arrays[f"in_{name}"] = a
        ins[name] = nc.dram_tensor(f"in_{name}", a.shape, mybir.dt.from_np(a.dtype), kind="ExternalInput").ap()
    outs = {n: nc.dram_tensor(f"out_{n}", s, F32, kind="ExternalOutput").ap() for n, s in _OUTS}
    scratch = {
        "mod_rows": nc.dram_tensor("mod_rows", [64, P], F32, kind="Internal").ap(),
        "h2": nc.dram_tensor("h2", [TOK, D], F32, kind="Internal").ap(),
        "slots": nc.dram_tensor("slots", [P * NBLK, 4], I32, kind="Internal").ap(),
        "rows": nc.dram_tensor("rows", [TOK * TOPK, D], F32, kind="Internal").ap(),
    }
    program(nc, ins, outs, scratch)
    r = run_bass_kernel_spmd(nc, [arrays], core_ids=[0])
    return tuple(r.results[0][f"out_{n}"] for n, _ in _OUTS)
```

```python
from contextlib import ExitStack

import numpy as np

import concourse.bass as bass
from concourse import mybir

F32 = mybir.dt.float32
I32 = mybir.dt.int32
ALU = mybir.AluOpType
ACT = mybir.ActivationFunctionType
AX_X = mybir.AxisListType.X

P = 128
D = 1024
SEQ, LAT, PAST = 128, 512, 128
TOK = SEQ + LAT
NT = TOK // P
KT = D // P
GRID_W = 64
EPS = 1e-6
THETA = 10000.0
N_MOD = 6
HA, KVA, HD = 8, 2, 128
HB, QL, KVL, NOPE, ROPE, VD = 8, 256, 128, 128, 64, 128
KEYS = TOK + PAST
NK = KEYS // P
NE, TOPK, NG, TOPG = 64, 8, 8, 4
FE = 256
ROUTED_SCALE = 2.5
BIG = 1e30
OVF = TOK * TOPK // P
NBLK = NE + OVF
RING = 4
C_QA, C_KA, C_VA = 0, 1024, 1280
C_CQ, C_CKV, C_KR = 1536, 1792, 1920
C_GA, C_GB = 1984, 3008
ZN = C_GA - C_KA
Z_K, Z_V, Z_CQ, Z_CKV, Z_KR = 0, 256, 512, 768, 896


def key_col(t):
    return 0 if t == 0 else P * (t + 1)


class Mem:

    def __init__(self, tensor):
        self.t = tensor

    def at(self, off, *shape, rows=P):
        n = int(np.prod(shape))
        v = self.t[0:rows, off:off + n]
        if len(shape) == 2:
            v = v.rearrange("p (a b) -> p a b", a=shape[0])
        if len(shape) == 3:
            v = v.rearrange("p (a b c) -> p a b c", a=shape[0], b=shape[1])
        return v


def program(nc, I, O, S):
    ctx = ExitStack()
    with ctx:
        build(nc, I, O, S, ctx)


def build(nc, I, O, S, ctx):
    def sb(name, shape, dt=F32):
        return ctx.enter_context(nc.sbuf_tensor(name, shape, dt))

    def sem(name):
        return ctx.enter_context(nc.semaphore(name))

    M_H, M_OA, M_OB, M_R, M_SC, M_TB = 0, 5120, 10240, 15360, 31744, 40320
    M_END = M_TB + 9728
    mem = Mem(sb("mem", [P, M_END]))
    hT = mem.at(M_H, KT, TOK)
    oA = mem.at(M_OA, HA, TOK)
    oB = mem.at(M_OB, HB, TOK)
    ident = sb("ident", [P, P])
    cols = sb("cols", [P, 84])
    modc = sb("modc", [P, 16, 2])
    small = sb("small", [P, 128])
    nhalf = sb("nhalf", [P, 16])
    psum = ctx.enter_context(nc.psum_tensor("psum", [P, 4096], F32))

    def bank(b, n=1):
        return psum[:, b * 512:(b + n) * 512]

    CqA = mem.at(M_TB, NT, HD)
    SqA = mem.at(M_TB + 640, NT, HD)
    CkA = mem.at(M_TB + 1280, NT, HD)
    SkA = mem.at(M_TB + 1920, NT, HD)
    CqB = mem.at(M_TB + 2560, NT, ROPE)
    SqB = mem.at(M_TB + 2880, NT, ROPE)
    CkB = mem.at(M_TB + 3200, NT, ROPE)
    SkB = mem.at(M_TB + 3520, NT, ROPE)
    kTA = mem.at(M_TB + 3840, KVA, KEYS)
    vA = mem.at(M_TB + 5376, NK, KVA, HD)
    krT = mem.at(M_TB + 6912, KEYS, rows=ROPE)
    cqT = mem.at(M_TB + 7680, 2, TOK)
    ckvT = mem.at(M_TB + 8960, KEYS)

    A1, rstd = small[:, 0:16].rearrange("p (k y) -> p k y", y=2), small[:, 16:21]
    ss = small[:, 24:29]
    invlen = small[:, 32:37]
    qk_gain = small[:, 40:41]

    SCALE_A = float(HD) ** -0.5
    SCALE_B = float(NOPE + ROPE) ** -0.5

    s_const = sem("s_const")
    s_rows = sem("s_rows")
    s_x = [sem(f"s_x{t}") for t in range(NT)]
    s_wm = [sem(f"s_wm{b}") for b in range(4)]
    s_wz = sem("s_wz")
    s_silu = sem("s_silu")
    s_rowsT = sem("s_rowsT")
    s_cols = sem("s_cols")
    s_mod1 = sem("s_mod1")
    s_modr = sem("s_modr")
    s_modT = sem("s_modT")
    s_A1 = sem("s_A1")
    s_sqx = sem("s_sqx")
    s_rstd = sem("s_rstd")
    s_xs = sem("s_xs")
    s_xT = sem("s_xT")
    s_xeV, s_xeA = sem("s_xeV"), sem("s_xeA")
    s_v = sem("s_v")
    s_p = sem("s_p")
    s_tabs = sem("s_tabs")
    s_gain = sem("s_gain")

    rows = mem.at(M_SC + 5120, 128, rows=84)
    xt = mem.at(M_SC, NT, D)
    sqd = mem.at(M_SC + 5248, D)
    gA = mem.at(M_R + 6144 + 7680, 4, HD)
    gB = mem.at(M_R + 6144 + 7680 + 512, 4, ROPE)
    wmod = [mem.at(M_OA + 4096 * b, KT, 512) for b in range(4)]
    wz = mem.at(M_R + 6144, KT, ZN)
    w_mod_v = I["w_mod"][0].rearrange("(k p) n -> p k n", p=P)
    w_in_v = I["w_in"][0].rearrange("(k p) n -> p k n", p=P)
    pm = bank(7)[:, 0:32].rearrange("p (c y) -> p c y", y=2)
    modr = mem.at(M_SC + 6272, 4, 512, rows=2)

    class Chain:

        def __init__(self, eng, s, n=0):
            self.eng, self.s, self.n = eng, s, n

        def __call__(self, ins):
            self.n = self.n + 1
            ins.then_inc(self.s, 1)
            self.eng.wait_ge(self.s, self.n)


    with nc.Block() as block:
        @block.sync
        def _(sp):
            sp.dma_start(rows[0:8, :], I["c_ctx"].rearrange("(k p) -> k p", p=P)).then_inc(s_rows, 16)
            sp.dma_start(rows[8:16, :], I["c"].rearrange("a (k p) -> (a k) p", p=P)).then_inc(s_rows, 16)
            sp.dma_start(rows[16:64, :], I["b_mod"].rearrange("a (k p) -> (a k) p", p=P)).then_inc(s_rows, 16)
            sp.dma_start(rows[64:72, :], I["norm1_g"].rearrange("a (k p) -> (a k) p", p=P)).then_inc(s_rows, 16)
            sp.dma_start(rows[72:80, :], I["norm2_g"].rearrange("a (k p) -> (a k) p", p=P)).then_inc(s_rows, 16)
            sp.dma_start(rows[80:82, :], I["mla_qa_g"].rearrange("a (k p) -> (a k) p", p=P)).then_inc(s_rows, 16)
            sp.dma_start(rows[82:83, :], I["mla_qn_nope"]).then_inc(s_rows, 16)
            sp.dma_start(rows[83:84, :], I["mla_kn_nope"]).then_inc(s_rows, 16)
            sp.dma_start(ident[:, :], I["ident"]).then_inc(s_const, 16)
            sp.dma_start(xt[:, 0, :], I["x_prompt"][0]).then_inc(s_x[0], 16)
            for c in range(4):
                sp.dma_start(wmod[c], w_mod_v[:, :, c * 512:(c + 1) * 512]).then_inc(s_wm[c], 16)
                if c == 1:
                    for t in range(1, NT):
                        sp.dma_start(xt[:, t, :], I["x_sample"][0, (t - 1) * P:t * P, :]).then_inc(s_x[t], 16)
            for n, (dst, src, w) in enumerate((
                    (gA[:, 0:2, :], I["gqa_qn"], HD), (gA[:, 2:4, :], I["gqa_kn"], HD),
                    (gB[:, 0:2, :], I["mla_qn_rope"], ROPE), (gB[:, 2:4, :], I["mla_kn_rope"], ROPE))):
                h = w // 2
                sp.dma_start(dst[:, 0, :], src.to_broadcast([P, w])).then_inc(s_gain, 16)
                sp.dma_start(dst[:, 1, 0:h], src[:, h:w].to_broadcast([P, h])).then_inc(s_gain, 16)
                sp.dma_start(dst[:, 1, h:w], src[:, 0:h].to_broadcast([P, h])).then_inc(s_gain, 16)
            for dst, src in ((CqA, I["cos_a"]), (SqA, I["sin_a"]), (CqB, I["cos_b"]), (SqB, I["sin_b"])):
                sp.dma_start(dst, src.rearrange("(t p) w -> p t w", p=P)).then_inc(s_tabs, 16)
            sp.dma_start(wz, w_in_v[:, :, C_KA:C_GA]).then_inc(s_wz, 16)

        @block.gpsimd
        def _(pool):
            pool.memset(nhalf[:, :], -0.5).then_inc(s_p, 1)
            pool.memset(invlen[:, 0:2], 1.0 / HD).then_inc(s_p, 1)
            pool.memset(invlen[:, 2:3], 1.0 / QL).then_inc(s_p, 1)
            pool.memset(invlen[:, 3:4], 1.0 / KVL).then_inc(s_p, 1)
            pool.memset(invlen[:, 4:5], 1.0 / ROPE).then_inc(s_p, 1)
            pool.wait_ge(s_sqx, NT)
            pool.wait_ge(s_p, 5)
            pool.tensor_scalar(ss, ss, 1.0 / D, EPS, ALU.mult, ALU.add).then_inc(s_p, 1)
            pool.wait_ge(s_p, 6)
            pool.tensor_tensor(rstd, ss, nhalf[:, 0:NT], ALU.pow).then_inc(s_rstd, 1)

        @block.scalar
        def _(act):
            act.wait_ge(s_rows, 16 * 8)
            act.activation(rows[0:16, :], rows[0:16, :], ACT.Silu).then_inc(s_silu, 1)
            for t in range(NT):
                act.wait_ge(s_x[t], 16)
                if t:
                    act.wait_ge(s_sqx, t)
                act.activation(sqd, xt[:, t, :], ACT.Square, accum_out=ss[:, t:t + 1]).then_inc(s_sqx, 1)
            for c in range(4):
                act.wait_ge(s_mod1, c + 1)
                act.activation(modr[:, c, :], bank(c)[0:2, :], ACT.Copy).then_inc(s_modr, 1)
            act.wait_ge(s_A1, 3)
            for t in range(NT):
                y = min(t, 1)
                act.wait_ge(s_xT, t + 1)
                for k in range(4, 8):
                    ins = act.activation(hT[:, k, t * P:(t + 1) * P],
                                         bank(2 * (t % 2) + 1)[:, (k - 4) * P:(k - 3) * P], ACT.Identity,
                                         bias=modc[:, k, y:y + 1], scale=A1[:, k, y:y + 1])
                ins.then_inc(s_xeA, 1)

        @block.vector
        def _(dve):
            chain = Chain(dve, s_v)
            dve.wait_ge(s_rowsT, 1)
            chain(dve.tensor_copy(cols[:, :], bank(6)[:, 0:84]))
            dve.sem_inc(s_cols, 1)
            chain(dve.tensor_tensor(qk_gain, cols[:, 82:83], cols[:, 83:84], ALU.mult))
            chain(dve.tensor_scalar(qk_gain, qk_gain, SCALE_B, None, ALU.mult))
            dve.wait_ge(s_rstd, 1)
            for t in range(NT):
                dve.tensor_scalar(xt[:, t, :], xt[:, t, :], rstd[:, t:t + 1], None, ALU.mult).then_inc(s_xs, 1)
            dve.wait_ge(s_gain, 16 * 12)
            dve.wait_ge(s_tabs, 16 * 4)

            def over(g, w):
                return g.unsqueeze(1).to_broadcast([P, NT, w])

            for q, k, raw, g, w, scale in ((CqA, CkA, CqA, gA, HD, SCALE_A), (SqA, SkA, SqA, gA, HD, SCALE_A),
                                           (CqB, CkB, CqB, gB, ROPE, SCALE_B), (SqB, SkB, SqB, gB, ROPE, SCALE_B)):
                swapped = int(raw is SqA or raw is SqB)
                chain(dve.tensor_tensor(k, raw, over(g[:, 2 + swapped, :], w), ALU.mult))
                chain(dve.tensor_tensor(q, raw, over(g[:, swapped, :], w), ALU.mult))
                chain(dve.tensor_scalar(q, q, scale, None, ALU.mult))
            dve.wait_ge(s_modT, 1)
            bias = cols[:, 16:32].unsqueeze(2).to_broadcast([P, 16, 2])
            dve.tensor_tensor(modc[:, 0:16, :], pm[:, 0:16, :], bias, ALU.add).then_inc(s_A1, 1)
            dve.wait_ge(s_A1, 1)
            dve.tensor_scalar(A1, modc[:, 8:16, :], 1.0, None, ALU.add).then_inc(s_A1, 1)
            dve.wait_ge(s_A1, 2)
            gain = cols[:, 64:72].unsqueeze(2).to_broadcast([P, KT, 2])
            dve.tensor_tensor(A1, A1, gain, ALU.mult).then_inc(s_A1, 1)
            dve.wait_ge(s_A1, 3)
            for t in range(NT):
                y = min(t, 1)
                dve.wait_ge(s_xT, t + 1)
                for k in range(4):
                    ins = dve.tensor_scalar(hT[:, k, t * P:(t + 1) * P],
                                            bank(2 * (t % 2))[:, k * P:(k + 1) * P],
                                            A1[:, k, y:y + 1], modc[:, k, y:y + 1], ALU.mult, ALU.add)
                ins.then_inc(s_xeV, 1)

        @block.tensor
        def _(pe):
            pe.wait_ge(s_const, 16)
            pe.wait_ge(s_silu, 1)
            pe.transpose(bank(6)[:, 0:84], rows[0:84, :], ident[0:84, 0:84]).then_inc(s_rowsT, 1)
            pe.wait_ge(s_cols, 1)
            for c in range(4):
                pe.wait_ge(s_wm[c], 16)
                for k in range(KT):
                    mm = pe.matmul(bank(c)[0:2, :], cols[:, k:k + 9:8], wmod[c][:, k, :],
                                   start=(k == 0), stop=(k == KT - 1))
                mm.then_inc(s_mod1, 1)
            for c in range(4):
                pe.wait_ge(s_modr, c + 1)
                for j in range(4):
                    tr = pe.transpose(pm[:, 4 * c + j, :], modr[:, c, j * P:(j + 1) * P], ident[0:2, 0:2])
            tr.then_inc(s_modT, 1)
            for t in range(NT):
                pe.wait_ge(s_xs, t + 1)
                if t >= 2:
                    pe.wait_ge(s_xeV, t - 1)
                    pe.wait_ge(s_xeA, t - 1)
                for k in range(KT):
                    tr = pe.transpose(bank(2 * (t % 2), 2)[:, k * P:(k + 1) * P],
                                      xt[:, t, k * P:(k + 1) * P], ident[:, :])
                tr.then_inc(s_xT, 1)

    zs = [mem.at(M_SC + 960 * b, ZN) for b in range(2)]
    zq = [mem.at(M_SC + 1920 + 960 * b, ZN) for b in range(2)]
    zn = [mem.at(M_SC + 3840 + 960 * b, ZN) for b in range(2)]
    rot = mem.at(M_SC + 5760, 256)
    kgB = mem.at(M_SC + 6016, KVL)
    cache = mem.at(M_SC + 6144, 448)
    wq = mem.at(M_OB, KT, HA * HD)
    s_z = sem("s_z")
    s_zs = sem("s_zs")
    s_zq = sem("s_zq")
    s_zm = sem("s_zm")
    s_zr = sem("s_zr")
    s_zn = sem("s_zn")
    s_zT = sem("s_zT")
    s_zeV, s_zeA = sem("s_zeV"), sem("s_zeA")
    s_cache = sem("s_cache")
    s_out = sem("s_out")
    s_v2 = sem("s_v2")
    s_p2 = sem("s_p2")
    s_wq = sem("s_wq")
    s_vc = sem("s_vc")

    with nc.Block() as block:
        @block.sync
        def _(sp):
            for g in range(KVA):
                sp.dma_start(cache[:, g * HD:(g + 1) * HD], I["cache_gqa_k"][0, 0, g]).then_inc(s_cache, 16)
                sp.dma_start(vA[:, 1, g, :], I["cache_gqa_v"][0, 0, g]).then_inc(s_vc, 16)
            sp.dma_start(cache[:, 256:384], I["cache_mla_ckv"][0, 0]).then_inc(s_cache, 16)
            sp.dma_start(cache[:, 384:448], I["cache_mla_krope"][0, 0]).then_inc(s_cache, 16)
            sp.dma_start(kgB, I["mla_kva_g"].to_broadcast([P, KVL])).then_inc(s_cache, 16)
            sp.dma_start(wq, w_in_v[:, :, C_QA:C_KA]).then_inc(s_wq, 16)
            sp.wait_ge(s_zn, 1)
            for g in range(KVA):
                sp.dma_start(O["gk"][0, 0, g], zn[0][:, Z_K + g * HD:Z_K + (g + 1) * HD]).then_inc(s_out, 16)
                sp.dma_start(O["gv"][0, 0, g], vA[:, 0, g, :]).then_inc(s_out, 16)
            sp.dma_start(O["ckv"][0, 0], zn[0][:, Z_CKV:Z_CKV + KVL]).then_inc(s_out, 16)
            sp.dma_start(O["kr"][0, 0], zn[0][:, Z_KR:Z_KR + ROPE]).then_inc(s_out, 16)
            sp.wait_ge(s_out, 16 * 6)

        @block.tensor
        def _(pe):
            pe.wait_ge(s_wz, 16)

            def project(t):
                b = 2 * (t % 2)
                if t >= 2:
                    pe.wait_ge(s_zs, t - 1)
                for c0, c1, bb in ((0, 512, b), (512, ZN, b + 1)):
                    for k in range(KT):
                        mm = pe.matmul(bank(bb)[:, 0:c1 - c0], hT[:, k, t * P:(t + 1) * P], wz[:, k, c0:c1],
                                       start=(k == 0), stop=(k == KT - 1))
                mm.then_inc(s_z, 1)

            def turn(t):
                if t < NT:
                    pe.wait_ge(s_zn, t + 1)
                    src = [zn[t % 2][:, o:o + w] for o, w in ((0, P), (P, P), (Z_CQ, P), (Z_CQ + P, P),
                                                              (Z_CKV, P), (Z_KR, ROPE))]
                    at = [0, 1, 2, 3, 4, 5]
                else:
                    pe.wait_ge(s_cache, 16 * 5)
                    src = [cache[:, o:o + w] for o, w in ((0, P), (P, P), (256, P), (384, ROPE))]
                    at = [0, 1, 4, 5]
                if t >= 1:
                    pe.wait_ge(s_zeV, t)
                    pe.wait_ge(s_zeA, t)
                for a, s in zip(at, src):
                    w = ROPE if a == 5 else P
                    tr = pe.transpose(bank(4, 2)[0:w, a * P:(a + 1) * P], s, ident[:, :])
                tr.then_inc(s_zT, 1)

            project(0)
            for t in range(1, NT):
                project(t)
                turn(t - 1)
            turn(NT - 1)
            turn(NT)

        @block.scalar
        def _(act):
            def take(t):
                act.wait_ge(s_z, t + 1)
                if t >= 2:
                    act.wait_ge(s_zn, t - 1)
                act.activation(zs[t % 2], psum[:, 1024 * (t % 2):1024 * (t % 2) + ZN], ACT.Copy).then_inc(s_zs, 1)
                act.wait_ge(s_zs, t + 1)
                act.activation(vA[:, key_col(t) // P, :, :].rearrange("p g d -> p (g d)"),
                               zs[t % 2][:, Z_V:Z_V + 256], ACT.Copy)
                act.activation(zq[t % 2], zs[t % 2], ACT.Square).then_inc(s_zq, 1)

            def untangle(t):
                act.wait_ge(s_zT, t + 1)
                c = key_col(t) if t < NT else P
                act.activation(ckvT[:, c:c + P], bank(5)[:, 0:P], ACT.Copy)
                act.activation(krT[:, c:c + P], bank(5)[0:ROPE, P:2 * P], ACT.Copy).then_inc(s_zeA, 1)

            take(0)
            take(1)
            for t in range(NT):
                untangle(t)
                if t + 2 < NT:
                    take(t + 2)
            untangle(NT)

        @block.gpsimd
        def _(pool):
            for t in range(NT):
                pool.wait_ge(s_zm, t + 1)
                pool.tensor_scalar(ss, ss, EPS, None, ALU.add).then_inc(s_p2, 1)
                pool.wait_ge(s_p2, t + 1)
                pool.tensor_tensor(rstd, ss, nhalf[:, 0:5], ALU.pow).then_inc(s_zr, 1)

        @block.vector
        def _(dve):
            chain = Chain(dve, s_v2)
            dve.wait_ge(s_cache, 16 * 5)

            def norms(t):
                z, q, n = zs[t % 2], zq[t % 2], zn[t % 2]
                dve.wait_ge(s_zq, t + 1)
                if t >= 1:
                    dve.wait_ge(s_zr, t)
                for a, b, c, w in ((0, 2, Z_K, HD), (2, 3, Z_CQ, QL), (3, 4, Z_CKV, KVL), (4, 5, Z_KR, ROPE)):
                    chain(dve.tensor_reduce(ss[:, a:b], q[:, c:c + (b - a) * w].rearrange("p (a w) -> p a w", w=w),
                                            AX_X, ALU.add))
                dve.tensor_tensor(ss, ss, invlen, ALU.mult).then_inc(s_zm, 1)
                dve.wait_ge(s_zr, t + 1)
                if t >= 2:
                    dve.wait_ge(s_zT, t - 1)
                if t == 2:
                    dve.wait_ge(s_out, 16 * 6)
                k3 = n[:, 0:256].rearrange("p (g d) -> p g d", g=KVA)
                z3 = z[:, 0:256].rearrange("p (g d) -> p g d", g=KVA)
                q3 = q[:, 0:256].rearrange("p (g d) -> p g d", g=KVA)
                r3 = rot.rearrange("p (g d) -> p g d", g=KVA)
                chain(dve.tensor_tensor(q3, z3, rstd[:, 0:2].unsqueeze(2).to_broadcast([P, KVA, HD]), ALU.mult))
                h = HD // 2
                for a, b in ((0, h), (h, 0)):
                    chain(dve.tensor_tensor(r3[:, :, a:a + h], q3[:, :, b:b + h],
                                            SkA[:, t, a:a + h].unsqueeze(1).to_broadcast([P, KVA, h]), ALU.mult))
                chain(dve.tensor_tensor(k3, q3, CkA[:, t, :].unsqueeze(1).to_broadcast([P, KVA, HD]), ALU.mult))
                chain(dve.tensor_tensor(k3, k3, r3, ALU.add))
                chain(dve.tensor_scalar(n[:, Z_CQ:Z_CQ + QL], z[:, Z_CQ:Z_CQ + QL], rstd[:, 2:3], None, ALU.mult))
                chain(dve.scalar_tensor_tensor(out=n[:, Z_CKV:Z_CKV + KVL], in0=z[:, Z_CKV:Z_CKV + KVL],
                                               scalar=rstd[:, 3:4], in1=kgB, op0=ALU.mult, op1=ALU.mult))
                zr, nr, qr = z[:, Z_KR:], n[:, Z_KR:], q[:, Z_KR:]
                h = ROPE // 2
                for a, b in ((0, h), (h, 0)):
                    chain(dve.scalar_tensor_tensor(out=qr[:, a:a + h], in0=zr[:, b:b + h], scalar=rstd[:, 4:5],
                                                   in1=SkB[:, t, a:a + h], op0=ALU.mult, op1=ALU.mult))
                chain(dve.scalar_tensor_tensor(out=nr[:, 0:ROPE], in0=zr[:, 0:ROPE], scalar=rstd[:, 4:5],
                                               in1=CkB[:, t, :], op0=ALU.mult, op1=ALU.mult))
                dve.tensor_tensor(nr[:, 0:ROPE], nr[:, 0:ROPE], qr[:, 0:ROPE], ALU.add).then_inc(s_zn, 1)

            def untangle(t):
                dve.wait_ge(s_zT, t + 1)
                c = key_col(t) if t < NT else P
                ins = dve.tensor_copy(kTA[:, :, c:c + P], bank(4)[:, 0:256].rearrange("p (g d) -> p g d", g=KVA))
                if t < NT:
                    for j in range(2):
                        ins = dve.tensor_scalar(cqT[:, j, t * P:(t + 1) * P], bank(4)[:, (2 + j) * P:(3 + j) * P],
                                                cols[:, 80 + j:81 + j], None, ALU.mult)
                ins.then_inc(s_zeV, 1)

            norms(0)
            norms(1)
            for t in range(NT):
                untangle(t)
                if t + 2 < NT:
                    norms(t + 2)
            untangle(NT)

    hz = mem.at(M_SC, 960)
    hq = mem.at(M_SC + 960, 960)
    hr = mem.at(M_SC + 1920, 640)
    qTh = mem.at(M_SC + 2560, TOK)
    qrT = mem.at(M_SC + 3200, TOK, rows=ROPE)
    pr = [mem.at(M_SC + 3840 + 640 * b, 640) for b in range(2)]
    pT = mem.at(M_SC + 5120, 5, LAT)
    pTc = mem.at(M_SC + 7680, P)
    vh = mem.at(M_SC + 7808, NK, VD)
    nmax = small[:, 48:53]
    rsum = small[:, 56:61]
    rinv = small[:, 64:69]
    hss = small[:, 72:82]
    hrs = small[:, 88:98]
    pZ, pS, pT_ps, pO, pC = psum[:, 0:1024], psum[:, 1024:2048], psum[:, 2048:3072], bank(6), bank(7)[:, 0:P]
    MODS = 4
    wmh = mem.at(M_OB + KT * HA * HD, KT, 512)
    modrow = mem.at(M_R + 11264, MODS * D, rows=2)
    gainrow = mem.at(M_R + 11264 + MODS * D, D, rows=2)
    pM = bank(7)[0:2, :]
    PROJECT = ((0, 1), (2, 3), (4,), (), ())
    s_mrow = sem("s_mrow")
    KEY_TILES = [2, 3, 4, 5, 1]

    def attend(kind, wqh, oT, kT_of, v_of, s_w):
        mla = kind == "b"
        names = ("S", "nm", "exp", "ri", "pn", "T", "TeV", "TeA", "Z", "sq", "ss", "ms", "rs", "qn", "rot", "q",
                 "QT", "qe", "O", "Oe", "C", "Ce", "vh", "qr") + (() if mla else ("wm", "br", "M", "Me", "mr"))
        s = {n: nc.alloc_semaphore(name=f"s_{kind}_{n}") for n in names}
        nh = HA
        W = (NOPE + ROPE) if mla else HD
        NS = 2 if mla else 1

        with nc.Block() as block:
            if not mla:
                @block.sync
                def _(sp):
                    sp.dma_start(modrow, I["b_mod"][:, 2 * D:6 * D].to_broadcast([2, MODS * D])).then_inc(s["br"], 16)
                    sp.dma_start(gainrow, I["norm2_g"].to_broadcast([2, D])).then_inc(s["br"], 16)
                    sp.dma_start(wmh, w_mod_v[:, :, 2 * D:2 * D + 512]).then_inc(s["wm"], 16)
                    with sp.Fori(1, nh) as h:
                        sp.wait_ge(s["M"], h)
                        sp.dma_start(wmh, w_mod_v[:, :, bass.ds(h * 512 + 2 * D, 512)]).then_inc(s["wm"], 16)
                    sp.wait_ge(s["mr"], 1)
                    sp.dma_start(S["mod_rows"].rearrange("(v y) d -> y v d", y=2),
                                 modrow.rearrange("y (v d) -> y v d", v=MODS)).then_inc(s_mrow, 16)
                    sp.wait_ge(s_mrow, 16)

            @block.tensor
            def _(pe):
                pe.wait_ge(s_w, 16)

                def project(h, t):
                    if mla:
                        for k in range(2):
                            pe.matmul(pZ[:, t * P:(t + 1) * P], cqT[:, k, t * P:(t + 1) * P],
                                      wqh[:, k, bass.ds(h * W, NOPE)], start=(k == 0), stop=(k == 1))
                        for k in range(2):
                            mm = pe.matmul(pZ[:, 640 + t * ROPE:640 + (t + 1) * ROPE], cqT[:, k, t * P:(t + 1) * P],
                                           wqh[:, k, bass.ds(h * W + NOPE, ROPE)], start=(k == 0), stop=(k == 1))
                    else:
                        for k in range(KT):
                            mm = pe.matmul(pZ[:, t * P:(t + 1) * P], hT[:, k, t * P:(t + 1) * P],
                                           wqh[:, k, bass.ds(h * W, W)], start=(k == 0), stop=(k == KT - 1))
                    if t == NT - 1:
                        mm.then_inc(s["Z"], 1)

                def turn_q(h):
                    pe.wait_ge(s["q"], h + 1)
                    for t in range(NT):
                        tr = pe.transpose(pZ[:, t * P:(t + 1) * P], hq[:, t * P:(t + 1) * P], ident[:, :])
                    tr.then_inc(s["QT"], 1)

                def turn_r(h):
                    pe.wait_ge(s["qe"], 2 * h + 1)
                    pe.matmul(pZ[0:ROPE, 0:P], hq[:, 640:640 + ROPE], ident[:, :], start=True, stop=True)
                    for t in range(1, NT):
                        tr = pe.transpose(pZ[0:ROPE, t * P:(t + 1) * P],
                                          hq[:, 640 + t * ROPE:640 + (t + 1) * ROPE], ident[:, :])
                    tr.then_inc(s["qr"], 1)

                def scores(h, t):
                    if t == 0:
                        pe.wait_ge(s["qe"], NS * h + NS)
                    else:
                        pe.wait_ge(s["exp"], NT * h + t)
                    kT = kT_of(h)
                    q = qTh[:, t * P:(t + 1) * P]
                    r = qrT[:, t * P:(t + 1) * P]
                    parts = [(0, 0, P)] if t == 0 else [(0, 2 * P, LAT), (LAT, P, P)]
                    for o, c, w in parts:
                        mm = pe.matmul(pS[:, o:o + w], q, kT(c, w), start=True, stop=not mla)
                        if mla:
                            mm = pe.matmul(pS[:, o:o + w], r, krT[:, c:c + w], start=False, stop=True)
                    mm.then_inc(s["S"], 1)

                def turn_p(h, t):
                    pe.wait_ge(s["pn"], NT * h + t + 1)
                    if t >= 1:
                        pe.wait_ge(s["TeV"], NT * h + t)
                        if t >= 2:
                            pe.wait_ge(s["TeA"], (NT - 1) * h + t - 1)
                    for j in range(1 if t == 0 else 5):
                        tr = pe.transpose(pT_ps[:, j * P:(j + 1) * P], pr[t % 2][:, j * P:(j + 1) * P], ident[:, :])
                    tr.then_inc(s["T"], 1)

                def values(h, t):
                    pe.wait_ge(s["TeV"], NT * h + t + 1)
                    if t == 0:
                        pe.wait_ge(s["vh"], h + 1)
                        if not mla:
                            pe.wait_ge(s["Me"], h + 1)
                        pe.matmul(pC, vh[:, 0, :], pTc, start=True, stop=True).then_inc(s["C"], 1)
                        return
                    pe.wait_ge(s["TeA"], (NT - 1) * h + t)
                    if t == 1:
                        pe.wait_ge(s["Oe"], h + 1)
                    for j, kt in enumerate(KEY_TILES):
                        mm = pe.matmul(pO[:, (t - 1) * P:t * P], vh[:, kt, :], pT[:, j, (t - 1) * P:t * P],
                                       start=(j == 0), stop=(j == 4))
                    if t == NT - 1:
                        mm.then_inc(s["O"], 1)

                def modulation(h, part):
                    if part == 0:
                        pe.wait_ge(s["wm"], 16 * (h + 1))
                        pe.wait_ge(s["Ce"], h + 1)
                    for k in range(4 * part, 4 * part + 4):
                        mm = pe.matmul(pM, cols[:, k:k + 9:8], wmh[:, k, :], start=(k == 0), stop=(k == KT - 1))
                    if part == 1:
                        mm.then_inc(s["M"], 1)

                def head(h, more):
                    for t in range(NT):
                        scores(h, t)
                        if more:
                            for p in PROJECT[t]:
                                project(h + 1, p)
                        if t >= 1:
                            turn_p(h, t - 1)
                        if t >= 2:
                            values(h, t - 2)
                        if t >= 3 and not mla:
                            modulation(h, t - 3)
                    if more:
                        turn_q(h + 1)
                    turn_p(h, NT - 1)
                    values(h, NT - 2)
                    if more and mla:
                        turn_r(h + 1)
                    values(h, NT - 1)

                for t in range(NT):
                    project(0, t)
                turn_q(0)
                if mla:
                    turn_r(0)
                with pe.Fori(0, nh - 1) as h:
                    head(h, True)
                head(nh - 1, False)

            @block.scalar
            def _(act):
                def squares(h):
                    act.wait_ge(s["Z"], h + 1)
                    n = 960 if mla else 640
                    act.activation(hz[:, 0:n], pZ[:, 0:n], ACT.Square).then_inc(s["sq"], 1)

                def take_q(h):
                    act.wait_ge(s["QT"], h + 1)
                    if mla:
                        act.activation(qTh, pZ[:, 0:TOK], ACT.Copy, scale=qk_gain).then_inc(s["qe"], 1)
                    else:
                        act.activation(qTh, pZ[:, 0:TOK], ACT.Copy).then_inc(s["qe"], 1)

                def take_r(h):
                    act.wait_ge(s["qr"], h + 1)
                    act.activation(qrT, pZ[0:ROPE, 0:TOK], ACT.Copy).then_inc(s["qe"], 1)

                def take_p(h, t):
                    act.wait_ge(s["T"], NT * h + t + 1)
                    act.activation(pT[:, 4, (t - 1) * P:t * P], pT_ps[:, 512:640], ACT.Copy).then_inc(s["TeA"], 1)

                def head(h, more):
                    for t in range(NT):
                        w = P if t == 0 else 640
                        act.wait_ge(s["nm"], NT * h + t + 1)
                        if t >= 2:
                            act.wait_ge(s["T"], NT * h + t - 1)
                        act.activation(pr[t % 2][:, 0:w], pS[:, 0:w], ACT.Exp, bias=nmax[:, t:t + 1],
                                       accum_out=rsum[:, t:t + 1]).then_inc(s["exp"], 1)
                        if t >= 2:
                            take_p(h, t - 1)
                        if t == 2 and more:
                            squares(h + 1)
                        if t == 3:
                            act.wait_ge(s["C"], h + 1)
                            act.activation(oT[:, bass.ds(h, 1), 0:P].rearrange("p a t -> p (a t)"), pC, ACT.Copy)\
                               .then_inc(s["Ce"], 1)
                    if more:
                        take_q(h + 1)
                    take_p(h, NT - 1)
                    if more and mla:
                        take_r(h + 1)
                    act.wait_ge(s["O"], h + 1)
                    act.activation(oT[:, bass.ds(h, 1), P:TOK].rearrange("p a t -> p (a t)"), pO,
                                   ACT.Copy).then_inc(s["Oe"], 1)

                act.sem_inc(s["Oe"], 1)
                squares(0)
                take_q(0)
                if mla:
                    take_r(0)
                with act.Fori(0, nh - 1) as h:
                    head(h, True)
                head(nh - 1, False)

            @block.gpsimd
            def _(pool):
                ns = NT * NS

                def prep(h):
                    pool.wait_ge(s["ms"], h + 1)
                    pool.tensor_tensor(hrs[:, 0:ns], hss[:, 0:ns], nhalf[:, 0:ns], ALU.pow).then_inc(s["rs"], 1)

                def copy_v(h):
                    pool.tensor_copy(vh, v_of(h)).then_inc(s["vh"], 1)

                prep(0)
                copy_v(0)
                with pool.Fori(0, nh - 1) as h:
                    prep(h + 1)
                    pool.wait_ge(s["O"], h + 1)
                    copy_v(h + 1)

            @block.vector
            def _(dve):
                w = ROPE if mla else HD
                o = 640 if mla else 0
                z3 = pZ[:, o:o + NT * w].rearrange("p (t d) -> p t d", t=NT)
                n3 = hz[:, o:o + NT * w].rearrange("p (t d) -> p t d", t=NT)
                q3 = hq[:, o:o + NT * w].rearrange("p (t d) -> p t d", t=NT)
                r3 = hr[:, 0:NT * w].rearrange("p (t d) -> p t d", t=NT)
                C, Sn = (CqB, SqB) if mla else (CqA, SqA)

                def sums(h):
                    dve.wait_ge(s["sq"], h + 1)
                    a = hz[:, 0:640].rearrange("p (t d) -> p t d", t=NT)
                    ins = dve.tensor_reduce(hss[:, 0:NT], a, AX_X, ALU.add)
                    if mla:
                        b = hz[:, 640:960].rearrange("p (t d) -> p t d", t=NT)
                        ins.then_inc(s["ss"], 1)
                        dve.tensor_reduce(hss[:, NT:2 * NT], b, AX_X, ALU.add).then_inc(s["ss"], 1)
                        dve.wait_ge(s["ss"], 3 * h + 2)
                        dve.tensor_scalar(hss[:, 0:NT], hss[:, 0:NT], 1.0 / HD, EPS, ALU.mult, ALU.add)\
                           .then_inc(s["ss"], 1)
                        dve.tensor_scalar(hss[:, NT:2 * NT], hss[:, NT:2 * NT], 1.0 / ROPE, EPS, ALU.mult, ALU.add)\
                           .then_inc(s["ms"], 1)
                    else:
                        ins.then_inc(s["ss"], 1)
                        dve.wait_ge(s["ss"], h + 1)
                        dve.tensor_scalar(hss[:, 0:NT], hss[:, 0:NT], 1.0 / HD, EPS, ALU.mult, ALU.add)\
                           .then_inc(s["ms"], 1)

                def scale(h):
                    dve.wait_ge(s["rs"], h + 1)
                    rs = hrs[:, NT * (NS - 1):NT * NS].unsqueeze(2).to_broadcast([P, NT, w])
                    dve.tensor_tensor(n3, z3, rs, ALU.mult).then_inc(s["qn"], 1)
                    if mla:
                        dve.tensor_tensor(hq[:, 0:640].rearrange("p (t d) -> p t d", t=NT),
                                          pZ[:, 0:640].rearrange("p (t d) -> p t d", t=NT),
                                          hrs[:, 0:NT].unsqueeze(2).to_broadcast([P, NT, NOPE]), ALU.mult)

                def rotate(h):
                    dve.wait_ge(s["qn"], h + 1)
                    x = w // 2
                    dve.tensor_tensor(r3[:, :, 0:x], n3[:, :, x:w], Sn[:, :, 0:x], ALU.mult).then_inc(s["rot"], 1)
                    dve.tensor_tensor(r3[:, :, x:w], n3[:, :, 0:x], Sn[:, :, x:w], ALU.mult).then_inc(s["rot"], 1)
                    dve.tensor_tensor(q3, n3, C, ALU.mult).then_inc(s["rot"], 1)
                    dve.wait_ge(s["rot"], 3 * h + 3)
                    dve.tensor_tensor(q3, q3, r3, ALU.add).then_inc(s["q"], 1)

                def maximum(h, t):
                    w = P if t == 0 else 640
                    dve.wait_ge(s["S"], NT * h + t + 1)
                    dve.tensor_reduce(nmax[:, t:t + 1], pS[:, 0:w], AX_X, ALU.max, negate=True).then_inc(s["nm"], 1)

                def normalise(h, t):
                    w = P if t == 0 else 640
                    dve.wait_ge(s["exp"], NT * h + t + 1)
                    dve.reciprocal(rinv[:, t:t + 1], rsum[:, t:t + 1]).then_inc(s["ri"], 1)
                    dve.wait_ge(s["ri"], NT * h + t + 1)
                    dve.tensor_scalar(pr[t % 2][:, 0:w], pr[t % 2][:, 0:w], rinv[:, t:t + 1], None, ALU.mult)\
                       .then_inc(s["pn"], 1)

                def take_p(h, t):
                    dve.wait_ge(s["T"], NT * h + t + 1)
                    if t == 0:
                        dve.tensor_copy(pTc, pT_ps[:, 0:P]).then_inc(s["TeV"], 1)
                    else:
                        dve.tensor_copy(pT[:, 0:4, (t - 1) * P:t * P],
                                        pT_ps[:, 0:512].rearrange("p (j q) -> p j q", j=4)).then_inc(s["TeV"], 1)

                def take_mod(h):
                    dve.wait_ge(s["M"], h + 1)
                    row = modrow[:, bass.ds(h * 512, 512)]
                    dve.tensor_tensor(row, row, pM, ALU.add).then_inc(s["Me"], 1)

                def head(h, more):
                    for t in range(NT):
                        maximum(h, t)
                        if t == 3 and more:
                            sums(h + 1)
                        if t >= 1:
                            take_p(h, t - 1)
                        if t == 4 and more:
                            rotate(h + 1)
                        normalise(h, t)
                        if t == 3 and more:
                            scale(h + 1)
                    take_p(h, NT - 1)
                    if not mla:
                        take_mod(h)

                sums(0)
                scale(0)
                rotate(0)
                if not mla:
                    dve.sem_inc(s["Me"], 1)
                    dve.wait_ge(s["br"], 32)
                with dve.Fori(0, nh - 1) as h:
                    head(h, True)
                head(nh - 1, False)
                if not mla:
                    dve.wait_ge(s["Me"], nh + 1)
                    row = modrow[:, 2 * D:3 * D]
                    dve.scalar_tensor_tensor(out=row, in0=row, scalar=1.0, in1=gainrow, op0=ALU.add, op1=ALU.mult)\
                       .then_inc(s["mr"], 1)

        nc.clear_and_free_semaphores(list(s.values()))
        nc.all_engine_barrier()

    def kT_gqa(h):
        return lambda c, w: kTA[:, h // (HA // KVA), c:c + w] if isinstance(h, int) else \
            kTA[:, bass.ds(h // (HA // KVA), 1), c:c + w].rearrange("p a k -> p (a k)")

    def v_gqa(h):
        if isinstance(h, int):
            return vA[:, :, h // (HA // KVA), :]
        return vA[:, :, bass.ds(h // (HA // KVA), 1), :].rearrange("p k a d -> p k (a d)")

    attend("a", wq, oA, kT_gqa, v_gqa, s_wq)

    kB = mem.at(M_R, HB, KEYS)
    vB = mem.at(M_R + 6144, NK, HB, VD)
    wqb = mem.at(M_R + 12288, 2, HB * (NOPE + ROPE))
    wkvb = mem.at(M_SC, HB * (NOPE + VD))
    kz = [mem.at(M_SC + 2048 + KEYS * b, KEYS) for b in range(2)]
    kn = [mem.at(M_SC + 2048 + KEYS * (2 + b), KEYS) for b in range(2)]
    kss = [small[:, 100 + 6 * b:106 + 6 * b] for b in range(2)]
    krs = [small[:, 112 + 6 * b:118 + 6 * b] for b in range(2)]
    s_wqb = sem("s_wqb")
    s_wkvb = sem("s_wkvb")
    names = ("kv", "sq", "ss", "ms", "rs", "kn", "v", "T", "e")
    sk = {n: sem(f"s_k_{n}") for n in names}
    KV = NOPE + VD
    pKV = [psum[:, 1536 * b:1536 * (b + 1)].rearrange("p (k c) -> p k c", c=KV) for b in range(2)]
    pKT = psum[:, 3072:3072 + KEYS]
    with nc.Block() as block:
        @block.sync
        def _(sp):
            sp.dma_start(wkvb, I["w_kvb"][0]).then_inc(s_wkvb, 16)
            sp.dma_start(wqb, I["w_qb"][0].rearrange("(k p) n -> p k n", p=P)).then_inc(s_wqb, 16)

        @block.tensor
        def _(pe):
            pe.wait_ge(s_wkvb, 16)

            def expand(h, b, first=False):
                if not first:
                    pe.wait_ge(sk["v"], h)
                for kt in range(NK):
                    mm = pe.matmul(pKV[b][:, kt, :], ckvT[:, kt * P:(kt + 1) * P], wkvb[:, bass.ds(h * KV, KV)],
                                   start=True, stop=True)
                mm.then_inc(sk["kv"], 1)

            def turn(h, b):
                pe.wait_ge(sk["kn"], h + 1)
                pe.wait_ge(sk["e"], h + 1)
                for kt in range(NK):
                    tr = pe.transpose(pKT[:, kt * P:(kt + 1) * P], kn[b][:, kt * P:(kt + 1) * P], ident[:, :])
                tr.then_inc(sk["T"], 1)

            expand(0, 0, True)
            with pe.Fori(0, HB // 2 - 1) as i:
                for b in range(2):
                    expand(2 * i + b + 1, 1 - b)
                    turn(2 * i + b, b)
            expand(HB - 1, 1)
            turn(HB - 2, 0)
            turn(HB - 1, 1)

        @block.scalar
        def _(act):
            def squares(h, b):
                act.wait_ge(sk["kv"], h + 1)
                act.activation(kz[b].rearrange("p (k d) -> p k d", k=NK), pKV[b][:, :, 0:NOPE], ACT.Square)\
                   .then_inc(sk["sq"], 1)

            def take_v(h, b):
                act.wait_ge(sk["kn"], h + 1)
                act.activation(vB[:, :, bass.ds(h, 1), :].rearrange("p k a d -> p k (a d)"), pKV[b][:, :, NOPE:KV],
                               ACT.Copy).then_inc(sk["v"], 1)

            act.sem_inc(sk["v"], 1)
            squares(0, 0)
            with act.Fori(0, HB // 2 - 1) as i:
                for b in range(2):
                    squares(2 * i + b + 1, 1 - b)
                    take_v(2 * i + b, b)
            squares(HB - 1, 1)
            take_v(HB - 2, 0)
            take_v(HB - 1, 1)

        @block.gpsimd
        def _(pool):
            with pool.Fori(0, HB // 2) as i:
                for b in range(2):
                    pool.wait_ge(sk["ms"], 2 * i + b + 1)
                    pool.tensor_tensor(krs[b], kss[b], nhalf[:, 0:NK], ALU.pow).then_inc(sk["rs"], 1)

        @block.vector
        def _(dve):
            def sums(h, b):
                dve.wait_ge(sk["sq"], h + 1)
                dve.tensor_reduce(kss[b], kz[b].rearrange("p (k d) -> p k d", k=NK), AX_X, ALU.add)\
                   .then_inc(sk["ss"], 1)
                dve.wait_ge(sk["ss"], h + 1)
                dve.tensor_scalar(kss[b], kss[b], 1.0 / NOPE, EPS, ALU.mult, ALU.add).then_inc(sk["ms"], 1)

            def norm(h, b):
                dve.wait_ge(sk["rs"], h + 1)
                dve.tensor_tensor(kn[b].rearrange("p (k d) -> p k d", k=NK), pKV[b][:, :, 0:NOPE],
                                  krs[b].unsqueeze(2).to_broadcast([P, NK, NOPE]), ALU.mult).then_inc(sk["kn"], 1)

            def take(h):
                dve.wait_ge(sk["T"], h + 1)
                dve.tensor_copy(kB[:, bass.ds(h, 1), :].rearrange("p a k -> p (a k)"), pKT).then_inc(sk["e"], 1)

            dve.sem_inc(sk["e"], 1)
            sums(0, 0)
            sums(1, 1)
            norm(0, 0)
            with dve.Fori(0, HB // 2 - 1) as i:
                for b in (1, 0):
                    h = 2 * i + 2 - b
                    sums(h + 1, 1 - b)
                    norm(h, b)
                    take(h - 1)
            norm(HB - 1, 1)
            take(HB - 2)
            take(HB - 1)

    attend("b", wqb, oB,
           lambda h: (lambda c, w: kB[:, bass.ds(h, 1), c:c + w].rearrange("p a k -> p (a k)")),
           lambda h: vB[:, :, bass.ds(h, 1), :].rearrange("p k a d -> p k (a d)"), s_wqb)

    wm = [[mem.at(M_R + 4096 * b + 1024 * q, KT, P) for q in range(4)] for b in range(2)]
    mT = mem.at(M_R + 8192, KT, TOK)
    wout = mem.at(M_SC, KT, D)
    HALF = TOK // 2
    sig = [mem.at(M_TB + 640 * b, 2, HALF) for b in range(2)]
    mx = [mem.at(M_TB + 1280 + 640 * b, 2, HALF) for b in range(2)]
    s_mw = [sem(f"s_mw{b}") for b in range(2)]
    s_wout = sem("s_wout")
    names = ("mm", "sig", "x", "m")
    sg = {n: [sem(f"s_g_{n}{f}") for f in range(2)] for n in names}
    with nc.Block() as block:
        @block.sync
        def _(sp):
            w_oa_v = I["w_oa"][0].rearrange("(k p) n -> p k n", p=P)
            w_ob_v = I["w_ob"][0].rearrange("(k p) n -> p k n", p=P)

            def load(j, b):
                for q, (w, c) in enumerate(((w_in_v, C_GA), (w_oa_v, 0), (w_in_v, C_GB), (w_ob_v, 0))):
                    sp.dma_start(wm[b][q], w[:, :, bass.ds(j * P + c, P)]).then_inc(s_mw[b], 16)

            load(0, 0)
            load(1, 1)
            sp.dma_start(wout, I["w_out"][0].rearrange("(k p) n -> p k n", p=P)).then_inc(s_wout, 16)
            with sp.Fori(1, KT // 2) as i:
                for b in range(2):
                    sp.wait_ge(sg["mm"][1], 2 * i - 1 + b)
                    load(2 * i + b, b)

        @block.tensor
        def _(pe):
            def chunk(i, b, first):
                pe.wait_ge(s_mw[b], 64 * (i + 1))
                for f in range(2):
                    if not first:
                        pe.wait_ge(sg["m"][f], 2 * i + b)
                    for q, src in enumerate((hT, oA, hT, oB)):
                        for k in range(KT):
                            mm = pe.matmul(bank(4 * f + q)[:, 0:HALF], wm[b][q][:, k, :],
                                           src[:, k, f * HALF:(f + 1) * HALF], start=(k == 0), stop=(k == KT - 1))
                    mm.then_inc(sg["mm"][f], 1)

            chunk(0, 0, True)
            chunk(0, 1, False)
            with pe.Fori(1, KT // 2) as i:
                for b in range(2):
                    chunk(i, b, False)

        @block.scalar
        def _(act):
            def gates(j, f, first):
                act.wait_ge(sg["mm"][f], j + 1)
                if not first:
                    act.wait_ge(sg["m"][f], j)
                for g in range(2):
                    ins = act.activation(sig[f][:, g, :], bank(4 * f + 2 * g)[:, 0:HALF], ACT.Sigmoid)
                ins.then_inc(sg["sig"][f], 1)

            for f in range(2):
                gates(0, f, True)
            with act.Fori(1, KT) as j:
                for f in range(2):
                    gates(j, f, False)

        @block.vector
        def _(dve):
            with dve.Fori(0, KT) as j:
                for f in range(2):
                    dve.wait_ge(sg["sig"][f], j + 1)
                    for g in range(2):
                        dve.tensor_tensor(mx[f][:, g, :], sig[f][:, g, :], bank(4 * f + 2 * g + 1)[:, 0:HALF],
                                          ALU.mult).then_inc(sg["x"][f], 1)
                    dve.wait_ge(sg["x"][f], 2 * j + 2)
                    dve.tensor_tensor(mT[:, bass.ds(j, 1), f * HALF:(f + 1) * HALF].rearrange("p a t -> p (a t)"),
                                      mx[f][:, 0, :], mx[f][:, 1, :], ALU.add).then_inc(sg["m"][f], 1)

    modb = mem.at(M_OA, 8, D)
    h2T = hT
    x1 = mem.at(M_TB, NT, D)
    xres = [mem.at(M_TB + 5120 + 1024 * b, D) for b in range(2)]
    h2 = mem.at(M_TB + 7168, D)
    h2p = mem.at(M_TB + 8192, D)
    wr = mem.at(M_OB + 3072, KT, NE)
    rbias = sb("rbias", [P, NE])
    sc = mem.at(M_OB + 3584, NT, NE)
    RS1, RS2 = small[:, 0:1], small[:, 1:2]
    sel = mem.at(M_OB + 3904, NT, NE)
    wn = mem.at(M_OB + 4224, NT, NE)
    rsc = mem.at(M_OB + 4544, 576)
    bia, msk, rep, gA64, gB64 = (rsc[:, 64 * n:64 * n + 64] for n in range(5))
    gm8 = rsc[:, 320:384].rearrange("p (a b) -> p a b", b=8)
    gs, rank, m8, wsum = rsc[:, 384:392], rsc[:, 392:400], rsc[:, 400:408], rsc[:, 408:409]
    cst = sb("cst", [P, 128 + 128 + 64 + 64 + 1 + 64 + 64])
    tri, ones = cst[:, 0:128], cst[:, 128:256]
    enum, gtri, pnum = cst[:, 256:320], cst[:, 320:384], cst[:, 384:385]
    triX, triI = cst[0:NE, 385:449], cst[0:NE, 449:513]
    recs = sb("recs", [P, NT * TOPK, 4], I32)
    tabs = sb("tabs", [P, NBLK + RING, 4], I32)
    w13 = [mem.at(M_R + 6144 * ((u + 1) % RING), 2, KT, FE) for u in range(RING)]
    w2 = [mem.at(M_R + 6144 * ((u + 1) % RING) + 4096, 2, D) for u in range(RING)]
    SH = RING - 1
    s_cst = sem("s_cst")
    s_rec = sem("s_rec")
    s_tin = sem("s_tin")
    s_tz = sem("s_tz")
    s_shw = sem("s_shw")
    s_sel = sem("s_sel")
    s_rsel = sem("s_rsel")
    s_modb = sem("s_modb")
    s_wr = sem("s_wr")
    s_rb = sem("s_rb")
    s_xr = [sem(f"s_xr{b}") for b in range(2)]
    s_hp = sem("s_hp")
    names = ("a", "x", "sq", "ms", "rs", "h", "hp", "T", "teV", "teA", "lg", "sc", "c")
    sr = {n: sem(f"s_r_{n}") for n in names}
    select_chain = [0]

    def select(dve, t):
        chain = Chain(dve, s_rsel, select_chain[0])
        dve.wait_ge(sr["sc"], t + 1)
        chain(dve.tensor_tensor(bia, sc[:, t, :], rbias[:, :], ALU.add))
        for g in range(NG):
            ins = dve.max(gm8[:, g, :], bia[:, g * 8:g * 8 + 8])
        chain(ins)
        chain(dve.tensor_tensor(gs.unsqueeze(2), gm8[:, :, 0:1], gm8[:, :, 1:2], ALU.add))
        other = gs.unsqueeze(1).to_broadcast([P, NG, NG])
        own = gs.unsqueeze(2).to_broadcast([P, NG, NG])
        a, b = gA64.rearrange("p (a b) -> p a b", a=8), gB64.rearrange("p (a b) -> p a b", a=8)
        dve.tensor_tensor(a, other, own, ALU.is_gt)
        chain(dve.tensor_tensor(b, other, own, ALU.is_equal))
        chain(dve.tensor_tensor(b, b, gtri.rearrange("p (a b) -> p a b", a=8), ALU.mult))
        chain(dve.tensor_tensor(a, a, b, ALU.add))
        chain(dve.tensor_reduce(rank, a, AX_X, ALU.add))
        chain(dve.tensor_scalar(rank, rank, float(TOPG), None, ALU.is_lt))
        chain(dve.tensor_scalar(gs, rank, BIG, -BIG, ALU.mult, ALU.add))
        bv = bia.rearrange("p (g e) -> p g e", g=NG)
        mv = msk.rearrange("p (g e) -> p g e", g=NG)
        chain(dve.tensor_tensor(mv, bv, rank.unsqueeze(2).to_broadcast([P, NG, 8]), ALU.mult))
        chain(dve.tensor_tensor(mv, mv, gs.unsqueeze(2).to_broadcast([P, NG, 8]), ALU.add))
        chain(dve.max(m8, msk))
        chain(dve.match_replace(rep, m8, msk, -2 * BIG))
        chain(dve.tensor_scalar(sel[:, t, :], rep, -1.5 * BIG, None, ALU.is_lt))
        dve.sem_inc(s_sel, 1)
        chain(dve.tensor_tensor(wn[:, t, :], sc[:, t, :], sel[:, t, :], ALU.mult))
        chain(dve.tensor_reduce(wsum, wn[:, t, :], AX_X, ALU.add))
        chain(dve.reciprocal(wsum, wsum))
        chain(dve.tensor_scalar(wn[:, t, :], wn[:, t, :], wsum, ROUTED_SCALE, ALU.mult, ALU.mult))
        select_chain[0] = chain.n

    with nc.Block() as block:
        @block.sync
        def _(sp):
            sp.wait_ge(s_mrow, 16)
            sp.dma_start(xres[0], I["x_prompt"][0]).then_inc(s_xr[0], 16)
            for r, a in enumerate((2, 3, 6, 7, 4, 5, 0, 1)):
                sp.dma_start(modb[:, a, :], S["mod_rows"][r:r + 1, :].to_broadcast([P, D])).then_inc(s_modb, 16)
            sp.dma_start(xres[1], I["x_sample"][0, 0:P, :]).then_inc(s_xr[1], 16)
            sp.dma_start(wr, I["w_router"][0].rearrange("(k p) n -> p k n", p=P)).then_inc(s_wr, 16)
            sp.dma_start(rbias[:, :], I["router_bias"].to_broadcast([P, NE])).then_inc(s_rb, 16)
            sp.dma_start(cst[:, :], I["route_consts"]).then_inc(s_cst, 16)
            for a, n in enumerate(("w_s1", "w_s3")):
                sp.dma_start(w13[SH][:, a], I[n][0].rearrange("(k p) n -> p k n", p=P)).then_inc(s_shw, 16)
            sp.dma_start(w2[SH], I["w_s2"][0].rearrange("(f p) n -> p f n", p=P)).then_inc(s_shw, 16)
            sp.dma_start(recs[:, :, :], I["records"]).then_inc(s_rec, 16)
            sp.dma_start(tabs[:, 0:NBLK, :], I["empty_slots"]).then_inc(s_tz, 16)
            sp.wait_ge(s_tz, 16)
            sp.dma_start(S["slots"].rearrange("(p n) w -> p n w", n=NBLK), tabs[:, 0:NBLK, :]).then_inc(s_tin, 16)
            for t in range(NT):
                if t >= 1 and t + 1 < NT:
                    sp.wait_ge(sr["x"], 2 * t)
                    sp.dma_start(xres[(t + 1) % 2], I["x_sample"][0, t * P:(t + 1) * P, :])\
                      .then_inc(s_xr[(t + 1) % 2], 16)
                sp.wait_ge(sr["hp"], t + 1)
                sp.dma_start(S["h2"][t * P:(t + 1) * P, :], h2p).then_inc(s_hp, 16)

        @block.tensor
        def _(pe):
            pe.wait_ge(s_wout, 16)

            def out_proj(t):
                if t >= 2:
                    pe.wait_ge(sr["x"], 2 * (t - 2) + 2)
                for c in range(2):
                    for k in range(KT):
                        mm = pe.matmul(bank(2 * (t % 2) + c), mT[:, k, t * P:(t + 1) * P],
                                       wout[:, k, c * 512:(c + 1) * 512], start=(k == 0), stop=(k == KT - 1))
                mm.then_inc(sr["a"], 1)

            def turn(t):
                pe.wait_ge(sr["h"], 2 * (t + 1))
                if t >= 1:
                    pe.wait_ge(sr["teV"], t)
                    pe.wait_ge(sr["teA"], t)
                for k in range(KT):
                    tr = pe.transpose(bank(4, 2)[:, k * P:(k + 1) * P], h2[:, k * P:(k + 1) * P], ident[:, :])
                tr.then_inc(sr["T"], 1)

            def router(t):
                if t == 0:
                    pe.wait_ge(s_wr, 16)
                pe.wait_ge(sr["teV"], t + 1)
                pe.wait_ge(sr["teA"], t + 1)
                if t >= 1:
                    pe.wait_ge(sr["sc"], t)
                for k in range(KT):
                    mm = pe.matmul(bank(6)[:, t * NE:(t + 1) * NE], h2T[:, k, t * P:(t + 1) * P], wr[:, k, :],
                                   start=(k == 0), stop=(k == KT - 1))
                mm.then_inc(sr["lg"], 1)

            out_proj(0)
            for t in range(1, NT):
                out_proj(t)
                turn(t - 1)
                router(t - 1)
            turn(NT - 1)
            router(NT - 1)

        @block.scalar
        def _(act):
            for t in range(NT):
                act.wait_ge(sr["x"], 2 * t + 2)
                if t >= 1:
                    act.wait_ge(sr["hp"], t)
                    act.wait_ge(s_hp, 16 * t)
                act.activation(h2p, x1[:, t, :], ACT.Square, accum_out=RS1).then_inc(sr["sq"], 1)
                act.wait_ge(sr["h"], 2 * t + 2)
                act.activation(h2p.rearrange("q (k p) -> q k p", k=KT), h2.rearrange("q (p k) -> q k p", k=KT),
                               ACT.Copy).then_inc(sr["hp"], 1)
                act.wait_ge(sr["T"], t + 1)
                act.activation(h2T[:, 4:8, t * P:(t + 1) * P], bank(5).rearrange("p (k t) -> p k t", k=4), ACT.Copy)\
                   .then_inc(sr["teA"], 1)
                act.wait_ge(sr["lg"], t + 1)
                act.activation(sc[:, t, :], bank(6)[:, t * NE:(t + 1) * NE], ACT.Sigmoid).then_inc(sr["sc"], 1)

        @block.gpsimd
        def _(pool):
            for t in range(NT):
                pool.wait_ge(sr["sq"], t + 1)
                pool.tensor_scalar(RS1, RS1, 1.0 / D, EPS, ALU.mult, ALU.add).then_inc(sr["ms"], 1)
                pool.wait_ge(sr["ms"], t + 1)
                pool.tensor_tensor(RS2, RS1, nhalf[:, 0:1], ALU.pow).then_inc(sr["rs"], 1)

        @block.vector
        def _(dve):
            dve.wait_ge(s_modb, 16 * 8)
            dve.wait_ge(s_rb, 16)
            dve.wait_ge(s_cst, 16)
            for t in range(NT):
                y = min(t, 1)
                dve.wait_ge(sr["a"], t + 1)
                dve.wait_ge(s_xr[t % 2], 16 * (t // 2 + 1))
                dve.tensor_tensor(x1[:, t, :], bank(2 * (t % 2), 2), modb[:, 2 + y, :], ALU.mult)\
                   .then_inc(sr["x"], 1)
                dve.wait_ge(sr["x"], 2 * t + 1)
                dve.tensor_tensor(x1[:, t, :], x1[:, t, :], xres[t % 2], ALU.add).then_inc(sr["x"], 1)
                dve.wait_ge(sr["rs"], t + 1)
                if t >= 1:
                    dve.wait_ge(sr["T"], t)
                    dve.wait_ge(sr["hp"], t)
                dve.scalar_tensor_tensor(out=h2, in0=x1[:, t, :], scalar=RS2, in1=modb[:, 4 + y, :],
                                         op0=ALU.mult, op1=ALU.mult).then_inc(sr["h"], 1)
                dve.wait_ge(sr["h"], 2 * t + 1)
                dve.tensor_tensor(h2, h2, modb[:, 6 + y, :], ALU.add).then_inc(sr["h"], 1)
                if t >= 1:
                    select(dve, t - 1)
                dve.wait_ge(sr["T"], t + 1)
                dve.tensor_copy(h2T[:, 0:4, t * P:(t + 1) * P], bank(4).rearrange("p (k t) -> p k t", k=4))\
                   .then_inc(sr["teV"], 1)

    g2b = modb[:, 0:2, :]
    ysh = mem.at(M_OA + 2048, NT, D)
    B0 = M_TB + 5120
    hs = mem.at(B0, FE)
    gg = mem.at(B0 + 256, FE)
    gT = mem.at(B0 + 512, 2, P)
    rt = mem.at(B0 + 768, 3840)

    def rv(n, *shape):
        off = n * 320
        v = rt[:, off:off + int(np.prod(shape))]
        return v.rearrange("p (a b) -> p a b", a=shape[0]) if len(shape) == 2 else v

    posv, jv, gsel = (rv(n, NT, NE) for n in range(3))
    ostart, oend = rt[:, 2880:2944], rt[:, 2944:3008]
    k8 = rt[:, 3136:3176].rearrange("p (t k) -> p t k", k=8)
    w8 = rt[:, 3176:3216].rearrange("p (t k) -> p t k", k=8)
    oblk, oblkb = rt[0:NE, 3216:3217], rt[0:NE, 3220:3348]
    ecol = rt[:, 3349:3350]
    cnt = rt[0:NE, 3350:3351]
    eqb = mem.at(M_OB + 2048, TOPK * NE)
    kidx = sb("kidx", [P, NT * TOPK], I32)
    ove = sb("ove", [1, P], I32)
    nblk = sb("nblk", [1, 1], I32)
    s_rv = sem("s_rv")
    s_acc = sem("s_acc")
    s_pos = sem("s_pos")
    s_cnt = sem("s_cnt")
    s_ob = sem("s_ob")
    s_os = sem("s_os")
    s_ec = sem("s_ec")
    s_er = sem("s_er")
    s_ove = sem("s_ove")
    s_k8 = sem("s_k8")
    s_tsc = sem("s_tsc")
    s_tab = sem("s_tab")
    s_w13 = [sem(f"s_w13_{u}") for u in range(RING)]
    s_w2 = [sem(f"s_w2_{u}") for u in range(RING)]
    names = ("h", "si", "g", "T", "te", "y", "ye")
    sh = {n: sem(f"s_sh_{n}") for n in names}
    w13_src = [I[n][0].rearrange("e (p k) n -> p e k n", k=KT) for n in ("w_e1", "w_e3")]
    w2_src = I["w_e2"][0].rearrange("e (f p) n -> p e f n", p=P)

    def load_w13(sp, n, u):
        for a in range(2):
            sp.dma_start(w13[u][:, a], w13_src[a][:, bass.ds(n, 1)].rearrange("p e k n -> p (e k) n"))\
              .then_inc(s_w13[u], 16)

    def load_w2(sp, n, u):
        sp.dma_start(w2[u], w2_src[:, bass.ds(n, 1)].rearrange("p e f n -> p (e f) n")).then_inc(s_w2[u], 16)

    with nc.Block() as block:
        @block.sync
        def _(sp):
            for u in range(SH):
                load_w13(sp, u, u)
                load_w2(sp, u, u)
            for t in range(NT - 1):
                sp.wait_ge(sh["ye"], t + 1)
                sp.dma_start(S["sums"][t * P:(t + 1) * P, :], ysh[:, t, :]).then_inc(s_acc, 16)
            sp.wait_ge(s_tsc, 16 * NT * TOPK)
            sp.dma_start(tabs[:, 0:NBLK, :], S["slots"].rearrange("(p n) w -> p n w", n=NBLK)).then_inc(s_tab, 16)
            sp.wait_ge(sh["ye"], NT)
            sp.dma_start(S["sums"][(NT - 1) * P:NT * P, :], ysh[:, NT - 1, :]).then_inc(s_acc, 16)

        @block.tensor
        def _(pe):
            def up(t):
                if t >= 1:
                    pe.wait_ge(sh["g"], t)
                for k in range(KT):
                    mm = pe.matmul(bank(0).rearrange("p (a n) -> p a n", a=2), h2T[:, k, t * P:(t + 1) * P],
                                   w13[SH][:, :, k, :], start=(k == 0), stop=(k == KT - 1))
                mm.then_inc(sh["h"], 1)

            def turn(t):
                pe.wait_ge(sh["g"], t + 1)
                for f in range(2):
                    tr = pe.transpose(bank(1)[:, f * P:(f + 1) * P], gg[:, f * P:(f + 1) * P], ident[:, :])
                tr.then_inc(sh["T"], 1)

            def down(t):
                pe.wait_ge(sh["te"], t + 1)
                if t >= 1:
                    pe.wait_ge(sh["ye"], t)
                for c in range(2):
                    for f in range(2):
                        mm = pe.matmul(bank(2 + c), gT[:, f, :], w2[SH][:, f, c * 512:(c + 1) * 512],
                                       start=(f == 0), stop=(f == 1))
                mm.then_inc(sh["y"], 1)

            pe.wait_ge(s_shw, 48)
            up(0)
            pe.wait_ge(s_cst, 16)
            pe.wait_ge(s_sel, NT)
            for t in range(NT):
                for a in range(t + 1):
                    mm = pe.matmul(bank(4)[:, t * NE:(t + 1) * NE], tri if a == t else ones, sel[:, a, :],
                                   start=(a == 0), stop=(a == t))
            mm.then_inc(s_pos, 1)
            for t in range(NT):
                mm = pe.matmul(bank(5)[0:NE, 0:1], sel[:, t, :], ones[:, 0:1], start=(t == 0), stop=(t == NT - 1))
            mm.then_inc(s_cnt, 1)
            pe.wait_ge(s_ob, 1)
            pe.matmul(bank(6)[:, 0:NE], oblkb, triX, start=True, stop=True)
            pe.matmul(bank(6)[:, NE:2 * NE], oblkb, triI, start=True, stop=True).then_inc(s_os, 1)
            pe.wait_ge(s_ec, 1)
            pe.matmul(bank(7)[0:1, 0:P], ecol, ident[:, :], start=True, stop=True).then_inc(s_er, 1)
            turn(0)
            for t in range(1, NT):
                up(t)
                down(t - 1)
                turn(t)
            down(NT - 1)

        @block.scalar
        def _(act):
            def silu(t):
                act.wait_ge(sh["h"], t + 1)
                act.activation(hs, bank(0)[:, 0:FE], ACT.Silu).then_inc(sh["si"], 1)

            silu(0)
            for t in range(NT):
                act.wait_ge(sh["T"], t + 1)
                act.activation(gT.rearrange("p f t -> p (f t)"), bank(1)[:, 0:256], ACT.Copy).then_inc(sh["te"], 1)
                if t + 1 < NT:
                    act.wait_ge(sh["g"], t + 1)
                    silu(t + 1)
                act.wait_ge(sh["y"], t + 1)
                act.activation(ysh[:, t, :], bank(2, 2), ACT.Copy).then_inc(sh["ye"], 1)

        @block.gpsimd
        def _(pool):
            pool.wait_ge(s_tin, 16)
            pool.wait_ge(s_k8, 2)
            for n in range(NT * TOPK):
                pool.indirect_dma_start(out=S["slots"], out_offset=bass.IndirectOffsetOnAxis(ap=kidx[:, n:n + 1], axis=0),
                                        in_=recs[:, n, :], in_offset=None,
                                        bounds_check=P * NBLK - 1, oob_is_err=False).then_inc(s_tsc, 16)

        @block.vector
        def _(dve):
            def product(t):
                dve.wait_ge(sh["si"], t + 1)
                if t >= 1:
                    dve.wait_ge(sh["T"], t)
                dve.tensor_tensor(gg, hs, bank(0)[:, FE:2 * FE], ALU.mult).then_inc(sh["g"], 1)

            chain = Chain(dve, s_rv)
            dve.wait_ge(s_hp, 16 * NT)
            select(dve, NT - 1)
            product(0)
            dve.wait_ge(s_cnt, 1)
            chain(dve.tensor_copy(cnt, bank(5)[0:NE, 0:1]))
            chain(dve.tensor_scalar(oblk, cnt, float(P), None, ALU.is_gt))
            for a in range(2, NT):
                chain(dve.scalar_tensor_tensor(out=oblk, in0=cnt, scalar=float(P * a), in1=oblk,
                                               op0=ALU.is_gt, op1=ALU.add))
            dve.tensor_scalar(oblkb, ones[0:NE, :], oblk, None, ALU.mult).then_inc(s_ob, 1)
            dve.wait_ge(s_os, 1)
            chain(dve.tensor_copy(rt[:, 2880:3008], bank(6)[:, 0:2 * NE]))
            chain(dve.tensor_scalar(eqb[:, 0:NE], oend, pnum, None, ALU.is_le))
            chain(dve.tensor_reduce(ecol, eqb[:, 0:NE], AX_X, ALU.add))
            dve.tensor_scalar(ecol, ecol, float(NE - 1), None, ALU.min).then_inc(s_ec, 1)
            chain(dve.tensor_scalar(nblk[:, :], oend[0:1, NE - 1:NE], float(NE), None, ALU.add))
            dve.wait_ge(s_er, 1)
            chain(dve.tensor_copy(ove[:, :], bank(7)[0:1, 0:P]))
            dve.wait_ge(s_pos, 1)
            chain(dve.tensor_copy(posv, bank(4)[:, 0:NT * NE].rearrange("p (t e) -> p t e", t=NT)))
            chain(dve.tensor_scalar(jv, posv, float(P), None, ALU.is_ge))
            for a in range(2, NT):
                chain(dve.scalar_tensor_tensor(out=jv, in0=posv, scalar=float(P * a), in1=jv,
                                               op0=ALU.is_ge, op1=ALU.add))
            chain(dve.scalar_tensor_tensor(out=posv, in0=jv, scalar=-float(P), in1=posv, op0=ALU.mult, op1=ALU.add))
            chain(dve.tensor_tensor(ostart, ostart, enum, ALU.subtract))
            chain(dve.tensor_scalar(ostart, ostart, float(NE - 1), None, ALU.add))
            chain(dve.tensor_tensor(gsel, jv, ostart.unsqueeze(1).to_broadcast([P, NT, NE]), ALU.add))
            chain(dve.tensor_scalar(jv, jv, 1.0, None, ALU.is_ge))
            chain(dve.tensor_tensor(gsel, gsel, jv, ALU.mult))
            chain(dve.tensor_tensor(gsel, gsel, enum.unsqueeze(1).to_broadcast([P, NT, NE]), ALU.add))
            chain(dve.scalar_tensor_tensor(out=gsel, in0=posv, scalar=float(NBLK), in1=gsel,
                                           op0=ALU.mult, op1=ALU.add))
            chain(dve.scalar_tensor_tensor(out=gsel, in0=gsel, scalar=1.0, in1=sel, op0=ALU.add, op1=ALU.mult))
            for t in range(NT):
                chain(dve.max(k8[:, t, :], gsel[:, t, :]))
                e3 = eqb.rearrange("p (k e) -> p k e", k=TOPK)
                chain(dve.tensor_tensor(e3, gsel[:, t, :].unsqueeze(1).to_broadcast([P, TOPK, NE]),
                                        k8[:, t, :].unsqueeze(2).to_broadcast([P, TOPK, NE]), ALU.is_equal))
                chain(dve.tensor_tensor(e3, e3, wn[:, t, :].unsqueeze(1).to_broadcast([P, TOPK, NE]), ALU.mult))
                chain(dve.tensor_reduce(w8[:, t, :], e3, AX_X, ALU.add))
            dve.tensor_scalar(kidx[:, :], k8.rearrange("p t k -> p (t k)"), -1.0, None, ALU.add).then_inc(s_k8, 1)
            dve.wait_ge(s_rec, 16)
            dve.tensor_copy(recs[:, :, 2:3].bitcast(F32), w8.rearrange("p t k -> p (t k)").unsqueeze(2))\
               .then_inc(s_k8, 1)
            for t in range(1, NT):
                product(t)

    xg = [mem.at(B0 + 768 + 1024 * b, D) for b in range(2)]
    xT = mem.at(B0 + 2816, KT, P)
    yb = sb("yb", [P, D])
    held = sb("held", [1, 2])
    gi = [sb(f"gi{b}", [P, 1], I32) for b in range(2)]
    si = sb("si", [P, 1], I32)
    names = ("gi", "si", "Tx", "xeV", "xeA", "u", "sl", "g", "Th", "te", "y", "yV", "yA", "z")
    se = {n: sem(f"s_e_{n}") for n in names}
    s_xg = [sem(f"s_xg{b}") for b in range(2)]
    s_sc = sem("s_sc")
    pX, pH, pG, pY = psum[:, 0:1024], bank(2), bank(3), psum[:, 2048:3072]

    def wslot(tab, n, w):
        return tab[:, bass.ds(n, 1), w:w + 1].rearrange("p n w -> p (n w)")

    with nc.Block() as block:
        def run(eng, step, total=None):
            for u in range(RING):
                step(u, 0, u, lambda k, u=u: None if u >= k else False)
            with eng.Fori(1, NE // RING) as i:
                for u in range(RING):
                    step(RING * i + u, i, u, lambda k: None)
            nb = eng.value_load(nblk[0:1, 0:1], min_val=NE, max_val=NBLK)
            with eng.Fori(NE // RING, NBLK // RING + 1) as i:
                with eng.If(RING * i - 3 < nb):
                    for u in range(RING):
                        n = RING * i + u
                        step(n, i, u, lambda k, n=n: n - k < nb)
            return nb

        def due(eng, cond, what):
            if cond is None:
                what()
            elif cond is not False:
                with eng.If(cond):
                    what()

        @block.sync
        def _(sp):
            def step(n, i, u, guard):
                def loads():
                    if isinstance(n, int):
                        if n < SH:
                            return
                        load_w13(sp, n, u)
                        load_w2(sp, n, u)
                        return
                    e = n
                    if past[0]:
                        e = sp.value_load(ove[0:1, bass.ds(n - NE, 1)], min_val=0, max_val=NE - 1)
                    sp.wait_ge(se["u"], n - RING + 1)
                    load_w13(sp, e, u)
                    sp.wait_ge(se["y"], n - RING + 1)
                    load_w2(sp, e, u)
                due(sp, guard(0), loads)

            past = [False]
            for u in range(RING):
                step(u, 0, u, lambda k: None)
            with sp.Fori(1, NE // RING) as i:
                for u in range(RING):
                    step(RING * i + u, i, u, lambda k: None)
            past[0] = True
            nb = sp.value_load(nblk[0:1, 0:1], min_val=NE, max_val=NBLK)
            with sp.Fori(NE // RING, NBLK // RING) as i:
                with sp.If(RING * i < nb):
                    for u in range(RING):
                        n = RING * i + u
                        step(n, i, u, lambda k, n=n: n < nb)

        @block.gpsimd
        def _(pool):
            pool.memset(xg[0], 0.0).then_inc(se["z"], 1)
            pool.memset(xg[1], 0.0).then_inc(se["z"], 1)
            pool.wait_ge(s_tab, 16)
            pool.wait_ge(s_acc, 16 * NT)
            pool.wait_ge(s_hp, 16 * NT)
            pool.wait_ge(se["z"], 2)

            def hold(pool, c=0):
                pool.tensor_tensor(held[:, c:c + 1], nhalf[0:1, 0:1], nhalf[0:1, 0:1], ALU.add)

            def step(n, i, u, guard):
                first = isinstance(n, int)

                def gather():
                    if not first or u >= 2:
                        pool.wait_ge(se["Tx"], n - 1)
                    pool.tensor_copy(gi[u % 2][:, :], wslot(tabs, n, 0)).then_inc(se["gi"], 1)
                    pool.wait_ge(se["gi"], n + 1)
                    hold(pool)
                    pool.indirect_dma_start(out=xg[u % 2], out_offset=None, in_=S["h2"],
                                            in_offset=bass.IndirectOffsetOnAxis(ap=gi[u % 2][:, 0:1], axis=0),
                                            bounds_check=TOK - 1, oob_is_err=False).then_inc(s_xg[u % 2], 16)

                def scatter():
                    m = n - 3
                    if not (first and u == 3):
                        pool.wait_ge(s_sc, 16 * m)
                        hold(pool, 1)
                    pool.tensor_copy(si[:, :], wslot(tabs, m, 0)).then_inc(se["si"], 1)
                    pool.wait_ge(se["si"], m + 1)
                    pool.wait_ge(se["yV"], m + 1)
                    pool.wait_ge(se["yA"], m + 1)
                    hold(pool)
                    pool.indirect_dma_start(out=S["sums"], out_offset=bass.IndirectOffsetOnAxis(ap=si[:, 0:1], axis=0),
                                            in_=yb[:, :], in_offset=None, compute_op=ALU.add,
                                            bounds_check=TOK - 1, oob_is_err=False).then_inc(s_sc, 16)

                due(pool, guard(0), gather)
                due(pool, guard(3), scatter)

            nb = run(pool, step)
            pool.wait_ge(s_sc, nb * 16)

        @block.tensor
        def _(pe):
            def step(n, i, u, guard):
                def turn_x():
                    pe.wait_ge(s_xg[u % 2], 32 * i + 16 * (u // 2 + 1))
                    for k in range(KT):
                        tr = pe.transpose(pX[:, k * P:(k + 1) * P], xg[u % 2][:, k * P:(k + 1) * P], ident[:, :])
                    tr.then_inc(se["Tx"], 1)

                def down():
                    v = (u - 2) % RING
                    pe.wait_ge(se["te"], n - 1)
                    pe.wait_ge(s_w2[v], 16 * (i + 1 if u >= 2 else i))
                    if not (isinstance(n, int) and u == 2):
                        pe.wait_ge(se["yV"], n - 2)
                        pe.wait_ge(se["yA"], n - 2)
                    for c in range(2):
                        for f in range(2):
                            mm = pe.matmul(pY[:, c * 512:(c + 1) * 512], gT[:, f, :],
                                           w2[v][:, f, c * 512:(c + 1) * 512], start=(f == 0), stop=(f == 1))
                    mm.then_inc(se["y"], 1)

                def turn_g():
                    pe.wait_ge(se["g"], n)
                    for f in range(2):
                        tr = pe.transpose(pG[:, f * P:(f + 1) * P], gg[:, f * P:(f + 1) * P], ident[:, :])
                    tr.then_inc(se["Th"], 1)

                def up():
                    pe.wait_ge(se["xeV"], n + 1)
                    pe.wait_ge(se["xeA"], n + 1)
                    pe.wait_ge(s_w13[u], 32 * (i + 1))
                    for k in range(KT):
                        mm = pe.matmul(pH.rearrange("p (a n) -> p a n", a=2), xT[:, k, :], w13[u][:, :, k, :],
                                       start=(k == 0), stop=(k == KT - 1))
                    mm.then_inc(se["u"], 1)

                due(pe, guard(0), turn_x)
                due(pe, guard(2), down)
                due(pe, guard(1), turn_g)
                due(pe, guard(0), up)

            run(pe, step)

        @block.scalar
        def _(act):
            def step(n, i, u, guard):
                def take_x():
                    act.wait_ge(se["Tx"], n + 1)
                    act.activation(xT[:, 4:8, :].rearrange("p k t -> p (k t)"), pX[:, 512:1024], ACT.Copy)\
                       .then_inc(se["xeA"], 1)

                def take_y():
                    m = n - 2
                    act.wait_ge(se["y"], m + 1)
                    if not (isinstance(n, int) and u == 2):
                        act.wait_ge(s_sc, 16 * m)
                    act.activation(yb[:, 512:1024], pY[:, 512:1024], ACT.Copy,
                                   scale=wslot(tabs, m, 2).bitcast(F32)).then_inc(se["yA"], 1)

                def silu():
                    act.wait_ge(se["u"], n + 1)
                    if not (isinstance(n, int) and u == 0):
                        act.wait_ge(se["g"], n)
                    act.activation(hs, pH[:, 0:FE], ACT.Silu).then_inc(se["sl"], 1)

                due(act, guard(0), take_x)
                due(act, guard(2), take_y)
                due(act, guard(0), silu)

            run(act, step)

        @block.vector
        def _(dve):
            def step(n, i, u, guard):
                def take_x():
                    dve.wait_ge(se["Tx"], n + 1)
                    dve.tensor_copy(xT[:, 0:4, :].rearrange("p k t -> p (k t)"), pX[:, 0:512]).then_inc(se["xeV"], 1)

                def take_y():
                    m = n - 2
                    dve.wait_ge(se["y"], m + 1)
                    if not (isinstance(n, int) and u == 2):
                        dve.wait_ge(s_sc, 16 * m)
                    dve.tensor_scalar(yb[:, 0:512], pY[:, 0:512], wslot(tabs, m, 2).bitcast(F32), None,
                                      ALU.mult).then_inc(se["yV"], 1)

                def take_g():
                    dve.wait_ge(se["Th"], n)
                    dve.tensor_copy(gT.rearrange("p f t -> p (f t)"), pG[:, 0:256]).then_inc(se["te"], 1)

                def product():
                    dve.wait_ge(se["sl"], n + 1)
                    dve.tensor_tensor(gg, hs, pH[:, FE:2 * FE], ALU.mult).then_inc(se["g"], 1)

                due(dve, guard(0), take_x)
                due(dve, guard(2), take_y)
                due(dve, guard(1), take_g)
                due(dve, guard(0), product)

            run(dve, step)

    yt = mem.at(M_R, NT, D)
    s_yt = [sem(f"s_yt{t}") for t in range(NT)]
    s_cb = sem("s_cb")
    s_cc = sem("s_cc")
    s_fin = sem("s_fin")
    with nc.Block() as block:
        @block.sync
        def _(sp):
            for t in range(NT):
                sp.dma_start(yt[:, t, :], S["sums"][t * P:(t + 1) * P, :]).then_inc(s_yt[t], 16)

        @block.scalar
        def _(act):
            for t in range(NT):
                act.wait_ge(s_cc, t + 1)
                dst = O["yp"][0] if t == 0 else O["ys"][0, (t - 1) * P:t * P, :]
                act.dma_start(dst, yt[:, t, :]).then_inc(s_fin, 16)
            act.wait_ge(s_fin, 16 * NT)

        @block.vector
        def _(dve):
            for t in range(NT):
                r = yt[:, t, :]
                dve.wait_ge(s_yt[t], 16)
                dve.tensor_tensor(r, r, g2b[:, min(t, 1), :], ALU.mult).then_inc(s_cb, 1)
                dve.wait_ge(s_cb, t + 1)
                dve.tensor_tensor(r, r, x1[:, t, :], ALU.add).then_inc(s_cc, 1)


def rope_tables(width):
    t = np.arange(LAT)
    axis = width // 2
    inv = THETA ** (-np.arange(0, axis, 2, dtype=np.float32) / axis)
    ang = np.concatenate([(t // GRID_W)[:, None] * inv, (t % GRID_W)[:, None] * inv], -1).astype(np.float32)
    cos, sin = np.cos(ang), np.sin(ang)
    c = np.concatenate([np.ones((SEQ, width)), np.concatenate([cos, cos], -1)], 0)
    s = np.concatenate([np.zeros((SEQ, width)), np.concatenate([-sin, sin], -1)], 0)
    return c.astype(np.float32), s.astype(np.float32)


def constants():
    c = {"ident": np.eye(P, dtype=np.float32)}
    c["cos_a"], c["sin_a"] = rope_tables(HD)
    c["cos_b"], c["sin_b"] = rope_tables(ROPE)
    i = np.arange(P)
    e = np.arange(NE)
    g = np.arange(NG)
    route = np.zeros((P, 513), np.float32)
    route[:, 0:128] = i[:, None] < i[None, :]
    route[:, 128:256] = 1
    route[:, 256:320] = e
    route[:, 320:384] = (g[None, :] < g[:, None]).reshape(1, -1)
    route[:, 384] = i
    route[0:NE, 385:449] = e[:, None] < e[None, :]
    route[0:NE, 449:513] = e[:, None] <= e[None, :]
    c["route_consts"] = route
    rec = np.zeros((P, NT, TOPK, 4), np.int32)
    tok = np.arange(NT)[None, :, None] * P + i[:, None, None]
    rec[..., 0] = tok
    c["records"] = rec.reshape(P, NT * TOPK, 4)
    empty = np.zeros((P, NBLK, 4), np.int32)
    empty[..., 0] = TOK
    c["empty_slots"] = empty
    return c


_INS = ["x_prompt", "x_sample", "c", "cache_gqa_k", "cache_gqa_v", "cache_mla_ckv", "cache_mla_krope", "c_ctx",
        "w_mod", "b_mod", "norm1_g", "norm2_g", "w_in", "gqa_qn", "gqa_kn", "mla_qa_g", "mla_kva_g", "w_qb",
        "w_kvb", "mla_qn_nope", "mla_qn_rope", "mla_kn_nope", "mla_kn_rope", "w_oa", "w_ob", "w_out",
        "w_router", "router_bias", "w_e1", "w_e3", "w_e2", "w_s1", "w_s3", "w_s2"]
_OUTS = [("yp", (1, SEQ, D)), ("ys", (1, LAT, D)), ("gk", (1, 1, KVA, SEQ, HD)), ("gv", (1, 1, KVA, SEQ, HD)),
         ("ckv", (1, 1, SEQ, KVL)), ("kr", (1, 1, SEQ, ROPE))]


def kernel(**inputs):
    import concourse.bacc as bacc
    from concourse.bass_utils import run_bass_kernel_spmd

    nc = bacc.Bacc("TRN2", target_bir_lowering=False, num_devices=1)
    arrays, ins = {}, {}
    for name, a in [(n, inputs[n]) for n in _INS] + list(constants().items()):
        a = np.ascontiguousarray(a)
        arrays[f"in_{name}"] = a
        ins[name] = nc.dram_tensor(f"in_{name}", a.shape, mybir.dt.from_np(a.dtype), kind="ExternalInput").ap()
    outs = {n: nc.dram_tensor(f"out_{n}", s, F32, kind="ExternalOutput").ap() for n, s in _OUTS}
    scratch = {
        "mod_rows": nc.dram_tensor("mod_rows", [8, D], F32, kind="Internal").ap(),
        "h2": nc.dram_tensor("h2", [TOK, D], F32, kind="Internal").ap(),
        "slots": nc.dram_tensor("slots", [P * NBLK, 4], I32, kind="Internal").ap(),
        "sums": nc.dram_tensor("sums", [TOK, D], F32, kind="Internal").ap(),
    }
    program(nc, ins, outs, scratch)
    r = run_bass_kernel_spmd(nc, [arrays], core_ids=[0])
    return tuple(r.results[0][f"out_{n}"] for n, _ in _OUTS)
```

```python
from contextlib import ExitStack

import numpy as np

import concourse.bass as bass
from concourse import mybir

F32 = mybir.dt.float32
F32R = mybir.dt.float32r
I32 = mybir.dt.int32
ALU = mybir.AluOpType
ACT = mybir.ActivationFunctionType
AX_X = mybir.AxisListType.X

P = 128
D = 1024
SEQ, LAT, PAST = 128, 512, 128
TOK = SEQ + LAT
NT = TOK // P
KT = D // P
GRID_W = 64
EPS = 1e-6
THETA = 10000.0
N_MOD = 6
HA, KVA, HD = 8, 2, 128
HB, QL, KVL, NOPE, ROPE, VD = 8, 256, 128, 128, 64, 128
KEYS = TOK + PAST
NK = KEYS // P
NE, TOPK, NG, TOPG = 64, 8, 8, 4
FE = 256
ROUTED_SCALE = 2.5
BIG = 1e30
OVF = TOK * TOPK // P
NBLK = NE + OVF
RING = 4
C_QA, C_KA, C_VA = 0, 1024, 1280
C_CQ, C_CKV, C_KR = 1536, 1792, 1920
C_GA, C_GB = 1984, 3008
ZN = C_GA - C_KA
Z_K, Z_V, Z_CQ, Z_CKV, Z_KR = 0, 256, 512, 768, 896


def key_col(t):
    return 0 if t == 0 else P * (t + 1)


class Mem:

    def __init__(self, first, second, border):
        self.tensors, self.border = (first, second), border

    def at(self, off, *shape, rows=P):
        n = int(np.prod(shape))
        t, base = (self.tensors[0], 0) if off < self.border else (self.tensors[1], self.border)
        v = t[0:rows, off - base:off - base + n]
        if len(shape) == 2:
            v = v.rearrange("p (a b) -> p a b", a=shape[0])
        if len(shape) == 3:
            v = v.rearrange("p (a b c) -> p a b c", a=shape[0], b=shape[1])
        return v


def program(nc, I, O, S):
    ctx = ExitStack()
    with ctx:
        build(nc, I, O, S, ctx)


def build(nc, I, O, S, ctx):
    def sb(name, shape, dt=F32):
        return ctx.enter_context(nc.sbuf_tensor(name, shape, dt))

    def sem(name):
        return ctx.enter_context(nc.semaphore(name))

    M_H, M_OA, M_OB, M_R, M_SC, M_TB = 0, 5120, 10240, 15360, 31744, 40320
    M_END = M_TB + 9728
    mem_at = -(-nc.sbuf_base // 32) * 32
    mem = Mem(sb("mem_h", [P, M_OA]), sb("mem", [P, M_END - M_OA]), M_OA)
    hT = mem.at(M_H, KT, TOK)
    oA = mem.at(M_OA, HA, TOK)
    oB = mem.at(M_OB, HB, TOK)
    ident = sb("ident", [P, P])
    cols = sb("cols", [P, 84])
    modc = sb("modc", [P, 16, 2])
    small = sb("small", [P, 128])
    nhalf = sb("nhalf", [P, 16])
    psum = ctx.enter_context(nc.psum_tensor("psum", [P, 4096], F32))

    def bank(b, n=1):
        return psum[:, b * 512:(b + n) * 512]

    CqA = mem.at(M_TB, NT, HD)
    SqA = mem.at(M_TB + 640, NT, HD)
    CkA = mem.at(M_TB + 1280, NT, HD)
    SkA = mem.at(M_TB + 1920, NT, HD)
    CqB = mem.at(M_TB + 2560, NT, ROPE)
    SqB = mem.at(M_TB + 2880, NT, ROPE)
    CkB = mem.at(M_TB + 3200, NT, ROPE)
    SkB = mem.at(M_TB + 3520, NT, ROPE)
    kTA = mem.at(M_TB + 3840, KVA, KEYS)
    vA = mem.at(M_TB + 5376, NK, KVA, HD)
    krT = mem.at(M_TB + 6912, KEYS, rows=ROPE)
    cqT = mem.at(M_TB + 7680, 2, TOK)
    ckvT = mem.at(M_TB + 8960, KEYS)

    A1, rstd = small[:, 0:16].rearrange("p (k y) -> p k y", y=2), small[:, 16:21]
    ss = small[:, 24:29]
    invlen = small[:, 32:37]
    qk_gain = small[:, 40:41]

    SCALE_A = float(HD) ** -0.5
    SCALE_B = float(NOPE + ROPE) ** -0.5

    s_const = sem("s_const")
    s_rows = sem("s_rows")
    s_x = [sem(f"s_x{t}") for t in range(NT)]
    s_wm = [sem(f"s_wm{b}") for b in range(8)]
    s_wz = [sem(f"s_wz{n}") for n in range(2)]
    s_silu = sem("s_silu")
    s_rowsT = sem("s_rowsT")
    s_cols = sem("s_cols")
    s_mod1 = sem("s_mod1")
    s_modr = sem("s_modr")
    s_modT = sem("s_modT")
    s_A1 = sem("s_A1")
    s_sqx = sem("s_sqx")
    s_rstd = sem("s_rstd")
    s_xs = sem("s_xs")
    s_xT = sem("s_xT")
    s_xeV, s_xeA = sem("s_xeV"), sem("s_xeA")
    s_v = sem("s_v")
    s_p = sem("s_p")
    s_tabs = sem("s_tabs")
    s_gain = sem("s_gain")

    rows = mem.at(M_SC + 5120, 128, rows=84)
    xt = mem.at(M_SC, NT, D)
    sqd = mem.at(M_SC + 5248, D)
    gA = mem.at(M_R + 6144 + 7680, 4, HD)
    gB = mem.at(M_R + 6144 + 7680 + 512, 4, ROPE)
    wmod = [mem.at(M_OA + 4096 * b, KT, 512) for b in range(4)]
    wz = mem.at(M_R + 6144, KT, ZN)
    w_mod_v = I["w_mod"][0].rearrange("(k p) n -> p k n", p=P)
    w_in_v = I["w_in"][0].rearrange("(k p) n -> p k n", p=P)
    pm = bank(7)[:, 0:32].rearrange("p (c y) -> p c y", y=2)
    modr = mem.at(M_SC + 6272, 4, 512, rows=2)

    class Chain:

        def __init__(self, eng, s, n=0):
            self.eng, self.s, self.n = eng, s, n

        def __call__(self, ins):
            self.n = self.n + 1
            ins.then_inc(self.s, 1)
            self.eng.wait_ge(self.s, self.n)


    with nc.Block() as block:
        @block.sync
        def _(sp):
            def load_mod(c, half):
                k = half * KT // 2
                sp.dma_start(wmod[c][:, k:k + KT // 2, :], w_mod_v[:, k:k + KT // 2, c * 512:(c + 1) * 512])\
                  .then_inc(s_wm[2 * c + half], 16)

            load_mod(0, 0)
            sp.dma_start(rows[0:8, :], I["c_ctx"].rearrange("(k p) -> k p", p=P)).then_inc(s_rows, 16)
            sp.dma_start(rows[8:16, :], I["c"].rearrange("a (k p) -> (a k) p", p=P)).then_inc(s_rows, 16)
            sp.dma_start(rows[16:64, :], I["b_mod"].rearrange("a (k p) -> (a k) p", p=P)).then_inc(s_rows, 16)
            sp.dma_start(rows[64:72, :], I["norm1_g"].rearrange("a (k p) -> (a k) p", p=P)).then_inc(s_rows, 16)
            sp.dma_start(rows[72:80, :], I["norm2_g"].rearrange("a (k p) -> (a k) p", p=P)).then_inc(s_rows, 16)
            sp.dma_start(rows[80:82, :], I["mla_qa_g"].rearrange("a (k p) -> (a k) p", p=P)).then_inc(s_rows, 16)
            sp.dma_start(rows[82:83, :], I["mla_qn_nope"]).then_inc(s_rows, 16)
            sp.dma_start(rows[83:84, :], I["mla_kn_nope"]).then_inc(s_rows, 16)
            sp.dma_start(ident[:, :], I["ident"]).then_inc(s_const, 16)
            for c in range(4):
                if c > 0:
                    load_mod(c, 0)
                load_mod(c, 1)
                if c == 1:
                    sp.dma_start(xt[:, 0, :], I["x_prompt"][0]).then_inc(s_x[0], 16)
                    for t in range(1, NT):
                        sp.dma_start(xt[:, t, :], I["x_sample"][0, (t - 1) * P:t * P, :]).then_inc(s_x[t], 16)
            for n, (a, b) in enumerate(((0, 512), (512, ZN))):
                sp.dma_start(wz[:, :, a:b], w_in_v[:, :, C_KA + a:C_KA + b]).then_inc(s_wz[n], 16)
            for n, (dst, src, w) in enumerate((
                    (gA[:, 0:2, :], I["gqa_qn"], HD), (gA[:, 2:4, :], I["gqa_kn"], HD),
                    (gB[:, 0:2, :], I["mla_qn_rope"], ROPE), (gB[:, 2:4, :], I["mla_kn_rope"], ROPE))):
                h = w // 2
                sp.dma_start(dst[:, 0, :], src.to_broadcast([P, w])).then_inc(s_gain, 16)
                sp.dma_start(dst[:, 1, 0:h], src[:, h:w].to_broadcast([P, h])).then_inc(s_gain, 16)
                sp.dma_start(dst[:, 1, h:w], src[:, 0:h].to_broadcast([P, h])).then_inc(s_gain, 16)
            for dst, src in ((CqA, I["cos_a"]), (SqA, I["sin_a"]), (CqB, I["cos_b"]), (SqB, I["sin_b"])):
                sp.dma_start(dst, src.rearrange("(t p) w -> p t w", p=P)).then_inc(s_tabs, 16)

        @block.gpsimd
        def _(pool):
            pool.memset(nhalf[:, :], -0.5).then_inc(s_p, 1)
            pool.memset(invlen[:, 0:2], 1.0 / HD).then_inc(s_p, 1)
            pool.memset(invlen[:, 2:3], 1.0 / QL).then_inc(s_p, 1)
            pool.memset(invlen[:, 3:4], 1.0 / KVL).then_inc(s_p, 1)
            pool.memset(invlen[:, 4:5], 1.0 / ROPE).then_inc(s_p, 1)
            pool.wait_ge(s_sqx, NT)
            pool.wait_ge(s_p, 5)
            pool.tensor_scalar(ss, ss, 1.0 / D, EPS, ALU.mult, ALU.add).then_inc(s_p, 1)
            pool.wait_ge(s_p, 6)
            pool.tensor_tensor(rstd, ss, nhalf[:, 0:NT], ALU.pow).then_inc(s_rstd, 1)

        @block.scalar
        def _(act):
            act.wait_ge(s_rows, 16 * 8)
            act.activation(rows[0:16, :], rows[0:16, :], ACT.Silu).then_inc(s_silu, 1)
            for t in range(NT):
                act.wait_ge(s_x[t], 16)
                if t:
                    act.wait_ge(s_sqx, t)
                act.activation(sqd, xt[:, t, :], ACT.Square, accum_out=ss[:, t:t + 1]).then_inc(s_sqx, 1)
            for c in range(4):
                act.wait_ge(s_mod1, c + 1)
                act.activation(modr[:, c, :], bank(c)[0:2, :], ACT.Copy).then_inc(s_modr, 1)
            act.wait_ge(s_A1, 3)
            for t in range(NT):
                y = min(t, 1)
                act.wait_ge(s_xT, t + 1)
                for k in range(4, 8):
                    ins = act.activation(hT[:, k, t * P:(t + 1) * P],
                                         bank(2 * (t % 2) + 1)[:, (k - 4) * P:(k - 3) * P], ACT.Identity,
                                         bias=modc[:, k, y:y + 1], scale=A1[:, k, y:y + 1])
                ins.then_inc(s_xeA, 1)

        @block.vector
        def _(dve):
            chain = Chain(dve, s_v)
            dve.wait_ge(s_rowsT, 1)
            chain(dve.tensor_copy(cols[:, :], bank(6)[:, 0:84]))
            dve.sem_inc(s_cols, 1)
            chain(dve.tensor_tensor(qk_gain, cols[:, 82:83], cols[:, 83:84], ALU.mult))
            chain(dve.tensor_scalar(qk_gain, qk_gain, SCALE_B, None, ALU.mult))
            dve.wait_ge(s_rstd, 1)
            for t in range(NT):
                dve.tensor_scalar(xt[:, t, :], xt[:, t, :], rstd[:, t:t + 1], None, ALU.mult).then_inc(s_xs, 1)
            dve.wait_ge(s_modT, 1)
            bias = cols[:, 16:32].unsqueeze(2).to_broadcast([P, 16, 2])
            dve.tensor_tensor(modc[:, 0:16, :], pm[:, 0:16, :], bias, ALU.add).then_inc(s_A1, 1)
            dve.wait_ge(s_A1, 1)
            dve.tensor_scalar(A1, modc[:, 8:16, :], 1.0, None, ALU.add).then_inc(s_A1, 1)
            dve.wait_ge(s_A1, 2)
            gain = cols[:, 64:72].unsqueeze(2).to_broadcast([P, KT, 2])
            dve.tensor_tensor(A1, A1, gain, ALU.mult).then_inc(s_A1, 1)
            dve.wait_ge(s_A1, 3)
            for t in range(NT):
                y = min(t, 1)
                dve.wait_ge(s_xT, t + 1)
                for k in range(4):
                    ins = dve.tensor_scalar(hT[:, k, t * P:(t + 1) * P],
                                            bank(2 * (t % 2))[:, k * P:(k + 1) * P],
                                            A1[:, k, y:y + 1], modc[:, k, y:y + 1], ALU.mult, ALU.add)
                ins.then_inc(s_xeV, 1)

        @block.tensor
        def _(pe):
            pe.wait_ge(s_const, 16)
            pe.wait_ge(s_silu, 1)
            pe.transpose(bank(6)[:, 0:84], rows[0:84, :], ident[0:84, 0:84]).then_inc(s_rowsT, 1)
            pe.wait_ge(s_cols, 1)
            for c in range(4):
                for k in range(KT):
                    if k % (KT // 2) == 0:
                        pe.wait_ge(s_wm[2 * c + min(k, 1)], 16)
                    mm = pe.matmul(bank(c)[0:2, :], cols[:, k:k + 9:8], wmod[c][:, k, :],
                                   start=(k == 0), stop=(k == KT - 1))
                mm.then_inc(s_mod1, 1)
            for c in range(4):
                pe.wait_ge(s_modr, c + 1)
                for j in range(4):
                    tr = pe.transpose(pm[:, 4 * c + j, :], modr[:, c, j * P:(j + 1) * P], ident[0:2, 0:2])
            tr.then_inc(s_modT, 1)
            for t in range(NT):
                pe.wait_ge(s_xs, t + 1)
                if t >= 2:
                    pe.wait_ge(s_xeV, t - 1)
                    pe.wait_ge(s_xeA, t - 1)
                for k in range(KT):
                    tr = pe.transpose(bank(2 * (t % 2), 2)[:, k * P:(k + 1) * P],
                                      xt[:, t, k * P:(k + 1) * P], ident[:, :])
                tr.then_inc(s_xT, 1)

    zs = [mem.at(M_SC + 960 * b, ZN) for b in range(2)]
    zq = [mem.at(M_SC + 1920 + 960 * b, ZN) for b in range(2)]
    zn = [mem.at(M_SC + 3840 + 960 * b, ZN) for b in range(2)]
    rot = mem.at(M_SC + 5760, 256)
    kgB = mem.at(M_SC + 6016, KVL)
    cache = mem.at(M_SC + 6144, 448)
    wq = mem.at(M_OB, KT, HA * HD)
    wqb = mem.at(M_R + 12288, 2, HB * (NOPE + ROPE))
    wkvb_at = -(-nc.sbuf_base // 32) * 32
    wkvb = sb("wkvb", [P, HB * (NOPE + VD)])[:, :]
    s_wqb = sem("s_wqb")
    s_wkvb = sem("s_wkvb")
    s_z = sem("s_z")
    s_zs = sem("s_zs")
    s_zq = sem("s_zq")
    s_zm = sem("s_zm")
    s_zr = sem("s_zr")
    s_zn = sem("s_zn")
    s_zT = sem("s_zT")
    s_zeV, s_zeA = sem("s_zeV"), sem("s_zeA")
    s_cache = sem("s_cache")
    s_out = sem("s_out")
    s_v2 = sem("s_v2")
    s_p2 = sem("s_p2")
    s_wq = sem("s_wq")
    s_vc = sem("s_vc")

    pZ, pS, pT_ps, pO, pC = psum[:, 0:1024], psum[:, 1024:2048], psum[:, 2048:3072], bank(6), bank(7)[:, 0:P]

    def project_gqa(pe, h, t):
        for k in range(KT):
            mm = pe.matmul(pZ[:, t * P:(t + 1) * P], hT[:, k, t * P:(t + 1) * P],
                           wq[:, k, bass.ds(h * HD, HD)], start=(k == 0), stop=(k == KT - 1))
        return mm

    def project_mla(pe, h, t):
        w = NOPE + ROPE
        for k in range(2):
            pe.matmul(pZ[:, t * P:(t + 1) * P], cqT[:, k, t * P:(t + 1) * P],
                      wqb[:, k, bass.ds(h * w, NOPE)], start=(k == 0), stop=(k == 1))
        for k in range(2):
            mm = pe.matmul(pZ[:, 640 + t * ROPE:640 + (t + 1) * ROPE], cqT[:, k, t * P:(t + 1) * P],
                           wqb[:, k, bass.ds(h * w + NOPE, ROPE)], start=(k == 0), stop=(k == 1))
        return mm

    with nc.Block() as block:
        @block.sync
        def _(sp):
            for g in range(KVA):
                sp.dma_start(cache[:, g * HD:(g + 1) * HD], I["cache_gqa_k"][0, 0, g]).then_inc(s_cache, 16)
                sp.dma_start(vA[:, 1, g, :], I["cache_gqa_v"][0, 0, g]).then_inc(s_vc, 16)
            sp.dma_start(cache[:, 256:384], I["cache_mla_ckv"][0, 0]).then_inc(s_cache, 16)
            sp.dma_start(cache[:, 384:448], I["cache_mla_krope"][0, 0]).then_inc(s_cache, 16)
            sp.dma_start(kgB, I["mla_kva_g"].to_broadcast([P, KVL])).then_inc(s_cache, 16)
            sp.dma_start(wq, w_in_v[:, :, C_QA:C_KA]).then_inc(s_wq, 16)
            sp.dma_start(wkvb, I["w_kvb"][0]).then_inc(s_wkvb, 16)
            sp.wait_ge(s_zn, 1)
            for g in range(KVA):
                sp.dma_start(O["gk"][0, 0, g], zn[0][:, Z_K + g * HD:Z_K + (g + 1) * HD]).then_inc(s_out, 16)
                sp.dma_start(O["gv"][0, 0, g], vA[:, 0, g, :]).then_inc(s_out, 16)
            sp.dma_start(O["ckv"][0, 0], zn[0][:, Z_CKV:Z_CKV + KVL]).then_inc(s_out, 16)
            sp.dma_start(O["kr"][0, 0], zn[0][:, Z_KR:Z_KR + ROPE]).then_inc(s_out, 16)
            sp.wait_ge(s_out, 16 * 6)

        @block.tensor
        def _(pe):
            def project(t):
                b = 2 * (t % 2)
                if t >= 2:
                    pe.wait_ge(s_zs, t - 1)
                for c0, c1, bb in ((0, 512, b), (512, ZN, b + 1)):
                    if t == 0:
                        pe.wait_ge(s_wz[bb - b], 16)
                    for k in range(KT):
                        mm = pe.matmul(bank(bb)[:, 0:c1 - c0], hT[:, k, t * P:(t + 1) * P], wz[:, k, c0:c1],
                                       start=(k == 0), stop=(k == KT - 1))
                mm.then_inc(s_z, 1)

            def turn(t):
                if t < NT:
                    pe.wait_ge(s_zn, t + 1)
                    src = [zn[t % 2][:, o:o + w] for o, w in ((0, P), (P, P), (Z_CQ, P), (Z_CQ + P, P),
                                                              (Z_CKV, P), (Z_KR, ROPE))]
                    at = [0, 1, 2, 3, 4, 5]
                else:
                    pe.wait_ge(s_cache, 16 * 5)
                    src = [cache[:, o:o + w] for o, w in ((0, P), (P, P), (256, P), (384, ROPE))]
                    at = [0, 1, 4, 5]
                if t >= 1:
                    pe.wait_ge(s_zeV, t)
                    pe.wait_ge(s_zeA, t)
                for a, s in zip(at, src):
                    w = ROPE if a == 5 else P
                    tr = pe.transpose(bank(4, 2)[0:w, a * P:(a + 1) * P], s, ident[:, :])
                tr.then_inc(s_zT, 1)

            project(0)
            for t in range(1, NT):
                project(t)
                turn(t - 1)
            pe.wait_ge(s_zs, NT)
            pe.wait_ge(s_wq, 16)
            for t in range(NT):
                project_gqa(pe, 0, t)
            turn(NT - 1)
            turn(NT)

        @block.scalar
        def _(act):
            def take(t):
                act.wait_ge(s_z, t + 1)
                if t >= 2:
                    act.wait_ge(s_zn, t - 1)
                act.activation(zs[t % 2], psum[:, 1024 * (t % 2):1024 * (t % 2) + ZN], ACT.Copy).then_inc(s_zs, 1)
                act.wait_ge(s_zs, t + 1)
                act.activation(vA[:, key_col(t) // P, :, :].rearrange("p g d -> p (g d)"),
                               zs[t % 2][:, Z_V:Z_V + 256], ACT.Copy)
                act.activation(zq[t % 2], zs[t % 2], ACT.Square).then_inc(s_zq, 1)

            def untangle(t):
                act.wait_ge(s_zT, t + 1)
                c = key_col(t) if t < NT else P
                act.activation(ckvT[:, c:c + P], bank(5)[:, 0:P], ACT.Copy)
                act.activation(krT[:, c:c + P], bank(5)[0:ROPE, P:2 * P], ACT.Copy).then_inc(s_zeA, 1)

            take(0)
            take(1)
            for t in range(NT):
                untangle(t)
                if t + 2 < NT:
                    take(t + 2)
            untangle(NT)

        @block.gpsimd
        def _(pool):
            for t in range(NT):
                pool.wait_ge(s_zm, t + 1)
                pool.tensor_scalar(ss, ss, EPS, None, ALU.add).then_inc(s_p2, 1)
                pool.wait_ge(s_p2, t + 1)
                pool.tensor_tensor(rstd, ss, nhalf[:, 0:5], ALU.pow).then_inc(s_zr, 1)

        @block.vector
        def _(dve):
            chain = Chain(dve, s_v2)
            dve.wait_ge(s_gain, 16 * 12)
            dve.wait_ge(s_tabs, 16 * 4)

            def over(g, w):
                return g.unsqueeze(1).to_broadcast([P, NT, w])

            for q, k, raw, g, w, scale in ((CqA, CkA, CqA, gA, HD, SCALE_A), (SqA, SkA, SqA, gA, HD, SCALE_A),
                                           (CqB, CkB, CqB, gB, ROPE, SCALE_B), (SqB, SkB, SqB, gB, ROPE, SCALE_B)):
                swapped = int(raw is SqA or raw is SqB)
                chain(dve.tensor_tensor(k, raw, over(g[:, 2 + swapped, :], w), ALU.mult))
                chain(dve.tensor_tensor(q, raw, over(g[:, swapped, :], w), ALU.mult))
                chain(dve.tensor_scalar(q, q, scale, None, ALU.mult))
            dve.wait_ge(s_cache, 16 * 5)

            def norms(t):
                z, q, n = zs[t % 2], zq[t % 2], zn[t % 2]
                dve.wait_ge(s_zq, t + 1)
                if t >= 1:
                    dve.wait_ge(s_zr, t)
                for a, b, c, w in ((0, 2, Z_K, HD), (2, 3, Z_CQ, QL), (3, 4, Z_CKV, KVL), (4, 5, Z_KR, ROPE)):
                    chain(dve.tensor_reduce(ss[:, a:b], q[:, c:c + (b - a) * w].rearrange("p (a w) -> p a w", w=w),
                                            AX_X, ALU.add))
                dve.tensor_tensor(ss, ss, invlen, ALU.mult).then_inc(s_zm, 1)
                dve.wait_ge(s_zr, t + 1)
                if t >= 2:
                    dve.wait_ge(s_zT, t - 1)
                if t == 2:
                    dve.wait_ge(s_out, 16 * 6)
                k3 = n[:, 0:256].rearrange("p (g d) -> p g d", g=KVA)
                z3 = z[:, 0:256].rearrange("p (g d) -> p g d", g=KVA)
                q3 = q[:, 0:256].rearrange("p (g d) -> p g d", g=KVA)
                r3 = rot.rearrange("p (g d) -> p g d", g=KVA)
                chain(dve.tensor_tensor(q3, z3, rstd[:, 0:2].unsqueeze(2).to_broadcast([P, KVA, HD]), ALU.mult))
                h = HD // 2
                for a, b in ((0, h), (h, 0)):
                    chain(dve.tensor_tensor(r3[:, :, a:a + h], q3[:, :, b:b + h],
                                            SkA[:, t, a:a + h].unsqueeze(1).to_broadcast([P, KVA, h]), ALU.mult))
                chain(dve.tensor_tensor(k3, q3, CkA[:, t, :].unsqueeze(1).to_broadcast([P, KVA, HD]), ALU.mult))
                chain(dve.tensor_tensor(k3, k3, r3, ALU.add))
                chain(dve.tensor_scalar(n[:, Z_CQ:Z_CQ + QL], z[:, Z_CQ:Z_CQ + QL], rstd[:, 2:3], None, ALU.mult))
                chain(dve.scalar_tensor_tensor(out=n[:, Z_CKV:Z_CKV + KVL], in0=z[:, Z_CKV:Z_CKV + KVL],
                                               scalar=rstd[:, 3:4], in1=kgB, op0=ALU.mult, op1=ALU.mult))
                zr, nr, qr = z[:, Z_KR:], n[:, Z_KR:], q[:, Z_KR:]
                h = ROPE // 2
                for a, b in ((0, h), (h, 0)):
                    chain(dve.scalar_tensor_tensor(out=qr[:, a:a + h], in0=zr[:, b:b + h], scalar=rstd[:, 4:5],
                                                   in1=SkB[:, t, a:a + h], op0=ALU.mult, op1=ALU.mult))
                chain(dve.scalar_tensor_tensor(out=nr[:, 0:ROPE], in0=zr[:, 0:ROPE], scalar=rstd[:, 4:5],
                                               in1=CkB[:, t, :], op0=ALU.mult, op1=ALU.mult))
                dve.tensor_tensor(nr[:, 0:ROPE], nr[:, 0:ROPE], qr[:, 0:ROPE], ALU.add).then_inc(s_zn, 1)

            def untangle(t):
                dve.wait_ge(s_zT, t + 1)
                c = key_col(t) if t < NT else P
                ins = dve.tensor_copy(kTA[:, :, c:c + P], bank(4)[:, 0:256].rearrange("p (g d) -> p g d", g=KVA))
                if t < NT:
                    for j in range(2):
                        ins = dve.tensor_scalar(cqT[:, j, t * P:(t + 1) * P], bank(4)[:, (2 + j) * P:(3 + j) * P],
                                                cols[:, 80 + j:81 + j], None, ALU.mult)
                ins.then_inc(s_zeV, 1)

            norms(0)
            norms(1)
            for t in range(NT):
                untangle(t)
                if t + 2 < NT:
                    norms(t + 2)
            untangle(NT)

    hz = mem.at(M_SC, 960)
    hq = mem.at(M_SC + 960, 960)
    hr = mem.at(M_SC + 1920, 640)
    qTh = mem.at(M_SC + 2560, TOK)
    qrT = mem.at(M_SC + 3200, TOK, rows=ROPE)
    pr = [mem.at(M_SC + 3840 + 640 * b, 640) for b in range(2)]
    pT = mem.at(M_SC + 5120, 5, LAT)
    pTc = mem.at(M_SC + 7680, P)
    vh = mem.at(M_SC + 7808, NK, VD)
    nmax = small[:, 48:53]
    rsum = small[:, 56:61]
    rinv = small[:, 64:69]
    hss = small[:, 72:82]
    hrs = small[:, 88:98]
    MODS = 4
    wmh = mem.at(M_OB + KT * HA * HD, KT, 512)
    modrow = mem.at(M_R + 11264, MODS * D, rows=2)
    gainrow = mem.at(M_R + 11264 + MODS * D, D, rows=2)
    pM = bank(7)[0:2, :]
    PROJECT = ((0, 1), (2, 3), (4,), (), ())
    s_mrow = sem("s_mrow")
    KEY_TILES = [2, 3, 4, 5, 1]

    wraw = [wkvb.rearrange("p (q k n) -> p q k n", q=2, k=KT),
            mem.at(M_TB + 4096, 2048).rearrange("p (q k n) -> p q k n", q=2, k=KT)]
    w_oa_v = I["w_oa"][0].rearrange("(k p) n -> p k n", p=P)
    w_ob_v = I["w_ob"][0].rearrange("(k p) n -> p k n", p=P)
    s_mwf = sem("s_mwf")

    def attend(kind, oT, kT_of, v_of):
        mla = kind == "b"
        names = ("S", "nm", "exp", "ri", "pn", "T", "TeV", "TeA", "Z", "sq", "ss", "ms", "rs", "qn", "rot", "q",
                 "QT", "qe", "O", "Oe", "C", "Ce", "vh", "qr") + (() if mla else ("wm", "br", "M", "Me", "mr"))
        s = {n: nc.alloc_semaphore(name=f"s_{kind}_{n}") for n in names}
        nh = HA
        NS = 2 if mla else 1

        with nc.Block() as block:
            if mla:
                @block.sync
                def _(sp):
                    for q, w, c in ((0, w_in_v, C_GA), (1, w_oa_v, 0)):
                        sp.dma_start(wraw[0][:, q], w[:, :, c:c + P]).then_inc(s_mwf, 16)
            else:
                @block.sync
                def _(sp):
                    sp.dma_start(modrow, I["b_mod"][:, 2 * D:6 * D].to_broadcast([2, MODS * D])).then_inc(s["br"], 16)
                    sp.dma_start(gainrow, I["norm2_g"].to_broadcast([2, D])).then_inc(s["br"], 16)
                    sp.dma_start(wmh, w_mod_v[:, :, 2 * D:2 * D + 512]).then_inc(s["wm"], 16)
                    with sp.Fori(1, nh) as h:
                        sp.wait_ge(s["M"], h)
                        sp.dma_start(wmh, w_mod_v[:, :, bass.ds(h * 512 + 2 * D, 512)]).then_inc(s["wm"], 16)
                    sp.wait_ge(s["mr"], 1)
                    sp.dma_start(S["mod_rows"].rearrange("(v y) d -> y v d", y=2),
                                 modrow.rearrange("y (v d) -> y v d", v=MODS)).then_inc(s_mrow, 16)
                    sp.wait_ge(s_mrow, 16)

            @block.tensor
            def _(pe):
                def project(h, t):
                    mm = (project_mla if mla else project_gqa)(pe, h, t)
                    if t == NT - 1:
                        mm.then_inc(s["Z"], 1)

                def turn_q(h):
                    pe.wait_ge(s["q"], h + 1)
                    for t in range(NT):
                        tr = pe.transpose(pZ[:, t * P:(t + 1) * P], hq[:, t * P:(t + 1) * P], ident[:, :])
                    tr.then_inc(s["QT"], 1)

                def turn_r(h):
                    pe.wait_ge(s["qe"], 2 * h + 1)
                    pe.matmul(pZ[0:ROPE, 0:P], hq[:, 640:640 + ROPE], ident[:, :], start=True, stop=True)
                    for t in range(1, NT):
                        tr = pe.transpose(pZ[0:ROPE, t * P:(t + 1) * P],
                                          hq[:, 640 + t * ROPE:640 + (t + 1) * ROPE], ident[:, :])
                    tr.then_inc(s["qr"], 1)

                def scores(h, t):
                    if t == 0:
                        pe.wait_ge(s["qe"], NS * h + NS)
                    else:
                        pe.wait_ge(s["exp"], NT * h + t)
                    kT = kT_of(h)
                    q = qTh[:, t * P:(t + 1) * P]
                    r = qrT[:, t * P:(t + 1) * P]
                    parts = [(0, 0, P)] if t == 0 else [(0, 2 * P, LAT), (LAT, P, P)]
                    for o, c, w in parts:
                        mm = pe.matmul(pS[:, o:o + w], q, kT(c, w), start=True, stop=not mla)
                        if mla:
                            mm = pe.matmul(pS[:, o:o + w], r, krT[:, c:c + w], start=False, stop=True)
                    mm.then_inc(s["S"], 1)

                def turn_p(h, t):
                    pe.wait_ge(s["pn"], NT * h + t + 1)
                    if t >= 1:
                        pe.wait_ge(s["TeV"], NT * h + t)
                        if t >= 2:
                            pe.wait_ge(s["TeA"], (NT - 1) * h + t - 1)
                    for j in range(1 if t == 0 else 5):
                        tr = pe.transpose(pT_ps[:, j * P:(j + 1) * P], pr[t % 2][:, j * P:(j + 1) * P], ident[:, :])
                    tr.then_inc(s["T"], 1)

                def values(h, t):
                    pe.wait_ge(s["TeV"], NT * h + t + 1)
                    if t == 0:
                        pe.wait_ge(s["vh"], h + 1)
                        if not mla:
                            pe.wait_ge(s["Me"], h + 1)
                        pe.matmul(pC, vh[:, 0, :], pTc, start=True, stop=True).then_inc(s["C"], 1)
                        return
                    pe.wait_ge(s["TeA"], (NT - 1) * h + t)
                    if t == 1:
                        pe.wait_ge(s["Oe"], h + 1)
                    for j, kt in enumerate(KEY_TILES):
                        mm = pe.matmul(pO[:, (t - 1) * P:t * P], vh[:, kt, :], pT[:, j, (t - 1) * P:t * P],
                                       start=(j == 0), stop=(j == 4))
                    if t == NT - 1:
                        mm.then_inc(s["O"], 1)

                def modulation(h, part):
                    if part == 0:
                        pe.wait_ge(s["wm"], 16 * (h + 1))
                        pe.wait_ge(s["Ce"], h + 1)
                    for k in range(4 * part, 4 * part + 4):
                        mm = pe.matmul(pM, cols[:, k:k + 9:8], wmh[:, k, :], start=(k == 0), stop=(k == KT - 1))
                    if part == 1:
                        mm.then_inc(s["M"], 1)

                def head(h, more):
                    for t in range(NT):
                        scores(h, t)
                        if more:
                            for p in PROJECT[t]:
                                project(h + 1, p)
                        if t >= 1:
                            turn_p(h, t - 1)
                        if t >= 2:
                            values(h, t - 2)
                        if t >= 3 and not mla:
                            modulation(h, t - 3)
                    if more:
                        turn_q(h + 1)
                    turn_p(h, NT - 1)
                    values(h, NT - 2)
                    if more and mla:
                        turn_r(h + 1)
                    values(h, NT - 1)

                pe.sem_inc(s["Z"], 1)
                turn_q(0)
                if mla:
                    turn_r(0)
                with pe.Fori(0, nh - 1) as h:
                    head(h, True)
                head(nh - 1, False)

            @block.scalar
            def _(act):
                def squares(h):
                    act.wait_ge(s["Z"], h + 1)
                    n = 960 if mla else 640
                    act.activation(hz[:, 0:n], pZ[:, 0:n], ACT.Square).then_inc(s["sq"], 1)

                def take_q(h):
                    act.wait_ge(s["QT"], h + 1)
                    if mla:
                        act.activation(qTh, pZ[:, 0:TOK], ACT.Copy, scale=qk_gain).then_inc(s["qe"], 1)
                    else:
                        act.activation(qTh, pZ[:, 0:TOK], ACT.Copy).then_inc(s["qe"], 1)

                def take_r(h):
                    act.wait_ge(s["qr"], h + 1)
                    act.activation(qrT, pZ[0:ROPE, 0:TOK], ACT.Copy).then_inc(s["qe"], 1)

                def take_p(h, t):
                    act.wait_ge(s["T"], NT * h + t + 1)
                    act.activation(pT[:, 4, (t - 1) * P:t * P], pT_ps[:, 512:640], ACT.Copy).then_inc(s["TeA"], 1)

                def head(h, more):
                    for t in range(NT):
                        w = P if t == 0 else 640
                        if t == 3:
                            act.wait_ge(s["C"], h + 1)
                            act.activation(oT[:, bass.ds(h, 1), 0:P].rearrange("p a t -> p (a t)"), pC, ACT.Copy)\
                               .then_inc(s["Ce"], 1)
                        act.wait_ge(s["nm"], NT * h + t + 1)
                        if t >= 2:
                            act.wait_ge(s["T"], NT * h + t - 1)
                        act.activation(pr[t % 2][:, 0:w], pS[:, 0:w], ACT.Exp, bias=nmax[:, t:t + 1],
                                       accum_out=rsum[:, t:t + 1]).then_inc(s["exp"], 1)
                        if t >= 2:
                            take_p(h, t - 1)
                        if t == 2 and more:
                            squares(h + 1)
                    if more:
                        take_q(h + 1)
                    take_p(h, NT - 1)
                    if more and mla:
                        take_r(h + 1)
                    act.wait_ge(s["O"], h + 1)
                    act.activation(oT[:, bass.ds(h, 1), P:TOK].rearrange("p a t -> p (a t)"), pO,
                                   ACT.Copy).then_inc(s["Oe"], 1)

                act.sem_inc(s["Oe"], 1)
                squares(0)
                take_q(0)
                if mla:
                    take_r(0)
                with act.Fori(0, nh - 1) as h:
                    head(h, True)
                head(nh - 1, False)

            @block.gpsimd
            def _(pool):
                ns = NT * NS

                def prep(h):
                    pool.wait_ge(s["ms"], h + 1)
                    pool.tensor_tensor(hrs[:, 0:ns], hss[:, 0:ns], nhalf[:, 0:ns], ALU.pow).then_inc(s["rs"], 1)

                def copy_v(h):
                    pool.tensor_copy(vh, v_of(h)).then_inc(s["vh"], 1)

                prep(0)
                copy_v(0)
                with pool.Fori(0, nh - 1) as h:
                    prep(h + 1)
                    pool.wait_ge(s["O"], h + 1)
                    copy_v(h + 1)

            @block.vector
            def _(dve):
                w = ROPE if mla else HD
                o = 640 if mla else 0
                z3 = pZ[:, o:o + NT * w].rearrange("p (t d) -> p t d", t=NT)
                n3 = hz[:, o:o + NT * w].rearrange("p (t d) -> p t d", t=NT)
                q3 = hq[:, o:o + NT * w].rearrange("p (t d) -> p t d", t=NT)
                r3 = hr[:, 0:NT * w].rearrange("p (t d) -> p t d", t=NT)
                C, Sn = (CqB, SqB) if mla else (CqA, SqA)

                def sums(h):
                    dve.wait_ge(s["sq"], h + 1)
                    a = hz[:, 0:640].rearrange("p (t d) -> p t d", t=NT)
                    ins = dve.tensor_reduce(hss[:, 0:NT], a, AX_X, ALU.add)
                    if mla:
                        b = hz[:, 640:960].rearrange("p (t d) -> p t d", t=NT)
                        ins.then_inc(s["ss"], 1)
                        dve.tensor_reduce(hss[:, NT:2 * NT], b, AX_X, ALU.add).then_inc(s["ss"], 1)
                        dve.wait_ge(s["ss"], 3 * h + 2)
                        dve.tensor_scalar(hss[:, 0:NT], hss[:, 0:NT], 1.0 / HD, EPS, ALU.mult, ALU.add)\
                           .then_inc(s["ss"], 1)
                        dve.tensor_scalar(hss[:, NT:2 * NT], hss[:, NT:2 * NT], 1.0 / ROPE, EPS, ALU.mult, ALU.add)\
                           .then_inc(s["ms"], 1)
                    else:
                        ins.then_inc(s["ss"], 1)
                        dve.wait_ge(s["ss"], h + 1)
                        dve.tensor_scalar(hss[:, 0:NT], hss[:, 0:NT], 1.0 / HD, EPS, ALU.mult, ALU.add)\
                           .then_inc(s["ms"], 1)

                def scale(h):
                    dve.wait_ge(s["rs"], h + 1)
                    rs = hrs[:, NT * (NS - 1):NT * NS].unsqueeze(2).to_broadcast([P, NT, w])
                    dve.tensor_tensor(n3, z3, rs, ALU.mult).then_inc(s["qn"], 1)
                    if mla:
                        dve.tensor_tensor(hq[:, 0:640].rearrange("p (t d) -> p t d", t=NT),
                                          pZ[:, 0:640].rearrange("p (t d) -> p t d", t=NT),
                                          hrs[:, 0:NT].unsqueeze(2).to_broadcast([P, NT, NOPE]), ALU.mult)

                def rotate(h, part):
                    if part == 0:
                        dve.wait_ge(s["qn"], h + 1)
                        x = w // 2
                        dve.tensor_tensor(r3[:, :, 0:x], n3[:, :, x:w], Sn[:, :, 0:x], ALU.mult).then_inc(s["rot"], 1)
                        dve.tensor_tensor(r3[:, :, x:w], n3[:, :, 0:x], Sn[:, :, x:w], ALU.mult).then_inc(s["rot"], 1)
                    else:
                        dve.tensor_tensor(q3, n3, C, ALU.mult).then_inc(s["rot"], 1)
                        dve.wait_ge(s["rot"], 3 * h + 3)
                        dve.tensor_tensor(q3, q3, r3, ALU.add).then_inc(s["q"], 1)

                def maximum(h, t):
                    w = P if t == 0 else 640
                    dve.wait_ge(s["S"], NT * h + t + 1)
                    dve.tensor_reduce(nmax[:, t:t + 1], pS[:, 0:w], AX_X, ALU.max, negate=True).then_inc(s["nm"], 1)

                def normalise(h, t):
                    w = P if t == 0 else 640
                    dve.wait_ge(s["exp"], NT * h + t + 1)
                    dve.reciprocal(rinv[:, t:t + 1], rsum[:, t:t + 1]).then_inc(s["ri"], 1)
                    dve.wait_ge(s["ri"], NT * h + t + 1)
                    dve.tensor_scalar(pr[t % 2][:, 0:w], pr[t % 2][:, 0:w], rinv[:, t:t + 1], None, ALU.mult)\
                       .then_inc(s["pn"], 1)

                def take_p(h, t):
                    dve.wait_ge(s["T"], NT * h + t + 1)
                    if t == 0:
                        dve.tensor_copy(pTc, pT_ps[:, 0:P]).then_inc(s["TeV"], 1)
                    else:
                        dve.tensor_copy(pT[:, 0:4, (t - 1) * P:t * P],
                                        pT_ps[:, 0:512].rearrange("p (j q) -> p j q", j=4)).then_inc(s["TeV"], 1)

                def take_mod(h):
                    dve.wait_ge(s["M"], h + 1)
                    row = modrow[:, bass.ds(h * 512, 512)]
                    dve.tensor_tensor(row, row, pM, ALU.add).then_inc(s["Me"], 1)

                def head(h, more):
                    for t in range(NT):
                        maximum(h, t)
                        if t >= 1:
                            take_p(h, t - 1)
                        if t == 4 and more:
                            rotate(h + 1, 1)
                        normalise(h, t)
                        if t == 2 and more:
                            sums(h + 1)
                        if t == 3 and more:
                            scale(h + 1)
                            rotate(h + 1, 0)
                    take_p(h, NT - 1)
                    if not mla:
                        take_mod(h)

                sums(0)
                scale(0)
                rotate(0, 0)
                rotate(0, 1)
                if not mla:
                    dve.sem_inc(s["Me"], 1)
                    dve.wait_ge(s["br"], 32)
                with dve.Fori(0, nh - 1) as h:
                    head(h, True)
                head(nh - 1, False)
                if not mla:
                    dve.wait_ge(s["Me"], nh + 1)
                    row = modrow[:, 2 * D:3 * D]
                    dve.scalar_tensor_tensor(out=row, in0=row, scalar=1.0, in1=gainrow, op0=ALU.add, op1=ALU.mult)\
                       .then_inc(s["mr"], 1)

        nc.clear_and_free_semaphores(list(s.values()))
        nc.all_engine_barrier()

    def kT_gqa(h):
        return lambda c, w: kTA[:, h // (HA // KVA), c:c + w] if isinstance(h, int) else \
            kTA[:, bass.ds(h // (HA // KVA), 1), c:c + w].rearrange("p a k -> p (a k)")

    def v_gqa(h):
        if isinstance(h, int):
            return vA[:, :, h // (HA // KVA), :]
        return vA[:, :, bass.ds(h // (HA // KVA), 1), :].rearrange("p k a d -> p k (a d)")

    attend("a", oA, kT_gqa, v_gqa)

    kB = mem.at(M_R, HB, KEYS)
    vB = mem.at(M_R + 6144, NK, HB, VD)
    kz = [mem.at(M_SC + 2048 + KEYS * b, KEYS) for b in range(2)]
    kn = [mem.at(M_SC + 2048 + KEYS * (2 + b), KEYS) for b in range(2)]
    kss = [small[:, 100 + 6 * b:106 + 6 * b] for b in range(2)]
    krs = [small[:, 112 + 6 * b:118 + 6 * b] for b in range(2)]
    names = ("kv", "sq", "ss", "ms", "rs", "kn", "v", "T", "e")
    sk = {n: sem(f"s_k_{n}") for n in names}
    KV = NOPE + VD
    pKV = [psum[:, 1536 * b:1536 * (b + 1)].rearrange("p (k c) -> p k c", c=KV) for b in range(2)]
    pKT = psum[:, 3072:3072 + KEYS]
    with nc.Block() as block:
        @block.sync
        def _(sp):
            sp.dma_start(wqb, I["w_qb"][0].rearrange("(k p) n -> p k n", p=P)).then_inc(s_wqb, 16)

        @block.tensor
        def _(pe):
            pe.wait_ge(s_wkvb, 16)

            def expand(h, b, first=False):
                if not first:
                    pe.wait_ge(sk["v"], h)
                for kt in range(NK):
                    mm = pe.matmul(pKV[b][:, kt, :], ckvT[:, kt * P:(kt + 1) * P], wkvb[:, bass.ds(h * KV, KV)],
                                   start=True, stop=True)
                mm.then_inc(sk["kv"], 1)

            def turn(h, b):
                pe.wait_ge(sk["kn"], h + 1)
                pe.wait_ge(sk["e"], h + 1)
                for kt in range(NK):
                    tr = pe.transpose(pKT[:, kt * P:(kt + 1) * P], kn[b][:, kt * P:(kt + 1) * P], ident[:, :])
                tr.then_inc(sk["T"], 1)

            expand(0, 0, True)
            with pe.Fori(0, HB // 2 - 1) as i:
                for b in range(2):
                    expand(2 * i + b + 1, 1 - b)
                    turn(2 * i + b, b)
            expand(HB - 1, 1)
            turn(HB - 2, 0)
            pe.wait_ge(sk["v"], HB)
            pe.wait_ge(s_wqb, 16)
            for t in range(NT):
                project_mla(pe, 0, t)
            turn(HB - 1, 1)

        @block.scalar
        def _(act):
            def squares(h, b):
                act.wait_ge(sk["kv"], h + 1)
                act.activation(kz[b].rearrange("p (k d) -> p k d", k=NK), pKV[b][:, :, 0:NOPE], ACT.Square)\
                   .then_inc(sk["sq"], 1)

            def take_v(h, b):
                act.wait_ge(sk["kn"], h + 1)
                act.activation(vB[:, :, bass.ds(h, 1), :].rearrange("p k a d -> p k (a d)"), pKV[b][:, :, NOPE:KV],
                               ACT.Copy).then_inc(sk["v"], 1)

            act.sem_inc(sk["v"], 1)
            squares(0, 0)
            with act.Fori(0, HB // 2 - 1) as i:
                for b in range(2):
                    squares(2 * i + b + 1, 1 - b)
                    take_v(2 * i + b, b)
            squares(HB - 1, 1)
            take_v(HB - 2, 0)
            take_v(HB - 1, 1)

        @block.gpsimd
        def _(pool):
            with pool.Fori(0, HB // 2) as i:
                for b in range(2):
                    pool.wait_ge(sk["ms"], 2 * i + b + 1)
                    pool.tensor_tensor(krs[b], kss[b], nhalf[:, 0:NK], ALU.pow).then_inc(sk["rs"], 1)

        @block.vector
        def _(dve):
            def sums(h, b):
                dve.wait_ge(sk["sq"], h + 1)
                dve.tensor_reduce(kss[b], kz[b].rearrange("p (k d) -> p k d", k=NK), AX_X, ALU.add)\
                   .then_inc(sk["ss"], 1)
                dve.wait_ge(sk["ss"], h + 1)
                dve.tensor_scalar(kss[b], kss[b], 1.0 / NOPE, EPS, ALU.mult, ALU.add).then_inc(sk["ms"], 1)

            def norm(h, b):
                dve.wait_ge(sk["rs"], h + 1)
                dve.tensor_tensor(kn[b].rearrange("p (k d) -> p k d", k=NK), pKV[b][:, :, 0:NOPE],
                                  krs[b].unsqueeze(2).to_broadcast([P, NK, NOPE]), ALU.mult).then_inc(sk["kn"], 1)

            def take(h):
                dve.wait_ge(sk["T"], h + 1)
                dve.tensor_copy(kB[:, bass.ds(h, 1), :].rearrange("p a k -> p (a k)"), pKT).then_inc(sk["e"], 1)

            dve.sem_inc(sk["e"], 1)
            sums(0, 0)
            norm(0, 0)
            sums(1, 1)
            with dve.Fori(0, HB // 2 - 1) as i:
                for b in (1, 0):
                    h = 2 * i + 2 - b
                    norm(h, b)
                    take(h - 1)
                    sums(h + 1, 1 - b)
            norm(HB - 1, 1)
            take(HB - 2)
            take(HB - 1)

    attend("b", oB,
           lambda h: (lambda c, w: kB[:, bass.ds(h, 1), c:c + w].rearrange("p a k -> p (a k)")),
           lambda h: vB[:, :, bass.ds(h, 1), :].rearrange("p k a d -> p k (a d)"))

    HALF = TOK // 2
    def parts(name, byte):
        return nc.alloc_sbuf_tensor_at(name, [P, KT, TOK], F32R, offset=byte)

    def wparts(name, byte):
        return nc.alloc_sbuf_tensor_at(name, [P, 2, KT, P], F32R, offset=byte)


    hHi, hLo = parts("h_hi", mem_at + 4 * M_R), parts("h_lo", mem_at + 4 * M_H)
    oAHi, oALo = parts("oa_hi", mem_at + 4 * (M_R + 5120)), parts("oa_lo", mem_at + 4 * M_OA)
    oBHi, oBLo = parts("ob_hi", mem_at + 4 * M_OA), parts("ob_lo", mem_at + 4 * M_OB)
    mT = mem.at(M_R + 10240, KT, TOK)
    whi = [wparts(f"w_hi{b}", mem_at + 4 * (M_TB + 2048 * b)) for b in range(2)]
    wlo = [wparts("w_lo0", wkvb_at), wparts("w_lo1", mem_at + 4 * (M_TB + 4096))]
    wout = mem.at(M_SC, KT, D)
    sig = [mem.at(M_TB + 6144 + HALF * f, HALF) for f in range(2)]
    part = [mem.at(M_TB + 6784 + HALF * f, HALF) for f in range(2)]
    s_mw = [sem(f"s_mw{b}") for b in range(2)]
    s_wout = sem("s_wout")
    names = ("wh", "wl", "xh", "xl", "g", "mm", "sig", "x", "m")
    sg = {n: sem(f"s_g_{n}") for n in names}

    with nc.Block() as block:
        def over_chunks(eng, do):
            for phase in range(2):
                do(phase, 8 * phase, 0, 0)
                do(phase, 8 * phase + 1, 1, 1)
                with eng.Fori(1, KT // 2) as i:
                    for b in range(2):
                        do(phase, 2 * i + 8 * phase + b, 2 * i + b, b)

        @block.sync
        def _(sp):
            def load(phase, c, j, b):
                if isinstance(c, int) and c == 0:
                    return
                if not (isinstance(c, int) and c == 1):
                    sp.wait_ge(sg["mm"], c - 1)
                for q, (w, o) in enumerate((((w_in_v, C_GA), (w_oa_v, 0)), ((w_in_v, C_GB), (w_ob_v, 0)))[phase]):
                    sp.dma_start(wraw[b][:, q], w[:, :, bass.ds(j * P + o, P)]).then_inc(s_mw[b], 16)
                if isinstance(c, int) and c == 1:
                    sp.dma_start(wout, I["w_out"][0].rearrange("(k p) n -> p k n", p=P)).then_inc(s_wout, 16)

            over_chunks(sp, load)

        @block.tensor
        def _(pe):
            def chunk(phase, c, j, b):
                if not (isinstance(c, int) and c < 2):
                    pe.wait_ge(sg["m"], 2 * c - 2)
                for q, (hi, lo) in enumerate((((hHi, hLo), (oAHi, oALo)), ((hHi, hLo), (oBHi, oBLo)))[phase]):
                    pe.wait_ge(sg["wl"], 2 * c + q + 1)
                    for f in range(2):
                        cols_ = slice(f * HALF, (f + 1) * HALF)
                        out = bank(4 * b + 2 * q + f)[:, 0:HALF]
                        for k in range(KT):
                            if isinstance(c, int) and j == 0 and f == 0 and (phase == 0 or q == 1):
                                pe.wait_ge(sg["xl"], 8 * (q + phase) + k + 1)
                            pe.matmul(out, whi[b][:, q, k, :], hi[:, k, cols_], start=(k == 0), stop=False)
                            pe.matmul(out, whi[b][:, q, k, :], lo[:, k, cols_], start=False, stop=False)
                            mm = pe.matmul(out, wlo[b][:, q, k, :], hi[:, k, cols_], start=False,
                                           stop=(k == KT - 1))
                    mm.then_inc(sg["g" if q == 0 else "mm"], 1)

            over_chunks(pe, chunk)

        @block.scalar
        def _(act):
            def weights_hi(c, b):
                if isinstance(c, int) and c == 0:
                    act.wait_ge(s_mwf, 32)
                elif b == 0:
                    act.wait_ge(s_mw[0], 16 * c)
                else:
                    act.wait_ge(s_mw[1], 16 * (c + 1))
                for q in range(2):
                    act.activation(whi[b][:, q, :, :], wraw[b][:, q], ACT.Copy).then_inc(sg["wh"], 1)

            def rows_hi(hi, raw):
                for k in range(KT):
                    act.activation(hi[:, k, :], raw[:, k, :], ACT.Copy).then_inc(sg["xh"], 1)

            def do(phase, c, j, b, last=False):
                if isinstance(c, int) and c == 0:
                    weights_hi(0, 0)
                    rows_hi(hHi, hT)
                    rows_hi(oAHi, oA)
                if isinstance(c, int) and c == 8:
                    act.wait_ge(sg["mm"], 8)
                    rows_hi(oBHi, oB)
                if not last:
                    weights_hi(c + 1, 1 - b)
                act.wait_ge(sg["g"], c + 1)
                if not (isinstance(c, int) and c == 0):
                    act.wait_ge(sg["m"], 2 * c)
                for f in range(2):
                    ins = act.activation(sig[f], bank(4 * b + f)[:, 0:HALF], ACT.Sigmoid)
                ins.then_inc(sg["sig"], 1)

            for phase in range(2):
                do(phase, 8 * phase, 0, 0)
                do(phase, 8 * phase + 1, 1, 1)
                with act.Fori(1, KT // 2 - phase) as i:
                    for b in range(2):
                        do(phase, 2 * i + 8 * phase + b, 2 * i + b, b)
            do(1, 14, 6, 0)
            do(1, 15, 7, 1, last=True)

        @block.gpsimd
        def _(pool):
            def weights_lo(phase, c, j, b):
                for q in range(2):
                    pool.wait_ge(sg["wh"], 2 * c + q + 1)
                    pool.tensor_tensor(wlo[b][:, q, :, :], wraw[b][:, q], whi[b][:, q, :, :].bitcast(F32),
                                       ALU.subtract).then_inc(sg["wl"], 1)

            over_chunks(pool, weights_lo)

        @block.vector
        def _(dve):
            def rows_lo(n, hi, lo, raw):
                for k in range(KT):
                    dve.wait_ge(sg["xh"], 8 * n + k + 1)
                    dve.tensor_tensor(lo[:, k, :], raw[:, k, :], hi[:, k, :].bitcast(F32), ALU.subtract).then_inc(sg["xl"], 1)

            def combine(phase, c, j, b):
                if isinstance(c, int) and c == 0:
                    rows_lo(0, hHi, hLo, hT)
                    rows_lo(1, oAHi, oALo, oA)
                if isinstance(c, int) and c == 8:
                    rows_lo(2, oBHi, oBLo, oB)
                dve.wait_ge(sg["sig"], c + 1)
                dve.wait_ge(sg["mm"], c + 1)
                for f in range(2):
                    m = mT[:, bass.ds(j, 1), f * HALF:(f + 1) * HALF].rearrange("p a t -> p (a t)")
                    y = bank(4 * b + 2 + f)[:, 0:HALF]
                    if phase == 0:
                        dve.tensor_tensor(m, sig[f], y, ALU.mult).then_inc(sg["m"], 1)
                    else:
                        dve.tensor_tensor(part[f], sig[f], y, ALU.mult).then_inc(sg["x"], 1)
                if phase == 1:
                    dve.wait_ge(sg["x"], 2 * c - 14)
                    for f in range(2):
                        m = mT[:, bass.ds(j, 1), f * HALF:(f + 1) * HALF].rearrange("p a t -> p (a t)")
                        dve.tensor_tensor(m, m, part[f], ALU.add).then_inc(sg["m"], 1)

            over_chunks(dve, combine)

    modb = mem.at(M_OA, 8, D)
    h2T = hT
    x1 = mem.at(M_TB, NT, D)
    xres = [mem.at(M_TB + 5120 + 1024 * b, D) for b in range(2)]
    h2 = mem.at(M_TB + 7168, D)
    h2p = mem.at(M_TB + 8192, D)
    wr = mem.at(M_OB + 3072, KT, NE)
    rbias = mem.at(M_SC + 8392, NE)
    sc = mem.at(M_OB + 3584, NT, NE)
    RS1, RS2 = small[:, 0:1], small[:, 1:2]
    sel = mem.at(M_OB + 3904, NT, NE)
    wn = mem.at(M_OB + 4224, NT, NE)
    rsc = mem.at(M_OB + 4544, 576)
    bia, msk, rep, gA64, gB64 = (rsc[:, 64 * n:64 * n + 64] for n in range(5))
    gm8 = rsc[:, 320:384].rearrange("p (a b) -> p a b", b=8)
    gs, rank, m8, wsum = rsc[:, 384:392], rsc[:, 392:400], rsc[:, 400:408], rsc[:, 408:409]
    cst = sb("cst", [P, 128 + 128 + 64 + 64 + 1 + 64 + 64])
    tri, ones = cst[:, 0:128], cst[:, 128:256]
    enum, gtri, pnum = cst[:, 256:320], cst[:, 320:384], cst[:, 384:385]
    triX, triI = cst[0:NE, 385:449], cst[0:NE, 449:513]
    recs = mem.at(M_SC + 8192, NT * TOPK, 4).bitcast(I32)
    kidx = mem.at(M_SC + 8352, NT * TOPK).bitcast(I32)
    tabs = mem.at(M_TB + 9288, NBLK + RING, 4).bitcast(I32)
    w13 = [mem.at(M_R + 6144 * ((u + 1) % RING), 2, KT, FE) for u in range(RING)]
    w2 = [mem.at(M_R + 6144 * ((u + 1) % RING) + 4096, 2, D) for u in range(RING)]
    SH = RING - 1
    s_cst = sem("s_cst")
    s_rec = sem("s_rec")
    s_tin = sem("s_tin")
    s_tz = sem("s_tz")
    s_shw = sem("s_shw")
    s_sel = sem("s_sel")
    s_rsel = sem("s_rsel")
    s_modb = sem("s_modb")
    s_wr = sem("s_wr")
    s_rb = sem("s_rb")
    s_xr = [sem(f"s_xr{b}") for b in range(2)]
    s_hp = sem("s_hp")
    names = ("a", "x", "sq", "ms", "rs", "h", "hp", "T", "teV", "teA", "lg", "sc", "c")
    sr = {n: sem(f"s_r_{n}") for n in names}
    sh = {n: sem(f"s_sh_{n}") for n in ("h", "si", "g", "T", "te", "y", "ye")}

    def shared_up(pe, t, out):
        for k in range(KT):
            mm = pe.matmul(out.rearrange("p (a n) -> p a n", a=2), h2T[:, k, t * P:(t + 1) * P],
                           w13[SH][:, :, k, :], start=(k == 0), stop=(k == KT - 1))
        return mm

    def up_bank(t):
        return bank(7 if t == 0 else 0)

    select_chain = [0]

    def select(dve, t):
        chain = Chain(dve, s_rsel, select_chain[0])
        dve.wait_ge(sr["sc"], t + 1)
        chain(dve.tensor_tensor(bia, sc[:, t, :], rbias, ALU.add))
        for g in range(NG):
            ins = dve.max(gm8[:, g, :], bia[:, g * 8:g * 8 + 8])
        chain(ins)
        chain(dve.tensor_tensor(gs.unsqueeze(2), gm8[:, :, 0:1], gm8[:, :, 1:2], ALU.add))
        other = gs.unsqueeze(1).to_broadcast([P, NG, NG])
        own = gs.unsqueeze(2).to_broadcast([P, NG, NG])
        a, b = gA64.rearrange("p (a b) -> p a b", a=8), gB64.rearrange("p (a b) -> p a b", a=8)
        dve.tensor_tensor(a, other, own, ALU.is_gt)
        chain(dve.tensor_tensor(b, other, own, ALU.is_equal))
        chain(dve.tensor_tensor(b, b, gtri.rearrange("p (a b) -> p a b", a=8), ALU.mult))
        chain(dve.tensor_tensor(a, a, b, ALU.add))
        chain(dve.tensor_reduce(rank, a, AX_X, ALU.add))
        chain(dve.tensor_scalar(rank, rank, float(TOPG), None, ALU.is_lt))
        chain(dve.tensor_scalar(gs, rank, BIG, -BIG, ALU.mult, ALU.add))
        bv = bia.rearrange("p (g e) -> p g e", g=NG)
        mv = msk.rearrange("p (g e) -> p g e", g=NG)
        chain(dve.tensor_tensor(mv, bv, rank.unsqueeze(2).to_broadcast([P, NG, 8]), ALU.mult))
        chain(dve.tensor_tensor(mv, mv, gs.unsqueeze(2).to_broadcast([P, NG, 8]), ALU.add))
        chain(dve.max(m8, msk))
        chain(dve.match_replace(rep, m8, msk, -2 * BIG))
        chain(dve.tensor_scalar(sel[:, t, :], rep, -1.5 * BIG, None, ALU.is_lt))
        dve.sem_inc(s_sel, 1)
        chain(dve.tensor_tensor(wn[:, t, :], sc[:, t, :], sel[:, t, :], ALU.mult))
        chain(dve.tensor_reduce(wsum, wn[:, t, :], AX_X, ALU.add))
        chain(dve.reciprocal(wsum, wsum))
        chain(dve.tensor_scalar(wn[:, t, :], wn[:, t, :], wsum, ROUTED_SCALE, ALU.mult, ALU.mult))
        select_chain[0] = chain.n

    with nc.Block() as block:
        @block.sync
        def _(sp):
            sp.wait_ge(s_mrow, 16)
            sp.dma_start(xres[0], I["x_prompt"][0]).then_inc(s_xr[0], 16)
            for r, a in enumerate((2, 3, 6, 7, 4, 5, 0, 1)):
                sp.dma_start(modb[:, a, :], S["mod_rows"][r:r + 1, :].to_broadcast([P, D])).then_inc(s_modb, 16)
            sp.dma_start(xres[1], I["x_sample"][0, 0:P, :]).then_inc(s_xr[1], 16)
            sp.dma_start(wr, I["w_router"][0].rearrange("(k p) n -> p k n", p=P)).then_inc(s_wr, 16)
            sp.dma_start(rbias, I["router_bias"].to_broadcast([P, NE])).then_inc(s_rb, 16)
            sp.dma_start(cst[:, :], I["route_consts"]).then_inc(s_cst, 16)
            for a, n in enumerate(("w_s1", "w_s3")):
                sp.dma_start(w13[SH][:, a], I[n][0].rearrange("(k p) n -> p k n", p=P)).then_inc(s_shw, 16)
            sp.dma_start(w2[SH], I["w_s2"][0].rearrange("(f p) n -> p f n", p=P)).then_inc(s_shw, 16)
            sp.dma_start(recs[:, :, :], I["records"]).then_inc(s_rec, 16)
            sp.dma_start(tabs[:, 0:NBLK, :], I["empty_slots"]).then_inc(s_tz, 16)
            sp.wait_ge(s_tz, 16)
            sp.dma_start(S["slots"].rearrange("(p n) w -> p n w", n=NBLK), tabs[:, 0:NBLK, :]).then_inc(s_tin, 16)
            for t in range(NT):
                if t >= 1 and t + 1 < NT:
                    sp.wait_ge(sr["x"], 2 * t)
                    sp.dma_start(xres[(t + 1) % 2], I["x_sample"][0, t * P:(t + 1) * P, :])\
                      .then_inc(s_xr[(t + 1) % 2], 16)
                sp.wait_ge(sr["hp"], t + 1)
                sp.dma_start(S["h2"][t * P:(t + 1) * P, :], h2p).then_inc(s_hp, 16)

        @block.tensor
        def _(pe):
            pe.wait_ge(s_wout, 16)

            def out_proj(t):
                if t >= 2:
                    pe.wait_ge(sr["x"], 2 * (t - 2) + 2)
                for c in range(2):
                    for k in range(KT):
                        mm = pe.matmul(bank(2 * (t % 2) + c), mT[:, k, t * P:(t + 1) * P],
                                       wout[:, k, c * 512:(c + 1) * 512], start=(k == 0), stop=(k == KT - 1))
                mm.then_inc(sr["a"], 1)

            def turn(t):
                pe.wait_ge(sr["h"], 2 * (t + 1))
                if t >= 1:
                    pe.wait_ge(sr["teV"], t)
                    pe.wait_ge(sr["teA"], t)
                for k in range(KT):
                    tr = pe.transpose(bank(4, 2)[:, k * P:(k + 1) * P], h2[:, k * P:(k + 1) * P], ident[:, :])
                tr.then_inc(sr["T"], 1)

            def router(t):
                if t == 0:
                    pe.wait_ge(s_wr, 16)
                pe.wait_ge(sr["teV"], t + 1)
                pe.wait_ge(sr["teA"], t + 1)
                if t >= 1:
                    pe.wait_ge(sr["sc"], t)
                for k in range(KT):
                    mm = pe.matmul(bank(6)[:, t * NE:(t + 1) * NE], h2T[:, k, t * P:(t + 1) * P], wr[:, k, :],
                                   start=(k == 0), stop=(k == KT - 1))
                mm.then_inc(sr["lg"], 1)

            out_proj(0)
            for t in range(1, NT):
                out_proj(t)
                turn(t - 1)
                router(t - 1)
            pe.wait_ge(s_shw, 48)
            shared_up(pe, 0, bank(7)).then_inc(sh["h"], 1)
            turn(NT - 1)
            router(NT - 1)

        @block.scalar
        def _(act):
            for t in range(NT):
                act.wait_ge(sr["x"], 2 * t + 2)
                if t >= 1:
                    act.wait_ge(sr["hp"], t)
                    act.wait_ge(s_hp, 16 * t)
                act.activation(h2p, x1[:, t, :], ACT.Square, accum_out=RS1).then_inc(sr["sq"], 1)
                act.wait_ge(sr["h"], 2 * t + 2)
                act.activation(h2p.rearrange("q (k p) -> q k p", k=KT), h2.rearrange("q (p k) -> q k p", k=KT),
                               ACT.Copy).then_inc(sr["hp"], 1)
                act.wait_ge(sr["T"], t + 1)
                act.activation(h2T[:, 4:8, t * P:(t + 1) * P], bank(5).rearrange("p (k t) -> p k t", k=4), ACT.Copy)\
                   .then_inc(sr["teA"], 1)
                act.wait_ge(sr["lg"], t + 1)
                act.activation(sc[:, t, :], bank(6)[:, t * NE:(t + 1) * NE], ACT.Sigmoid).then_inc(sr["sc"], 1)

        @block.gpsimd
        def _(pool):
            for t in range(NT):
                pool.wait_ge(sr["sq"], t + 1)
                pool.tensor_scalar(RS1, RS1, 1.0 / D, EPS, ALU.mult, ALU.add).then_inc(sr["ms"], 1)
                pool.wait_ge(sr["ms"], t + 1)
                pool.tensor_tensor(RS2, RS1, nhalf[:, 0:1], ALU.pow).then_inc(sr["rs"], 1)

        @block.vector
        def _(dve):
            dve.wait_ge(s_modb, 16 * 8)
            dve.wait_ge(s_rb, 16)
            dve.wait_ge(s_cst, 16)
            for t in range(NT):
                y = min(t, 1)
                dve.wait_ge(sr["a"], t + 1)
                dve.wait_ge(s_xr[t % 2], 16 * (t // 2 + 1))
                dve.tensor_tensor(x1[:, t, :], bank(2 * (t % 2), 2), modb[:, 2 + y, :], ALU.mult)\
                   .then_inc(sr["x"], 1)
                dve.wait_ge(sr["x"], 2 * t + 1)
                dve.tensor_tensor(x1[:, t, :], x1[:, t, :], xres[t % 2], ALU.add).then_inc(sr["x"], 1)
                dve.wait_ge(sr["rs"], t + 1)
                if t >= 1:
                    dve.wait_ge(sr["T"], t)
                    dve.wait_ge(sr["hp"], t)
                dve.scalar_tensor_tensor(out=h2, in0=x1[:, t, :], scalar=RS2, in1=modb[:, 4 + y, :],
                                         op0=ALU.mult, op1=ALU.mult).then_inc(sr["h"], 1)
                dve.wait_ge(sr["h"], 2 * t + 1)
                dve.tensor_tensor(h2, h2, modb[:, 6 + y, :], ALU.add).then_inc(sr["h"], 1)
                if 1 <= t < NT - 1:
                    select(dve, t - 1)
                dve.wait_ge(sr["T"], t + 1)
                dve.tensor_copy(h2T[:, 0:4, t * P:(t + 1) * P], bank(4).rearrange("p (k t) -> p k t", k=4))\
                   .then_inc(sr["teV"], 1)
            select(dve, NT - 2)

    g2b = modb[:, 0:2, :]
    ysh = mem.at(M_OA + 2048, NT, D)
    B0 = M_TB + 5120
    hs = mem.at(B0, FE)
    gg = mem.at(B0 + 256, FE)
    gT = mem.at(B0 + 512, 2, P)
    rt = mem.at(B0 + 768, 3392)

    def rv(n, *shape):
        off = n * 320
        v = rt[:, off:off + int(np.prod(shape))]
        return v.rearrange("p (a b) -> p a b", a=shape[0]) if len(shape) == 2 else v

    posv, jv, gsel = (rv(n, NT, NE) for n in range(3))
    ostart, oend = rt[:, 2880:2944], rt[:, 2944:3008]
    k8 = rt[:, 3136:3176].rearrange("p (t k) -> p t k", k=8)
    w8 = rt[:, 3176:3216].rearrange("p (t k) -> p t k", k=8)
    oblk, oblkb = rt[0:NE, 3216:3217], rt[0:NE, 3220:3348]
    ecol = rt[:, 3349:3350]
    cnt = rt[0:NE, 3350:3351]
    eqb = mem.at(M_OB + 2048, TOPK * NE)
    ove = sb("ove", [1, P], I32)
    nblk = sb("nblk", [1, 1], I32)
    s_rv = sem("s_rv")
    s_acc = sem("s_acc")
    s_pos = sem("s_pos")
    s_cnt = sem("s_cnt")
    s_ob = sem("s_ob")
    s_os = sem("s_os")
    s_ec = sem("s_ec")
    s_er = sem("s_er")
    s_ove = sem("s_ove")
    s_k8 = sem("s_k8")
    s_tsc = sem("s_tsc")
    s_tab = sem("s_tab")
    s_w13 = [sem(f"s_w13_{u}") for u in range(RING)]
    s_w2 = [sem(f"s_w2_{u}") for u in range(RING)]
    w13_src = [I[n][0].rearrange("e (p k) n -> p e k n", k=KT) for n in ("w_e1", "w_e3")]
    w2_src = I["w_e2"][0].rearrange("e (f p) n -> p e f n", p=P)

    def load_w13(sp, n, u):
        for a in range(2):
            sp.dma_start(w13[u][:, a], w13_src[a][:, bass.ds(n, 1)].rearrange("p e k n -> p (e k) n"))\
              .then_inc(s_w13[u], 16)

    def load_w2(sp, n, u):
        sp.dma_start(w2[u], w2_src[:, bass.ds(n, 1)].rearrange("p e f n -> p (e f) n")).then_inc(s_w2[u], 16)

    xg = [mem.at(B0 + 768 + 1024 * b, D) for b in range(2)]
    xT = mem.at(B0 + 2816, KT, P)
    yb = mem.at(M_OB + 2560, D)
    held = sb("held", [1, 2])
    gi = [sb(f"gi{b}", [P, 1], I32) for b in range(2)]
    si = sb("si", [P, 1], I32)
    names = ("gi", "si", "Tx", "xeV", "xeA", "u", "sl", "g", "Th", "te", "y", "yV", "yA", "z")
    se = {n: sem(f"s_e_{n}") for n in names}
    s_xg = [sem(f"s_xg{b}") for b in range(2)]
    s_sc = sem("s_sc")
    pX, pH, pG, pY = psum[:, 0:1024], bank(2), bank(3), psum[:, 2048:3072]

    def wslot(tab, n, w):
        return tab[:, bass.ds(n, 1), w:w + 1].rearrange("p n w -> p (n w)")

    with nc.Block() as block:
        @block.sync
        def _(sp):
            for u in range(SH):
                load_w13(sp, u, u)
                load_w2(sp, u, u)
            for t in range(NT - 1):
                sp.wait_ge(sh["ye"], t + 1)
                sp.dma_start(S["sums"][t * P:(t + 1) * P, :], ysh[:, t, :]).then_inc(s_acc, 16)
            sp.wait_ge(s_tsc, 16 * NT * TOPK)
            sp.dma_start(tabs[:, 0:NBLK, :], S["slots"].rearrange("(p n) w -> p n w", n=NBLK)).then_inc(s_tab, 16)
            sp.wait_ge(sh["ye"], NT)
            sp.dma_start(S["sums"][(NT - 1) * P:NT * P, :], ysh[:, NT - 1, :]).then_inc(s_acc, 16)

        @block.tensor
        def _(pe):
            def turn(t):
                pe.wait_ge(sh["g"], t + 1)
                for f in range(2):
                    tr = pe.transpose(bank(1)[:, f * P:(f + 1) * P], gg[:, f * P:(f + 1) * P], ident[:, :])
                tr.then_inc(sh["T"], 1)

            def down(t):
                pe.wait_ge(sh["te"], t + 1)
                if t >= 1:
                    pe.wait_ge(sh["ye"], t)
                for c in range(2):
                    for f in range(2):
                        mm = pe.matmul(bank(2 + c), gT[:, f, :], w2[SH][:, f, c * 512:(c + 1) * 512],
                                       start=(f == 0), stop=(f == 1))
                mm.then_inc(sh["y"], 1)

            pe.wait_ge(s_cst, 16)
            def count(t):
                return pe.matmul(bank(5)[0:NE, 0:1], sel[:, t, :], ones[:, 0:1], start=(t == 0), stop=(t == NT - 1))

            def place(t, a):
                return pe.matmul(bank(4)[:, t * NE:(t + 1) * NE], tri if a == t else ones, sel[:, a, :],
                                 start=(a == 0), stop=(a == t))

            pe.wait_ge(s_sel, NT - 1)
            for t in range(NT):
                for a in range(min(t + 1, NT - 1)):
                    place(t, a)
            for t in range(NT - 1):
                count(t)
            pe.wait_ge(s_sel, NT)
            count(NT - 1).then_inc(s_cnt, 1)
            mm = place(NT - 1, NT - 1)
            mm.then_inc(s_pos, 1)
            pe.wait_ge(s_ob, 1)
            pe.matmul(bank(6)[:, 0:NE], oblkb, triX, start=True, stop=True)
            pe.matmul(bank(6)[:, NE:2 * NE], oblkb, triI, start=True, stop=True).then_inc(s_os, 1)
            turn(0)
            for t in range(1, NT):
                pe.wait_ge(sh["g"], t)
                shared_up(pe, t, up_bank(t)).then_inc(sh["h"], 1)
                if t == 2:
                    pe.wait_ge(s_ec, 1)
                    pe.matmul(bank(7)[0:1, 0:P], ecol, ident[:, :], start=True, stop=True).then_inc(s_er, 1)
                down(t - 1)
                turn(t)
            down(NT - 1)

        @block.scalar
        def _(act):
            def silu(t):
                act.wait_ge(sh["h"], t + 1)
                act.activation(hs, up_bank(t)[:, 0:FE], ACT.Silu).then_inc(sh["si"], 1)

            silu(0)
            for t in range(NT):
                act.wait_ge(sh["T"], t + 1)
                act.activation(gT.rearrange("p f t -> p (f t)"), bank(1)[:, 0:256], ACT.Copy).then_inc(sh["te"], 1)
                if t + 1 < NT:
                    act.wait_ge(sh["g"], t + 1)
                    silu(t + 1)
                act.wait_ge(sh["y"], t + 1)
                act.activation(ysh[:, t, :], bank(2, 2), ACT.Copy).then_inc(sh["ye"], 1)

        @block.gpsimd
        def _(pool):
            pool.wait_ge(s_tin, 16)
            for n in range(NT * TOPK):
                if n % TOPK == 0:
                    pool.wait_ge(s_k8, 2 * (n // TOPK + 1))
                pool.indirect_dma_start(out=S["slots"], out_offset=bass.IndirectOffsetOnAxis(ap=kidx[:, n:n + 1], axis=0),
                                        in_=recs[:, n, :], in_offset=None,
                                        bounds_check=P * NBLK - 1, oob_is_err=False).then_inc(s_tsc, 16)
            pool.wait_ge(s_tab, 16)
            pool.wait_ge(s_hp, 16 * NT)
            pool.wait_ge(se["z"], 2)
            for n in range(2):
                pool.tensor_copy(gi[n][:, :], wslot(tabs, n, 0)).then_inc(se["gi"], 1)
                pool.wait_ge(se["gi"], n + 1)
                pool.indirect_dma_start(out=xg[n], out_offset=None, in_=S["h2"],
                                        in_offset=bass.IndirectOffsetOnAxis(ap=gi[n][:, 0:1], axis=0),
                                        bounds_check=TOK - 1, oob_is_err=False).then_inc(s_xg[n], 16)

        @block.vector
        def _(dve):
            def product(t):
                dve.wait_ge(sh["si"], t + 1)
                if t >= 1:
                    dve.wait_ge(sh["T"], t)
                dve.tensor_tensor(gg, hs, up_bank(t)[:, FE:2 * FE], ALU.mult).then_inc(sh["g"], 1)

            chain = Chain(dve, s_rv)
            dve.wait_ge(s_hp, 16 * NT)
            select(dve, NT - 1)
            product(0)
            dve.wait_ge(s_cnt, 1)
            chain(dve.tensor_copy(cnt, bank(5)[0:NE, 0:1]))
            chain(dve.tensor_scalar(oblk, cnt, float(P), None, ALU.is_gt))
            for a in range(2, NT):
                chain(dve.scalar_tensor_tensor(out=oblk, in0=cnt, scalar=float(P * a), in1=oblk,
                                               op0=ALU.is_gt, op1=ALU.add))
            dve.tensor_scalar(oblkb, ones[0:NE, :], oblk, None, ALU.mult).then_inc(s_ob, 1)
            dve.wait_ge(s_pos, 1)
            chain(dve.tensor_copy(posv, bank(4)[:, 0:NT * NE].rearrange("p (t e) -> p t e", t=NT)))
            chain(dve.tensor_scalar(jv, posv, float(P), None, ALU.is_ge))
            for a in range(2, NT):
                chain(dve.scalar_tensor_tensor(out=jv, in0=posv, scalar=float(P * a), in1=jv,
                                               op0=ALU.is_ge, op1=ALU.add))
            chain(dve.scalar_tensor_tensor(out=posv, in0=jv, scalar=-float(P), in1=posv, op0=ALU.mult, op1=ALU.add))
            dve.wait_ge(s_os, 1)
            chain(dve.tensor_copy(rt[:, 2880:3008], bank(6)[:, 0:2 * NE]))
            chain(dve.tensor_tensor(ostart, ostart, enum, ALU.subtract))
            chain(dve.tensor_scalar(ostart, ostart, float(NE - 1), None, ALU.add))
            chain(dve.tensor_tensor(gsel, jv, ostart.unsqueeze(1).to_broadcast([P, NT, NE]), ALU.add))
            chain(dve.tensor_scalar(jv, jv, 1.0, None, ALU.is_ge))
            chain(dve.tensor_tensor(gsel, gsel, jv, ALU.mult))
            chain(dve.tensor_tensor(gsel, gsel, enum.unsqueeze(1).to_broadcast([P, NT, NE]), ALU.add))
            chain(dve.scalar_tensor_tensor(out=gsel, in0=posv, scalar=float(NBLK), in1=gsel,
                                           op0=ALU.mult, op1=ALU.add))
            chain(dve.scalar_tensor_tensor(out=gsel, in0=gsel, scalar=1.0, in1=sel, op0=ALU.add, op1=ALU.mult))
            dve.wait_ge(s_rec, 16)
            for t in range(NT):
                chain(dve.max(k8[:, t, :], gsel[:, t, :]))
                e3 = eqb.rearrange("p (k e) -> p k e", k=TOPK)
                chain(dve.tensor_tensor(e3, gsel[:, t, :].unsqueeze(1).to_broadcast([P, TOPK, NE]),
                                        k8[:, t, :].unsqueeze(2).to_broadcast([P, TOPK, NE]), ALU.is_equal))
                chain(dve.tensor_tensor(e3, e3, wn[:, t, :].unsqueeze(1).to_broadcast([P, TOPK, NE]), ALU.mult))
                chain(dve.tensor_reduce(w8[:, t, :], e3, AX_X, ALU.add))
                dve.tensor_scalar(kidx[:, t * TOPK:(t + 1) * TOPK], k8[:, t, :], -1.0, None, ALU.add)\
                   .then_inc(s_k8, 1)
                dve.tensor_copy(recs[:, t * TOPK:(t + 1) * TOPK, 2:3].bitcast(F32), w8[:, t, :].unsqueeze(2))\
                   .then_inc(s_k8, 1)
                if t == 0:
                    product(1)
                    chain(dve.tensor_scalar(eqb[:, 0:NE], oend, pnum, None, ALU.is_le))
                    chain(dve.tensor_reduce(ecol, eqb[:, 0:NE], AX_X, ALU.add))
                    dve.tensor_scalar(ecol, ecol, float(NE - 1), None, ALU.min).then_inc(s_ec, 1)
                    chain(dve.tensor_scalar(nblk[:, :], oend[0:1, NE - 1:NE], float(NE), None, ALU.add))
            dve.wait_ge(s_k8, 2 * NT)
            for b in range(2):
                dve.memset(xg[b], 0.0).then_inc(se["z"], 1)
            dve.wait_ge(s_er, 1)
            chain(dve.tensor_copy(ove[:, :], bank(7)[0:1, 0:P]))
            for t in range(2, NT):
                product(t)

    with nc.Block() as block:
        def run(eng, step, total=None):
            for u in range(RING):
                step(u, 0, u, lambda k, u=u: None if u >= k else False)
            with eng.Fori(1, NE // RING) as i:
                for u in range(RING):
                    step(RING * i + u, i, u, lambda k: None)
            nb = eng.value_load(nblk[0:1, 0:1], min_val=NE, max_val=NBLK)
            with eng.Fori(NE // RING, NBLK // RING + 1) as i:
                with eng.If(RING * i - 3 < nb):
                    for u in range(RING):
                        n = RING * i + u
                        step(n, i, u, lambda k, n=n: n - k < nb)
            return nb

        def due(eng, cond, what):
            if cond is None:
                what()
            elif cond is not False:
                with eng.If(cond):
                    what()

        @block.sync
        def _(sp):
            def step(n, i, u, guard):
                def loads():
                    if isinstance(n, int):
                        if n < SH:
                            return
                        load_w13(sp, n, u)
                        load_w2(sp, n, u)
                        return
                    e = n
                    if past[0]:
                        e = sp.value_load(ove[0:1, bass.ds(n - NE, 1)], min_val=0, max_val=NE - 1)
                    sp.wait_ge(se["u"], n - RING + 1)
                    load_w13(sp, e, u)
                    sp.wait_ge(se["y"], n - RING + 1)
                    load_w2(sp, e, u)
                due(sp, guard(0), loads)

            past = [False]
            for u in range(RING):
                step(u, 0, u, lambda k: None)
            with sp.Fori(1, NE // RING) as i:
                for u in range(RING):
                    step(RING * i + u, i, u, lambda k: None)
            past[0] = True
            nb = sp.value_load(nblk[0:1, 0:1], min_val=NE, max_val=NBLK)
            with sp.Fori(NE // RING, NBLK // RING) as i:
                with sp.If(RING * i < nb):
                    for u in range(RING):
                        n = RING * i + u
                        step(n, i, u, lambda k, n=n: n < nb)

        @block.gpsimd
        def _(pool):
            pool.wait_ge(s_acc, 16 * NT)

            def hold(pool, c=0):
                pool.tensor_tensor(held[:, c:c + 1], nhalf[0:1, 0:1], nhalf[0:1, 0:1], ALU.add)

            def step(n, i, u, guard):
                first = isinstance(n, int)

                def gather():
                    if first and u < 2:
                        return
                    pool.wait_ge(se["Tx"], n - 1)
                    pool.tensor_copy(gi[u % 2][:, :], wslot(tabs, n, 0)).then_inc(se["gi"], 1)
                    pool.wait_ge(se["gi"], n + 1)
                    hold(pool)
                    pool.indirect_dma_start(out=xg[u % 2], out_offset=None, in_=S["h2"],
                                            in_offset=bass.IndirectOffsetOnAxis(ap=gi[u % 2][:, 0:1], axis=0),
                                            bounds_check=TOK - 1, oob_is_err=False).then_inc(s_xg[u % 2], 16)

                def scatter():
                    m = n - 3
                    if not (first and u == 3):
                        pool.wait_ge(s_sc, 16 * m)
                        hold(pool, 1)
                    pool.tensor_copy(si[:, :], wslot(tabs, m, 0)).then_inc(se["si"], 1)
                    pool.wait_ge(se["si"], m + 1)
                    pool.wait_ge(se["yV"], m + 1)
                    pool.wait_ge(se["yA"], m + 1)
                    hold(pool)
                    pool.indirect_dma_start(out=S["sums"], out_offset=bass.IndirectOffsetOnAxis(ap=si[:, 0:1], axis=0),
                                            in_=yb, in_offset=None, compute_op=ALU.add,
                                            bounds_check=TOK - 1, oob_is_err=False).then_inc(s_sc, 16)

                due(pool, guard(0), gather)
                due(pool, guard(3), scatter)

            nb = run(pool, step)
            pool.wait_ge(s_sc, nb * 16)

        @block.tensor
        def _(pe):
            def step(n, i, u, guard):
                def turn_x():
                    pe.wait_ge(s_xg[u % 2], 32 * i + 16 * (u // 2 + 1))
                    for k in range(KT):
                        tr = pe.transpose(pX[:, k * P:(k + 1) * P], xg[u % 2][:, k * P:(k + 1) * P], ident[:, :])
                    tr.then_inc(se["Tx"], 1)

                def down():
                    v = (u - 2) % RING
                    pe.wait_ge(se["te"], n - 1)
                    pe.wait_ge(s_w2[v], 16 * (i + 1 if u >= 2 else i))
                    if not (isinstance(n, int) and u == 2):
                        pe.wait_ge(se["yV"], n - 2)
                        pe.wait_ge(se["yA"], n - 2)
                    for c in range(2):
                        for f in range(2):
                            mm = pe.matmul(pY[:, c * 512:(c + 1) * 512], gT[:, f, :],
                                           w2[v][:, f, c * 512:(c + 1) * 512], start=(f == 0), stop=(f == 1))
                    mm.then_inc(se["y"], 1)

                def turn_g():
                    pe.wait_ge(se["g"], n)
                    for f in range(2):
                        tr = pe.transpose(pG[:, f * P:(f + 1) * P], gg[:, f * P:(f + 1) * P], ident[:, :])
                    tr.then_inc(se["Th"], 1)

                def up():
                    pe.wait_ge(se["xeV"], n + 1)
                    pe.wait_ge(se["xeA"], n + 1)
                    pe.wait_ge(s_w13[u], 32 * (i + 1))
                    for k in range(KT):
                        mm = pe.matmul(pH.rearrange("p (a n) -> p a n", a=2), xT[:, k, :], w13[u][:, :, k, :],
                                       start=(k == 0), stop=(k == KT - 1))
                    mm.then_inc(se["u"], 1)

                due(pe, guard(0), turn_x)
                due(pe, guard(2), down)
                due(pe, guard(1), turn_g)
                due(pe, guard(0), up)

            run(pe, step)

        @block.scalar
        def _(act):
            def step(n, i, u, guard):
                def take_x():
                    act.wait_ge(se["Tx"], n + 1)
                    act.activation(xT[:, 4:8, :].rearrange("p k t -> p (k t)"), pX[:, 512:1024], ACT.Copy)\
                       .then_inc(se["xeA"], 1)

                def take_y():
                    m = n - 2
                    act.wait_ge(se["y"], m + 1)
                    if not (isinstance(n, int) and u == 2):
                        act.wait_ge(s_sc, 16 * m)
                    act.activation(yb[:, 512:1024], pY[:, 512:1024], ACT.Copy,
                                   scale=wslot(tabs, m, 2).bitcast(F32)).then_inc(se["yA"], 1)

                def silu():
                    act.wait_ge(se["u"], n + 1)
                    if not (isinstance(n, int) and u == 0):
                        act.wait_ge(se["g"], n)
                    act.activation(hs, pH[:, 0:FE], ACT.Silu).then_inc(se["sl"], 1)

                due(act, guard(0), take_x)
                due(act, guard(2), take_y)
                due(act, guard(0), silu)

            run(act, step)

        @block.vector
        def _(dve):
            def step(n, i, u, guard):
                def take_x():
                    dve.wait_ge(se["Tx"], n + 1)
                    dve.tensor_copy(xT[:, 0:4, :].rearrange("p k t -> p (k t)"), pX[:, 0:512]).then_inc(se["xeV"], 1)

                def take_y():
                    m = n - 2
                    dve.wait_ge(se["y"], m + 1)
                    if not (isinstance(n, int) and u == 2):
                        dve.wait_ge(s_sc, 16 * m)
                    dve.tensor_scalar(yb[:, 0:512], pY[:, 0:512], wslot(tabs, m, 2).bitcast(F32), None,
                                      ALU.mult).then_inc(se["yV"], 1)

                def take_g():
                    dve.wait_ge(se["Th"], n)
                    dve.tensor_copy(gT.rearrange("p f t -> p (f t)"), pG[:, 0:256]).then_inc(se["te"], 1)

                def product():
                    dve.wait_ge(se["sl"], n + 1)
                    dve.tensor_tensor(gg, hs, pH[:, FE:2 * FE], ALU.mult).then_inc(se["g"], 1)

                due(dve, guard(0), take_x)
                due(dve, guard(2), take_y)
                due(dve, guard(1), take_g)
                due(dve, guard(0), product)

            run(dve, step)

    yt = mem.at(M_R, NT, D)
    s_yt = [sem(f"s_yt{t}") for t in range(NT)]
    s_cb = sem("s_cb")
    s_cc = sem("s_cc")
    s_fin = sem("s_fin")
    with nc.Block() as block:
        @block.sync
        def _(sp):
            for t in range(NT):
                sp.dma_start(yt[:, t, :], S["sums"][t * P:(t + 1) * P, :]).then_inc(s_yt[t], 16)

        @block.scalar
        def _(act):
            for t in range(NT):
                act.wait_ge(s_cc, t + 1)
                dst = O["yp"][0] if t == 0 else O["ys"][0, (t - 1) * P:t * P, :]
                act.dma_start(dst, yt[:, t, :]).then_inc(s_fin, 16)
            act.wait_ge(s_fin, 16 * NT)

        @block.vector
        def _(dve):
            for t in range(NT):
                r = yt[:, t, :]
                dve.wait_ge(s_yt[t], 16)
                dve.tensor_tensor(r, r, g2b[:, min(t, 1), :], ALU.mult).then_inc(s_cb, 1)
                dve.wait_ge(s_cb, t + 1)
                dve.tensor_tensor(r, r, x1[:, t, :], ALU.add).then_inc(s_cc, 1)


def rope_tables(width):
    t = np.arange(LAT)
    axis = width // 2
    inv = THETA ** (-np.arange(0, axis, 2, dtype=np.float32) / axis)
    ang = np.concatenate([(t // GRID_W)[:, None] * inv, (t % GRID_W)[:, None] * inv], -1).astype(np.float32)
    cos, sin = np.cos(ang), np.sin(ang)
    c = np.concatenate([np.ones((SEQ, width)), np.concatenate([cos, cos], -1)], 0)
    s = np.concatenate([np.zeros((SEQ, width)), np.concatenate([-sin, sin], -1)], 0)
    return c.astype(np.float32), s.astype(np.float32)


def constants():
    c = {"ident": np.eye(P, dtype=np.float32)}
    c["cos_a"], c["sin_a"] = rope_tables(HD)
    c["cos_b"], c["sin_b"] = rope_tables(ROPE)
    i = np.arange(P)
    e = np.arange(NE)
    g = np.arange(NG)
    route = np.zeros((P, 513), np.float32)
    route[:, 0:128] = i[:, None] < i[None, :]
    route[:, 128:256] = 1
    route[:, 256:320] = e
    route[:, 320:384] = (g[None, :] < g[:, None]).reshape(1, -1)
    route[:, 384] = i
    route[0:NE, 385:449] = e[:, None] < e[None, :]
    route[0:NE, 449:513] = e[:, None] <= e[None, :]
    c["route_consts"] = route
    rec = np.zeros((P, NT, TOPK, 4), np.int32)
    tok = np.arange(NT)[None, :, None] * P + i[:, None, None]
    rec[..., 0] = tok
    c["records"] = rec.reshape(P, NT * TOPK, 4)
    empty = np.zeros((P, NBLK, 4), np.int32)
    empty[..., 0] = TOK
    c["empty_slots"] = empty
    return c


_INS = ["x_prompt", "x_sample", "c", "cache_gqa_k", "cache_gqa_v", "cache_mla_ckv", "cache_mla_krope", "c_ctx",
        "w_mod", "b_mod", "norm1_g", "norm2_g", "w_in", "gqa_qn", "gqa_kn", "mla_qa_g", "mla_kva_g", "w_qb",
        "w_kvb", "mla_qn_nope", "mla_qn_rope", "mla_kn_nope", "mla_kn_rope", "w_oa", "w_ob", "w_out",
        "w_router", "router_bias", "w_e1", "w_e3", "w_e2", "w_s1", "w_s3", "w_s2"]
_OUTS = [("yp", (1, SEQ, D)), ("ys", (1, LAT, D)), ("gk", (1, 1, KVA, SEQ, HD)), ("gv", (1, 1, KVA, SEQ, HD)),
         ("ckv", (1, 1, SEQ, KVL)), ("kr", (1, 1, SEQ, ROPE))]


def kernel(**inputs):
    import concourse.bacc as bacc
    from concourse.bass_utils import run_bass_kernel_spmd

    nc = bacc.Bacc("TRN2", target_bir_lowering=False, num_devices=1)
    arrays, ins = {}, {}
    for name, a in [(n, inputs[n]) for n in _INS] + list(constants().items()):
        a = np.ascontiguousarray(a)
        arrays[f"in_{name}"] = a
        ins[name] = nc.dram_tensor(f"in_{name}", a.shape, mybir.dt.from_np(a.dtype), kind="ExternalInput").ap()
    outs = {n: nc.dram_tensor(f"out_{n}", s, F32, kind="ExternalOutput").ap() for n, s in _OUTS}
    scratch = {
        "mod_rows": nc.dram_tensor("mod_rows", [8, D], F32, kind="Internal").ap(),
        "h2": nc.dram_tensor("h2", [TOK, D], F32, kind="Internal").ap(),
        "slots": nc.dram_tensor("slots", [P * NBLK, 4], I32, kind="Internal").ap(),
        "sums": nc.dram_tensor("sums", [TOK, D], F32, kind="Internal").ap(),
    }
    program(nc, ins, outs, scratch)
    r = run_bass_kernel_spmd(nc, [arrays], core_ids=[0])
    return tuple(r.results[0][f"out_{n}"] for n, _ in _OUTS)
```
